# Optimizing a Trainium2 kernel written in Bass

```python
import math
import jax, jax.numpy as jnp
from jax import lax
import numpy as np

D_MODEL = 1024
BATCH = 1
SEQ = 256
DEPTH = 2

GRID_W = 64
CTX_LEN = 256
N_MIXERS = 2
N_SSD = (DEPTH + 1) // 2
N_ATT = DEPTH // 2
RMS_EPS = 1e-6

SSD_EXPAND = 2
SSD_INNER = SSD_EXPAND * D_MODEL
SSD_HEADDIM = 64
SSD_HEADS = SSD_INNER // SSD_HEADDIM
SSD_GROUPS = 4
SSD_STATE = 128
SSD_CONV = 5
SSD_CHUNK = 128
SSD_CONV_DIM = SSD_INNER + 2 * SSD_GROUPS * SSD_STATE
SSD_IN_DIM = SSD_INNER + SSD_CONV_DIM + 2 * SSD_HEADS

DA_HEADS = D_MODEL // 128
DA_HEAD_DIM = 64
DA_V_DIM = 2 * DA_HEAD_DIM
DA_IN_DIM = DA_HEADS * (4 * DA_HEAD_DIM + DA_V_DIM)
Q_BLOCK = 128
ROPE_BASE = 10000.0

N_EXPERTS = 16
N_GROUPS = 4
EXPERTS_PER_GROUP = N_EXPERTS // N_GROUPS
TOP_K = 2
D_EXPERT = D_MODEL // 2

kernel_name = "hybrid_ssd_diffattn_grouped_moe_dit"

F32 = jnp.float32

def rmsnorm(x, g):
    xf = x.astype(F32)
    y = xf * lax.rsqrt(jnp.mean(xf * xf, axis=-1, keepdims=True) + RMS_EPS)
    return (y * g.astype(F32)).astype(x.dtype)

def modulate(h, shift, scale):
    return h * (1.0 + scale) + shift

def depthwise_conv_centred(u, w, b):
    k, ch = w.shape
    y = lax.conv_general_dilated(u, w.astype(u.dtype)[:, None, :], window_strides=(1,),
                                 padding=[(k // 2, k // 2)],
                                 dimension_numbers=("NWC", "WIO", "NWC"),
                                 feature_group_count=ch)
    return y + b.astype(u.dtype)

def ssd_chunked_scan(xs, a, bm, cm, h0):
    b, l, h, p = xs.shape
    g, n = bm.shape[2], bm.shape[3]
    r = h // g
    nch = l // SSD_CHUNK
    xs = xs.reshape(b, nch, SSD_CHUNK, g, r, p)
    bm = bm.reshape(b, nch, SSD_CHUNK, g, n)
    cm = cm.reshape(b, nch, SSD_CHUNK, g, n)
    a_cs = jnp.cumsum(a.reshape(b, nch, SSD_CHUNK, g, r), axis=2)
    a_t = a_cs.transpose(0, 1, 3, 4, 2)
    lower = jnp.tril(jnp.ones((SSD_CHUNK, SSD_CHUNK), dtype=bool))
    seg = jnp.exp(jnp.where(lower, a_t[..., :, None] - a_t[..., None, :], -jnp.inf))
    cb = jnp.einsum("bclgn,bcsgn->bcgls", cm, bm)
    y_diag = jnp.einsum("bcgrls,bcsgrp->bclgrp", cb[:, :, :, None] * seg, xs)
    to_end = jnp.exp(a_cs[:, :, -1:] - a_cs)
    chunk_states = jnp.einsum("bclgn,bclgrp->bcgrpn", bm, xs * to_end[..., None])
    chunk_decay = jnp.exp(a_cs[:, :, -1])

    def carry_state(state, inp):
        s_chunk, d_chunk = inp
        return state * d_chunk[..., None, None] + s_chunk, state

    h_last, h_start = lax.scan(carry_state, h0.reshape(b, g, r, p, n),
                               (jnp.moveaxis(chunk_states, 1, 0), jnp.moveaxis(chunk_decay, 1, 0)))
    h_start = jnp.moveaxis(h_start, 0, 1)
    y_off = jnp.einsum("bclgn,bcgrpn->bclgrp", cm, h_start) * jnp.exp(a_cs)[..., None]
    return (y_diag + y_off).reshape(b, l, h, p), h_last.reshape(b, h, p, n)

def ssd_mixer(hl, hc, w_in, conv_w, conv_b, dt_bias, a_log, d_skip, norm_g, w_out, need_ctx):
    def project(h):
        bsz, n = h.shape[0], h.shape[1]
        zxbcdt = h @ w_in
        z, xbc, dt = jnp.split(zxbcdt, [SSD_INNER, SSD_INNER + SSD_CONV_DIM], axis=-1)
        xbc = jax.nn.silu(depthwise_conv_centred(xbc, conv_w, conv_b))
        xs, bm, cm = jnp.split(xbc, [SSD_INNER, SSD_INNER + SSD_GROUPS * SSD_STATE], axis=-1)
        return (z, xs.reshape(bsz, n, SSD_HEADS, SSD_HEADDIM),
                bm.reshape(bsz, n, SSD_GROUPS, SSD_STATE), cm.reshape(bsz, n, SSD_GROUPS, SSD_STATE),
                dt.reshape(bsz, n, 2, SSD_HEADS))

    zl, xl, bl, cl, dtl = project(hl)
    zc, xc, bc, cc, dtc = project(hc)
    bsz = hl.shape[0]
    yl = (d_skip[:, None] * xl).astype(F32)
    yc = (d_skip[:, None] * xc).astype(F32)
    for k, rev in ((0, False), (1, True)):
        a_coef = -jnp.exp(a_log[k].astype(F32))

        def scan_inputs(xs, bm, cm, dt):
            dtk = jax.nn.softplus(dt[:, :, k].astype(F32) + dt_bias[k].astype(F32))
            seqs = (xs.astype(F32) * dtk[..., None], a_coef * dtk, bm.astype(F32), cm.astype(F32))
            return tuple(jnp.flip(s, axis=1) for s in seqs) if rev else seqs

        h0 = jnp.zeros((bsz, SSD_HEADS, SSD_HEADDIM, SSD_STATE), F32)
        y_c, h_ctx = ssd_chunked_scan(*scan_inputs(xc, bc, cc, dtc), h0)
        y_l, _ = ssd_chunked_scan(*scan_inputs(xl, bl, cl, dtl), h_ctx)
        if rev:
            y_c, y_l = jnp.flip(y_c, axis=1), jnp.flip(y_l, axis=1)
        yl = yl + y_l
        yc = yc + y_c

    def finish(y, z):
        y = y.astype(z.dtype).reshape(z.shape[0], z.shape[1], SSD_INNER)
        return rmsnorm(y * jax.nn.silu(z), norm_g) @ w_out

    return finish(yl, zl), (finish(yc, zc) if need_ctx else None)

def axial_rope_tables(n_tok, dtype):
    t = jnp.arange(n_tok, dtype=jnp.int32)
    pos = jnp.stack([t // GRID_W, t % GRID_W], axis=-1).astype(F32)
    n_freq = DA_HEAD_DIM // 4
    inv_freq = ROPE_BASE ** (-jnp.arange(n_freq, dtype=F32) / n_freq)
    ang = pos[..., None] * inv_freq
    return jnp.cos(ang).astype(dtype), jnp.sin(ang).astype(dtype)

def apply_axial_rope(x, cos, sin):
    b, n, m, h, d = x.shape
    xr = x.reshape(b, n, m, h, 2, 2, d // 4)
    x1, x2 = xr[..., 0, :], xr[..., 1, :]
    cs, sn = cos[:, None, None], sin[:, None, None]
    out = jnp.stack([x1 * cs - x2 * sn, x2 * cs + x1 * sn], axis=-2)
    return out.reshape(b, n, m, h, d)

def diff_softmax_attend(q, k, v, lam):
    s = jnp.einsum("bqmhd,bkmhd->bmhqk", q, k).astype(F32) * (DA_HEAD_DIM ** -0.5)
    p = jax.nn.softmax(s, axis=-1)
    att = p[:, 0] - lam * p[:, 1]
    return jnp.einsum("bhqk,bkhe->bqhe", att.astype(v.dtype), v)

def diff_attn_mixer(hl, hc, w_in, q_norm, k_norm, lam_q, lam_k, sub_norm, w_out, lam_init, need_ctx):
    bsz, n = hl.shape[0], hl.shape[1]
    lq, lk = lam_q.astype(F32), lam_k.astype(F32)
    lam = jnp.exp(jnp.sum(lq[0] * lk[0])) - jnp.exp(jnp.sum(lq[1] * lk[1])) + lam_init

    def project(h):
        qkv = h @ w_in
        q, k, v = jnp.split(qkv, [2 * DA_HEADS * DA_HEAD_DIM, 4 * DA_HEADS * DA_HEAD_DIM], axis=-1)
        q = rmsnorm(q.reshape(bsz, -1, 2, DA_HEADS, DA_HEAD_DIM), q_norm[:, None, :])
        k = rmsnorm(k.reshape(bsz, -1, 2, DA_HEADS, DA_HEAD_DIM), k_norm[:, None, :])
        return q, k, v.reshape(bsz, -1, DA_HEADS, DA_V_DIM)

    ql, kl, vl = project(hl)
    cos, sin = axial_rope_tables(n, hl.dtype)
    ql = apply_axial_rope(ql, cos, sin)
    kl = apply_axial_rope(kl, cos, sin)
    qc, kc, vc = project(hc)
    k_all = jnp.concatenate([kc, kl], axis=1)
    v_all = jnp.concatenate([vc, vl], axis=1)
    nb = n // Q_BLOCK
    q_blocks = ql.reshape(bsz, nb, Q_BLOCK, 2, DA_HEADS, DA_HEAD_DIM).transpose(1, 0, 2, 3, 4, 5)
    o = lax.map(lambda qb: diff_softmax_attend(qb, k_all, v_all, lam), q_blocks)
    o = o.transpose(1, 0, 2, 3, 4).reshape(bsz, n, DA_HEADS, DA_V_DIM)

    def finish(o):
        o = rmsnorm(o, sub_norm) * (1.0 - lam_init)
        return o.reshape(o.shape[0], o.shape[1], DA_HEADS * DA_V_DIM) @ w_out

    yc = finish(diff_softmax_attend(qc, kc, vc, lam)) if need_ctx else None
    return finish(o), yc

def grouped_moe(h, router_w, router_b, w_gate, w_up, w_down):
    shp = h.shape
    hf = h.reshape(-1, shp[-1])
    t = hf.shape[0]
    scores = jax.nn.sigmoid((hf @ router_w).astype(F32))
    biased = scores + router_b.astype(F32)
    grp = biased.reshape(t, N_GROUPS, EXPERTS_PER_GROUP)
    grp_score = jnp.sum(lax.top_k(grp, 2)[0], axis=-1)
    gsel = jax.nn.one_hot(jnp.argmax(grp_score, axis=-1), N_GROUPS, dtype=F32)
    masked = jnp.where(gsel[..., None] > 0, grp, -jnp.inf).reshape(t, N_EXPERTS)
    _, idx = lax.top_k(masked, TOP_K)
    wsel = jnp.take_along_axis(scores, idx, axis=-1)
    wsel = wsel / jnp.sum(wsel, axis=-1, keepdims=True)
    combine = jnp.sum(jax.nn.one_hot(idx, N_EXPERTS, dtype=F32) * wsel[..., None], axis=1).astype(h.dtype)
    out = jnp.zeros_like(hf)
    for e in range(N_EXPERTS):
        u = jax.nn.silu(hf @ w_gate[e]) * (hf @ w_up[e])
        out = out + combine[:, e:e + 1] * (u @ w_down[e])
    return out.reshape(shp)

def setup_inputs(seed: int = 0) -> dict:
    key = jax.random.key(seed)
    ks = iter(jax.random.split(key, 40))

    def nrm(shape, scale):
        return jax.random.normal(next(ks), shape, F32) * scale

    x = nrm((BATCH, SEQ, D_MODEL), 1.0)
    c = nrm((BATCH, D_MODEL), 1.0)
    ctx = nrm((BATCH, CTX_LEN, D_MODEL), 1.0)
    c_ctx = nrm((D_MODEL,), 1.0)
    ada_w = nrm((DEPTH, D_MODEL, 6 * D_MODEL), 0.5 * D_MODEL ** -0.5)
    ada_b = nrm((DEPTH, 6 * D_MODEL), 0.02)
    norm1_g = 1.0 + nrm((DEPTH, D_MODEL), 0.02)
    norm2_g = 1.0 + nrm((DEPTH, D_MODEL), 0.02)
    ssd_w_in = nrm((N_SSD, D_MODEL, SSD_IN_DIM), D_MODEL ** -0.5)
    ssd_conv_w = nrm((N_SSD, SSD_CONV, SSD_CONV_DIM), SSD_CONV ** -0.5)
    ssd_conv_b = nrm((N_SSD, SSD_CONV_DIM), 0.02)
    dt0 = jnp.exp(jax.random.uniform(next(ks), (N_SSD, 2, SSD_HEADS), F32, math.log(1e-3), math.log(1e-1)))
    ssd_dt_bias = dt0 + jnp.log(-jnp.expm1(-dt0))
    ssd_a_log = jnp.log(jax.random.uniform(next(ks), (N_SSD, 2, SSD_HEADS), F32, 1.0, 16.0))
    ssd_d = 1.0 + nrm((N_SSD, SSD_HEADS), 0.02)
    ssd_norm_g = 1.0 + nrm((N_SSD, SSD_INNER), 0.02)
    ssd_w_out = nrm((N_SSD, SSD_INNER, D_MODEL), SSD_INNER ** -0.5)
    da_w_in = nrm((N_ATT, D_MODEL, DA_IN_DIM), D_MODEL ** -0.5)
    da_q_norm = 1.0 + nrm((N_ATT, 2, DA_HEAD_DIM), 0.02)
    da_k_norm = 1.0 + nrm((N_ATT, 2, DA_HEAD_DIM), 0.02)
    da_lam_q = nrm((N_ATT, 2, DA_HEAD_DIM), 0.1)
    da_lam_k = nrm((N_ATT, 2, DA_HEAD_DIM), 0.1)
    da_sub_norm = 1.0 + nrm((N_ATT, DA_V_DIM), 0.02)
    da_w_out = nrm((N_ATT, DA_HEADS * DA_V_DIM, D_MODEL), (DA_HEADS * DA_V_DIM) ** -0.5)
    router_w = nrm((D_MODEL, N_EXPERTS), D_MODEL ** -0.5)
    router_b = nrm((N_EXPERTS,), 0.01)
    moe_w_gate = nrm((DEPTH, N_EXPERTS, D_MODEL, D_EXPERT), D_MODEL ** -0.5)
    moe_w_up = nrm((DEPTH, N_EXPERTS, D_MODEL, D_EXPERT), D_MODEL ** -0.5)
    moe_w_down = nrm((DEPTH, N_EXPERTS, D_EXPERT, D_MODEL), D_EXPERT ** -0.5)
    return {"x": x, "c": c, "ctx": ctx, "c_ctx": c_ctx, "ada_w": ada_w, "ada_b": ada_b,
            "norm1_g": norm1_g, "norm2_g": norm2_g,
            "ssd_w_in": ssd_w_in, "ssd_conv_w": ssd_conv_w, "ssd_conv_b": ssd_conv_b,
            "ssd_dt_bias": ssd_dt_bias, "ssd_a_log": ssd_a_log, "ssd_d": ssd_d,
            "ssd_norm_g": ssd_norm_g, "ssd_w_out": ssd_w_out,
            "da_w_in": da_w_in, "da_q_norm": da_q_norm, "da_k_norm": da_k_norm,
            "da_lam_q": da_lam_q, "da_lam_k": da_lam_k, "da_sub_norm": da_sub_norm, "da_w_out": da_w_out,
            "router_w": router_w, "router_b": router_b,
            "moe_w_gate": moe_w_gate, "moe_w_up": moe_w_up, "moe_w_down": moe_w_down}

def reference(x, c, ctx, c_ctx, ada_w, ada_b, norm1_g, norm2_g,
              ssd_w_in, ssd_conv_w, ssd_conv_b, ssd_dt_bias, ssd_a_log, ssd_d, ssd_norm_g, ssd_w_out,
              da_w_in, da_q_norm, da_k_norm, da_lam_q, da_lam_k, da_sub_norm, da_w_out,
              router_w, router_b, moe_w_gate, moe_w_up, moe_w_down):
    n_ctx = ctx.shape[1]
    xl, xc = x, ctx
    for i in range(DEPTH):
        need_ctx = i < DEPTH - 1
        mod_l = (jax.nn.silu(c) @ ada_w[i] + ada_b[i])[:, None, :]
        mod_c = (jax.nn.silu(c_ctx) @ ada_w[i] + ada_b[i])[None, None, :]
        sh1, sc1, g1, sh2, sc2, g2 = jnp.split(mod_l, 6, axis=-1)
        csh1, csc1, cg1, csh2, csc2, cg2 = jnp.split(mod_c, 6, axis=-1)
        hl = modulate(rmsnorm(xl, norm1_g[i]), sh1, sc1)
        hc = modulate(rmsnorm(xc, norm1_g[i]), csh1, csc1)
        j = i // N_MIXERS
        if i % N_MIXERS == 0:
            yl, yc = ssd_mixer(hl, hc, ssd_w_in[j], ssd_conv_w[j], ssd_conv_b[j], ssd_dt_bias[j],
                               ssd_a_log[j], ssd_d[j], ssd_norm_g[j], ssd_w_out[j], need_ctx)
        else:
            lam_init = 0.8 - 0.6 * math.exp(-0.3 * i)
            yl, yc = diff_attn_mixer(hl, hc, da_w_in[j], da_q_norm[j], da_k_norm[j], da_lam_q[j],
                                     da_lam_k[j], da_sub_norm[j], da_w_out[j], lam_init, need_ctx)
        xl = xl + g1 * yl
        hl2 = modulate(rmsnorm(xl, norm2_g[i]), sh2, sc2)
        if need_ctx:
            xc = xc + cg1 * yc
            hc2 = modulate(rmsnorm(xc, norm2_g[i]), csh2, csc2)
            m = grouped_moe(jnp.concatenate([hc2, hl2], axis=1), router_w, router_b,
                            moe_w_gate[i], moe_w_up[i], moe_w_down[i])
            xc = xc + cg2 * m[:, :n_ctx]
            xl = xl + g2 * m[:, n_ctx:]
        else:
            xl = xl + g2 * grouped_moe(hl2, router_w, router_b, moe_w_gate[i], moe_w_up[i], moe_w_down[i])
    return xl


_drawn_inputs = setup_inputs


def setup_inputs(seed=0):
    import zlib

    import numpy as np

    out = dict(_drawn_inputs(seed))
    spreads = {}
    factors = {'ssd_d': 3.208,
     'da_q_norm': 6.61,
     'da_k_norm': 8.0,
     'da_lam_k': 4.095,
     'da_sub_norm': 4.488}
    for name, (base, spread) in spreads.items():
        noise = np.random.default_rng([zlib.crc32(name.encode()), seed]).standard_normal(out[name].shape)
        drawn = base * np.exp(spread * noise) if base else spread * noise
        out[name] = __import__('jax').numpy.asarray(drawn.astype(out[name].dtype))
    for name, factor in factors.items():
        out[name] = (out[name] * factor).astype(out[name].dtype)
    return out
```

```python
import math
from contextlib import ExitStack

import numpy as np
import concourse.bass as bass
from concourse import mybir

F32 = mybir.dt.float32
I32 = mybir.dt.int32
U32 = mybir.dt.uint32
ALU = mybir.AluOpType
ACT = mybir.ActivationFunctionType
AX = mybir.AxisListType

P = 128
D = 1024
KD = D // P
TT = 4
T = TT * P
NB = 512
EPS = 1e-6
SLOTS = 6
SLOT = 4096

INNER = 2048
HEADS = 32
HD = 64
GROUPS = 4
HPG = HEADS // GROUPS
STATE = 128
TAPS = 5
CONV = INNER + 2 * GROUPS * STATE
PAD = TAPS // 2
SEG = 2 * P
IN_DT = INNER + CONV

DA_H = 8
DA_D = 64
DA_V = 128
LAM_INIT = 0.8 - 0.6 * math.exp(-0.3 * 1)

NE = 16
NG = 4
EPG = NE // NG
DE = D // 2
CAP = P
BIG = 1.0e30


class Chain:

    def __init__(self, eng, sem):
        self.eng, self.sem, self.at, self.k = eng, sem, 0, 0

    def __call__(self, ins):
        ins.then_inc(self.sem, 1)
        self.k += 1
        self.eng.wait_ge(self.sem, self.at + self.k)
        return ins

    def enter(self, i, per):
        self.start = self.at + self.k
        self.at, self.k, self.per = i * per + self.start, 0, per

    def leave_body(self):
        assert self.k == self.per, self.k

    def leave(self, n):
        self.at, self.k = 0, self.start + n * self.per


def rope_tables():
    t = np.arange(SEG)
    pos = np.stack([t // 64, t % 64], -1).astype(np.float32)
    n_freq = DA_D // 4
    inv = (10000.0 ** (-np.arange(n_freq, dtype=np.float32) / n_freq)).astype(np.float32)
    ang = pos[..., None] * inv
    cos, sin = np.cos(ang).astype(np.float32), np.sin(ang).astype(np.float32)
    c = np.stack([cos, cos], 2).reshape(SEG, DA_D)
    s = np.stack([-sin, sin], 2).reshape(SEG, DA_D)
    return np.stack([c, s], 1)


def backbone(nc, x, c, ctx, c_ctx, ada_w, ada_b, norm1_g, norm2_g,
             ssd_w_in, ssd_conv_w, ssd_conv_b, ssd_dt_bias, ssd_a_log, ssd_d, ssd_norm_g, ssd_w_out,
             da_w_in, da_q_norm, da_k_norm, da_lam_q, da_lam_k, da_sub_norm, da_w_out,
             router_w, router_b, moe_w_gate, moe_w_up, moe_w_down, out):
    es = ExitStack()
    with es:
        def sb(name, shape, dt=F32):
            return es.enter_context(nc.sbuf_tensor(name, shape, dt))

        def sem(name):
            return es.enter_context(nc.semaphore(name))

        ring = sb("ring", [P, SLOTS, SLOT])
        X = sb("X", [P, TT, D])
        hT = sb("hT", [P, KD, T])
        ARENA = 18432
        arena = sb("arena", [P, ARENA])
        ident = sb("ident", [P, P])
        tri_up = sb("tri_up", [P, P])
        tri_lo = sb("tri_lo", [P, P])
        ones = sb("ones", [P, P])
        cols = sb("cols", [P, 176])
        small = sb("small", [P, 32])
        psum = es.enter_context(nc.psum_tensor("psum", [P, 8, NB], F32))
        dts = sb("dts", [P, 5, 4 * 64])
        mhalf = small[:, 0:1]
        zero_col, inv_inner, eps_col = (small[:, n:n + 1] for n in (13, 14, 15))
        ss = small[:, 1:5]
        rstd = small[:, 8:12]

        def carve(base, at, *shape):
            n = int(np.prod(shape))
            v = base[:, at:at + n]
            if len(shape) == 2:
                v = v.rearrange("p (a b) -> p a b", a=shape[0])
            if len(shape) == 3:
                v = v.rearrange("p (a b c) -> p a b c", a=shape[0], b=shape[1])
            return v

        def slot(s, a):
            return ring[:, s, :].rearrange("p (a b) -> p a b", a=a)

        mod_d = nc.dram_tensor("mod_d", [6, 2, 2 * D], F32).ap()
        acs_d = nc.dram_tensor("acs_d", [TT, 2 * HEADS, P], F32).ap()
        zs_d = nc.dram_tensor("zs_d", [TT, P, INNER], F32).ap()
        id_d = nc.inline_tensor(np.eye(P, dtype=np.float32), "id_d").ap()
        up_d = nc.inline_tensor(np.triu(np.ones((P, P), np.float32)), "up_d").ap()
        lo_d = nc.inline_tensor(np.tril(np.ones((P, P), np.float32)), "lo_d").ap()
        rope_d = nc.inline_tensor(rope_tables(), "rope_d").ap()

        full = [sem(f"slot{s}_full") for s in range(SLOTS)]

        def load(eng, s, src, a):
            eng.dma_start(slot(s, a), src).then_inc(full[s], 16)

        def wait_full(pe, s, fill):
            pe.wait_ge(full[s], fill * 16 + 16)

        def row(v):
            return v.rearrange("(o n) -> o n", o=1).broadcast_to([P, v.shape[0]])

        def mod_row(layer, v, cond):
            q = 3 * layer + v // 2
            return row(mod_d[q, cond, (v % 2) * D:(v % 2 + 1) * D])

        def blocks(w, c0, n=NB):
            return w[:, c0:c0 + n].rearrange("(k p) n -> p k n", p=P)

        Xflat = X[:, :, :].rearrange("p t n -> p (t n)")
        hflat = hT[:, :, :].rearrange("p k t -> p (k t)")
        xa = carve(arena, 0, TT, D)
        rows1 = carve(arena, 12288, P)
        rows2 = carve(arena, 12288 + P, P)
        N1, N2 = TAPS * CONV // P, 24 + 16 + 8 + 8
        TAP0, CB0, SN0, CC0 = 0, N1, N1 + 24, N1 + 40
        c_sil = carve(Xflat, 0, KD, 32)
        ada_row = carve(Xflat, 256, 2 * D)
        mod_sb = carve(Xflat, 2304, NB)
        w_dt = carve(Xflat, 2816, KD, 64)
        Abc = carve(arena, 4096, 2, D)
        Sbc = carve(arena, 6144, 2, D)
        gbc = carve(arena, 8192, D)
        hbuf = carve(arena, 9216, 2, D)
        junk = carve(arena, 11264, D)

        consts_in = sem("consts_in")
        rows_in = sem("rows_in")
        x_in = sem("x_in")
        pool_set = sem("pool_set")
        rows_T = sem("rows_transposed")
        cols_ready = sem("cols_ready")
        csil_ready = sem("csil_ready")
        adab_in = sem("adab_in")
        ada_done = sem("ada_psum_done")
        ada_copied = sem("ada_copied")
        mod_out = sem("mod_out")
        dve_step = sem("dve_step")
        act_step = sem("act_step")
        pool_step = sem("pool_step")

        def setup_sync(sp):
            for dst, src in ((ident, id_d), (tri_up, up_d), (tri_lo, lo_d)):
                sp.dma_start(dst[:, :], src).then_inc(consts_in, 16)
            sp.dma_start(rows1[0:N1, :], ssd_conv_w[0].rearrange("j (t c) -> (j t) c", c=P)).then_inc(rows_in, 16)
            for r, v in ((0, ssd_conv_b[0]), (24, ssd_norm_g[0]), (40, c[0]), (48, c_ctx)):
                n = v.shape[0] // P
                sp.dma_start(rows2[r:r + n, :], v.rearrange("(t c) -> t c", c=P)).then_inc(rows_in, 16)

        def load_x(eng, dst, signal):
            for half, src in ((0, ctx), (2, x)):
                eng.dma_start(dst[:, half:half + 2, :], src[0].rearrange("(t p) n -> p t n", p=P)).then_inc(signal, 16)

        def setup_pool(pool):
            pool.memset(ones[:, :], 1.0).then_inc(pool_set, 1)
            pool.memset(small[:, :], 0.0).then_inc(pool_set, 1)
            pool.memset(Xflat[:, 0:256], 0.0).then_inc(pool_set, 1)
            pool.wait_ge(pool_set, 3)
            pool.memset(mhalf, -0.5).then_inc(pool_set, 1)
            pool.memset(inv_inner, 1.0 / INNER).then_inc(pool_set, 1)
            pool.memset(eps_col, EPS).then_inc(pool_set, 1)
            pool.wait_ge(pool_set, 6)

        def setup_tensor(pe):
            pe.wait_ge(consts_in, 48)
            pe.wait_ge(rows_in, 80)
            pe.transpose(psum[:, 6, 0:N1], rows1[0:N1, :], ident[0:N1, 0:N1])
            pe.transpose(psum[:, 6, N1:N1 + N2], rows2[0:N2, :], ident[0:N2, 0:N2]).then_inc(rows_T, 1)

        def setup_vector(v, step):
            v.wait_ge(rows_T, 1)
            v.tensor_copy(cols[:, 0:N1 + N2], psum[:, 6, 0:N1 + N2]).then_inc(cols_ready, 1)

        def setup_scalar(act):
            act.wait_ge(cols_ready, 1)
            act.wait_ge(pool_set, 6)
            for cond, at in ((0, CC0 + 8), (1, CC0)):
                act.activation(c_sil[:, :, cond], cols[:, at:at + KD], ACT.Silu).then_inc(csil_ready, 1)

        def ada_sync(sp, q):
            if q:
                sp.wait_ge(ada_done, q)
            for j in range(4):
                load(sp, j, blocks(ada_w[q // 3], (q % 3) * 2 * D + j * NB), KD)

        def ada_tensor(pe, q):
            for j in range(4):
                wait_full(pe, j, q)
            pe.wait_ge(adab_in, 16 * q + 16)
            if q:
                pe.wait_ge(ada_copied, q)
            else:
                pe.wait_ge(csil_ready, 2)
            for j in range(4):
                pe.matmul(psum[32 * j:32 * j + 32, 7, :], ones[0:1, 0:32], ada_row[0:1, j * NB:(j + 1) * NB],
                          start=True, stop=False)
            for k in range(KD):
                for j in range(4):
                    m = pe.matmul(psum[32 * j:32 * j + 32, 7, :], c_sil[:, k, :], slot(j, KD)[:, k, :],
                                  start=False, stop=(k == KD - 1))
            m.then_inc(ada_done, 1)

        def ada_scalar(act, q):
            act.wait_ge(ada_done, q + 1)
            if q:
                act.wait_ge(mod_out, 32 * q)
            act.activation(mod_sb, psum[:, 7, :], ACT.Copy).then_inc(ada_copied, 1)
            act.wait_ge(ada_copied, q + 1)
            for cond in range(2):
                act.dma_start(mod_d[q, cond, :].rearrange("(j n) -> j n", j=4),
                              mod_sb[cond:cond + 97:32, :]).then_inc(mod_out, 16)
            if q < 5:
                act.dma_start(ada_row[0:1, :], ada_bias(q + 1)).then_inc(adab_in, 16)

        def ada_bias(q):
            return ada_b[q // 3:q // 3 + 1, (q % 3) * 2 * D:(q % 3 + 1) * 2 * D]

        class Norm:

            def __init__(self, tag, src, layer, g, v_shift, tiles, conds, base, before):
                self.src = src
                self.layer, self.g, self.vs, self.tiles, self.conds = layer, g, v_shift, tiles, conds
                if before is None:
                    self.s = dict(**{n: sem(f"norm_{n}") for n in "par_in sumsq rst h_ready h_T evac".split()})
                    self.at = dict(par_in=0, sumsq=0, rst=0, h_ready=0, h_T=0, evac=0)
                else:
                    b, n = before.at, len(before.tiles)
                    self.s = before.s
                    self.at = dict(par_in=b["par_in"] + 16 * (1 + 2 * len(before.conds)), sumsq=b["sumsq"] + n, rst=b["rst"] + n,
                                              h_ready=b["h_ready"] + n, h_T=b["h_T"] + n, evac=b["evac"] + 2 * n)
                self.A, self.S, self.gb, self.h, self.junk = base

            def load(self, eng, wait):
                wait(eng)
                eng.dma_start(self.gb, row(self.g)).then_inc(self.s["par_in"], 16)
                for cd in self.conds:
                    eng.dma_start(self.A[:, cd - self.conds[0], :], mod_row(self.layer, self.vs + 1, cd)).then_inc(self.s["par_in"], 16)
                    eng.dma_start(self.S[:, cd - self.conds[0], :], mod_row(self.layer, self.vs, cd)).then_inc(self.s["par_in"], 16)

            def scalar(self, act, wait):
                wait(act)
                for n, t in enumerate(self.tiles):
                    if self.src_ready:
                        act.wait_ge(*self.src_ready[n])
                    act.activation(self.junk, self.src[:, t, :], ACT.Square, accum_out=ss[:, t:t + 1]).then_inc(self.s["sumsq"], 1)
                    act.wait_ge(self.s["sumsq"], self.at["sumsq"] + n + 1)
                for n, t in enumerate(self.tiles):
                    if self.store:
                        act.wait_ge(self.s["h_ready"], self.at["h_ready"] + n + 1)
                        act.dma_start(self.h_d[n * P:(n + 1) * P, :], self.h[:, n % 2, :]).then_inc(self.stored[n % 2], 16)
                    act.wait_ge(self.s["h_T"], self.at["h_T"] + n + 1)
                    for hf in range(2):
                        act.activation(hT[:, 4 * hf:4 * hf + 4, t * P:(t + 1) * P],
                                       psum[:, 2 * (n % 2) + hf, :].rearrange("p (k t) -> p k t", k=4),
                                       ACT.Copy).then_inc(self.s["evac"], 1)

            def pool(self, pool, step):
                for n, t in enumerate(self.tiles):
                    pool.wait_ge(self.s["sumsq"], self.at["sumsq"] + n + 1)
                    step(pool.tensor_scalar(ss[:, t:t + 1], ss[:, t:t + 1], 1.0 / D, EPS, ALU.mult, ALU.add))
                    pool.tensor_tensor(out=rstd[:, t:t + 1], in0=ss[:, t:t + 1], in1=mhalf, op=ALU.pow).then_inc(self.s["rst"], 1)

            def vector(self, v, step):
                v.wait_ge(self.s["par_in"], self.at["par_in"] + 16 * (1 + 2 * len(self.conds)))
                for cd in self.conds:
                    step(v.scalar_tensor_tensor(out=self.A[:, cd - self.conds[0], :], in0=self.A[:, cd - self.conds[0], :], scalar=1.0,
                                                in1=self.gb, op0=ALU.add, op1=ALU.mult))
                for n, t in enumerate(self.tiles):
                    cd = 0 if t < 2 else 1
                    v.wait_ge(self.s["rst"], self.at["rst"] + n + 1)
                    if n >= 2:
                        v.wait_ge(self.s["h_T"], self.at["h_T"] + n - 1)
                        if self.store:
                            v.wait_ge(self.stored[n % 2], self.stored_at + 16 * (n // 2))
                    step(v.scalar_tensor_tensor(out=self.h[:, n % 2, :], in0=self.src[:, t, :], scalar=rstd[:, t:t + 1],
                                                in1=self.A[:, cd - self.conds[0], :], op0=ALU.mult, op1=ALU.mult))
                    v.tensor_tensor(out=self.h[:, n % 2, :], in0=self.h[:, n % 2, :], in1=self.S[:, cd - self.conds[0], :],
                                    op=ALU.add).then_inc(self.s["h_ready"], 1)
            store = False
            src_ready = None

            def tensor(self, pe):
                for n, t in enumerate(self.tiles):
                    pe.wait_ge(self.s["h_ready"], self.at["h_ready"] + n + 1)
                    if n >= 2:
                        pe.wait_ge(self.s["evac"], self.at["evac"] + 2 * (n - 1))
                    for k in range(KD):
                        m = pe.transpose(psum[:, 2 * (n % 2) + k // 4, (k % 4) * P:(k % 4 + 1) * P],
                                         self.h[:, n % 2, k * P:(k + 1) * P], ident[:, :])
                    m.then_inc(self.s["h_T"], 1)

        norm_a = Norm("norm_a", xa, 0, norm1_g[0], 0, range(TT), (0, 1), (Abc, Sbc, gbc, hbuf, junk), None)

        xtok = carve(arena, 0, TT, INNER)
        BC = carve(arena, 8192, 8, T)
        Bt = carve(arena, 12288, TT, GROUPS * STATE)
        U = carve(arena, 14336, 2, 2, SEG + 2 * PAD)
        conv = carve(arena, 14336 + 1040, 2, T)
        xs = carve(arena, 14336 + 1040 + 1024, 2, T)
        v_dt = carve(arena, 12288, T)
        e_dt = carve(arena, 12800, T)
        dtT = carve(arena, 17424, T)
        dt_b = small[0:64, 12:13]
        expA = cols[:, 0:64]
        d_skip = cols[:, 64:96]
        dt, acs, eacs, wend, dec = (dts[:, n, :] for n in range(5))

        w_dt_in = sem("w_dt_in")
        pads_set = sem("pads_set")
        dt_mm = sem("dt_mm")
        dt_neg = sem("dt_neg")
        dt_ln = sem("dt_ln")
        dt_T = sem("dt_T")
        dt_tok_mm = sem("dt_tok_mm")
        heads_in = sem("heads_in")
        expa_ready = sem("expa_ready")
        a_ready = sem("a_ready")
        acs_mm = sem("acs_mm")
        acs_copied = sem("acs_copied")
        acs_exp = sem("acs_exp")
        acs_stored = sem("acs_stored")
        acsT_ready = sem("acsT_ready")
        dt_all = sem("dt_all")
        xb_mm = sem("conv_in_psum")
        xb_copied = sem("conv_in_copied")
        xb_conv = sem("conv_done")
        xb_silu = sem("conv_silu")
        xb_T = sem("conv_transposed")
        xb_out = sem("conv_tok_ready")
        z_mm = sem("z_mm")
        z_silu = sem("z_silu")
        z_stored = [sem(f"z_stored{n}") for n in range(2)]

        w_in = ssd_w_in[0]

        def dt_tensor(pe):
            pe.wait_ge(w_dt_in, 32)
            pe.wait_ge(norm_a.s["evac"], 2 * TT)
            for k in range(KD):
                m = pe.matmul(psum[0:64, 4, :], w_dt[:, k, :], hT[:, k, :], start=(k == 0), stop=(k == KD - 1))
            m.then_inc(dt_mm, 1)

        def dt_vector(v, step):
            v.wait_ge(dt_mm, 1)
            step(v.tensor_scalar(v_dt[0:64, :], psum[0:64, 4, :], dt_b, None, ALU.add))
            v.scalar_tensor_tensor(out=e_dt[0:64, :], in0=v_dt[0:64, :], scalar=-1.0, in1=v_dt[0:64, :],
                                   op0=ALU.mult, op1=ALU.min).then_inc(dt_neg, 1)
            v.wait_ge(dt_ln, 2)
            v.scalar_tensor_tensor(out=dtT[0:64, :], in0=v_dt[0:64, :], scalar=0.0, in1=e_dt[0:64, :],
                                   op0=ALU.max, op1=ALU.add).then_inc(dt_T, 1)

        def dt_scalar(act):
            act.wait_ge(dt_neg, 1)
            act.activation(e_dt[0:64, :], e_dt[0:64, :], ACT.Exp).then_inc(dt_ln, 1)
            act.wait_ge(dt_ln, 1)
            act.activation(e_dt[0:64, :], e_dt[0:64, :], ACT.Ln, bias=1.0).then_inc(dt_ln, 1)

        def xb_project(pe, n, slot_, ct, j):
            if not (isinstance(n, int) and n < 2):
                pe.wait_ge(xb_copied, n - 1)
            for k in range(KD):
                m = pe.matmul(psum[:, j, :], slot(slot_, KD)[:, k, ct * P:(ct + 1) * P], hT[:, k, :],
                              start=(k == 0), stop=(k == KD - 1))
            m.then_inc(xb_mm, 1)

        def xb_transpose(pe, n, j, src):
            pe.wait_ge(xb_silu, n + 1)
            if not (isinstance(n, int) and n < 2):
                pe.wait_ge(xb_out, n - 1)
            for t in range(TT):
                m = pe.transpose(psum[:, 2 + j, t * P:(t + 1) * P], src[:, t * P:(t + 1) * P], ident[:, :])
            m.then_inc(xb_T, 1)

        def xb_scalar(act, n, j, post, peeled):
            act.wait_ge(xb_conv, n + 1)
            dst = xs[:, j, :] if post == "x" else BC[:, n - 16, :]
            act.activation(dst, conv[:, j, :], ACT.Silu).then_inc(xb_silu, 1)
            if not (isinstance(n, int) and n == 23):
                xb_copy(act, n + 1, 1 - j)
            if post == "C":
                return
            act.wait_ge(xb_T, n + 1)
            src = psum[:, 2 + j, :].rearrange("p (t c) -> p t c", t=TT)
            dst = xtok[:, :, bass.ds(n * P, P)] if post == "x" else Bt[:, :, (n - 16) * P:(n - 15) * P]
            act.activation(dst, src, ACT.Copy).then_inc(xb_out, 1)

        def xb_copy(act, n, j):
            act.wait_ge(xb_mm, n + 1)
            act.activation(U[:, j, :, PAD:PAD + SEG], psum[:, j, :].rearrange("p (s t) -> p s t", s=2),
                           ACT.Copy).then_inc(xb_copied, 1)

        def xb_vector(v, n, j, step, peeled):
            v.wait_ge(xb_copied, n + 1)
            if not (isinstance(n, int) and n < 2):
                v.wait_ge(xb_silu, n - 1)
            o = conv[:, j, :].rearrange("p (s t) -> p s t", s=2)
            step(v.tensor_scalar(o, U[:, j, :, 0:SEG], cols[:, bass.ds(TAP0 + n, 1)], cols[:, bass.ds(CB0 + n, 1)],
                                 ALU.mult, ALU.add))
            for tap in range(1, TAPS):
                m = v.scalar_tensor_tensor(out=o, in0=U[:, j, :, tap:tap + SEG], scalar=cols[:, bass.ds(TAP0 + 24 * tap + n, 1)],
                                           in1=o, op0=ALU.mult, op1=ALU.add)
                if tap < TAPS - 1:
                    step(m)
                else:
                    m.then_inc(xb_conv, 1)

        def xb_load(sp, i, odd, wait):
            if wait is not None:
                sp.wait_ge(xb_mm, wait)
            load(sp, 4 + odd, w_in[:, bass.ds(i * NB + INNER, NB)].rearrange("(k p) n -> p k n", p=P), KD)

        def proj_sync(sp):
            xb_load(sp, 0, 0, None)
            xb_load(sp, 1, 1, None)
            for i in range(2, 6):
                ada_sync(sp, i - 1)
                xb_load(sp, i, i % 2, 4 * (i - 1))
            ada_sync(sp, 5)
            sp.wait_ge(ada_done, 6)
            for n in range(4):
                load(sp, n, blocks(w_in, n * NB), KD)
            for n in range(4):
                for t in range(TT):
                    m = n * TT + t
                    sp.wait_ge(z_silu, m + 1)
                    sp.dma_start(zs_d[t, :, n * NB:(n + 1) * NB], xs[:, m % 2, :]).then_inc(z_stored[m % 2], 16)
                if n == 0:
                    sp.wait_ge(acsT_ready, 1)
                    sp.dma_start(acs_d.rearrange("c r l -> r c l"), dtT[0:64, :].rearrange("r (c l) -> r c l", c=TT)).then_inc(acs_stored, 16)

        def proj_tensor(pe):
            dt_tensor(pe)
            wait_full(pe, 4, 0)
            xb_project(pe, 0, 4, 0, 0)
            wait_full(pe, 5, 0)
            for i in range(6):
                for ct in range(4):
                    n = 4 * i + ct
                    if n < 23:
                        if ct == 3:
                            wait_full(pe, 4 + (i + 1) % 2, (i + 1) // 2)
                        xb_project(pe, n + 1, 4 + ((n + 1) // 4) % 2, (n + 1) % 4, (n + 1) % 2)
                    if n < 20:
                        xb_transpose(pe, n, n % 2, xs[:, n % 2, :] if n < 16 else BC[:, n - 16, :])
                if i < 5:
                    ada_tensor(pe, i + 1)
            pe.wait_ge(dt_T, 1)
            for t in range(TT):
                m = pe.transpose(psum[:, 5, t * 64:(t + 1) * 64], dtT[0:64, t * P:(t + 1) * P], ident[0:64, 0:64])
            m.then_inc(dt_tok_mm, 1)
            for n in range(4):
                for t in range(TT):
                    m_ = n * TT + t
                    if t == 0:
                        wait_full(pe, n, 6)
                    if m_ >= 2:
                        pe.wait_ge(z_silu, m_ - 1)
                    else:
                        pe.wait_ge(xb_copied, 24)
                    for k in range(KD):
                        m = pe.matmul(psum[:, m_ % 2, :], hT[:, k, t * P:(t + 1) * P], slot(n, KD)[:, k, :],
                                      start=(k == 0), stop=(k == KD - 1))
                    m.then_inc(z_mm, 1)
                if n == 0:
                    acs_tensor(pe)

        def acs_tensor(pe):
            pe.wait_ge(a_ready, 1)
            a4 = dec.rearrange("p (c r) -> p c r", c=TT)
            pe.matmul(psum[:, 4, 0:128].rearrange("p (c r) -> p c r", c=TT), tri_up[:, :], a4[:, :, 0:HEADS], start=True, stop=True)
            pe.matmul(psum[:, 4, 128:256].rearrange("p (c r) -> p c r", c=TT), tri_lo[:, :], a4[:, :, HEADS:64], start=True, stop=True)
            pe.matmul(psum[:, 4, 256:512], ones[:, :], dec, start=True, stop=True)
            for c_ in range(TT):
                for d_, tri in ((0, tri_up), (1, tri_lo)):
                    m = pe.matmul(psum[32 * d_:32 * d_ + 32, 5, c_ * P:(c_ + 1) * P], a4[:, c_, 32 * d_:32 * d_ + 32], tri[:, :],
                                  start=True, stop=True)
            m.then_inc(acs_mm, 1)

        def proj_scalar(act):
            dt_scalar(act)
            xb_copy(act, 0, 0)
            for i in range(6):
                for ct in range(4):
                    n = 4 * i + ct
                    xb_scalar(act, n, n % 2, "x" if n < 16 else "B" if n < 20 else "C", True)
                if i < 5:
                    ada_scalar(act, i + 1)
            act.wait_ge(xb_conv, 24)
            act.dma_start(expA, row(ssd_a_log[0].rearrange("d h -> (d h)"))).then_inc(heads_in, 16)
            act.dma_start(d_skip, row(ssd_d[0])).then_inc(heads_in, 16)
            act.wait_ge(heads_in, 32)
            act.activation(expA, expA, ACT.Exp).then_inc(expa_ready, 1)
            for n in range(4):
                for t in range(TT):
                    m = n * TT + t
                    act.wait_ge(z_mm, m + 1)
                    if m >= 2:
                        act.wait_ge(z_stored[m % 2], 16 * (m // 2))
                    else:
                        act.wait_ge(xb_T, 20)
                    act.activation(xs[:, m % 2, :], psum[:, m % 2, :], ACT.Silu).then_inc(z_silu, 1)
            act.wait_ge(acs_copied, 1)
            for n, (dst, src) in enumerate(((eacs, acs), (wend, wend), (dec, dec))):
                act.activation(dst, src, ACT.Exp).then_inc(acs_exp, 1)

        def proj_vector(v, step):
            dt_vector(v, step)
            for n in range(24):
                xb_vector(v, n, n % 2, step, True)
            v.wait_ge(dt_tok_mm, 1)
            v.wait_ge(expa_ready, 1)
            step(v.tensor_copy(dt, psum[:, 5, 0:256]))
            v.scalar_tensor_tensor(out=dec.rearrange("p (c r) -> p c r", c=TT), in0=dt.rearrange("p (c r) -> p c r", c=TT),
                                   scalar=-1.0, in1=expA.rearrange("p (o r) -> p o r", o=1).broadcast_to([P, TT, 64]),
                                   op0=ALU.mult, op1=ALU.mult).then_inc(a_ready, 1)
            v.wait_ge(acs_mm, 1)
            a4 = acs.rearrange("p (c r) -> p c r", c=TT)
            v.tensor_copy(dtT[0:64, :], psum[0:64, 5, :]).then_inc(acsT_ready, 1)
            step(v.tensor_copy(a4[:, :, 0:HEADS], psum[:, 4, 0:128].rearrange("p (c r) -> p c r", c=TT)))
            step(v.tensor_copy(a4[:, :, HEADS:64], psum[:, 4, 128:256].rearrange("p (c r) -> p c r", c=TT)))
            step(v.tensor_copy(dec, psum[:, 4, 256:512]))
            v.tensor_tensor(out=wend, in0=dec, in1=acs, op=ALU.subtract).then_inc(acs_copied, 1)
            v.wait_ge(acs_exp, 3)
            v.tensor_tensor(out=wend, in0=wend, in1=dt, op=ALU.mult).then_inc(dt_all, 1)

        ringflat = ring[:, :, :].rearrange("p s n -> p (s n)")
        R = carve(ringflat, 2 * SLOT, TT, INNER)
        E = [carve(ringflat, 0, HEADS, P), carve(Xflat, 0, HEADS, P)]
        XS = carve(ringflat, SLOT, 2, INNER)
        y = carve(hflat, 0, INNER)
        zs = carve(hflat, INNER, INNER)
        cbm = carve(hflat, INNER, 2, GROUPS * P)
        F = carve(arena, 14336, INNER)
        cur = carve(arena, 16384, 3, GROUPS, P)
        tmp = carve(arena, 17920, NB)
        GB = carve(arena, 14336, 2, D)
        yT = carve(ringflat, 2 * SLOT, KD * 2, T)

        cleared = sem("states_cleared")
        xd_ready = sem("xd_ready")
        st_mm = sem("state_mm")
        st_used = sem("state_used")
        g_used = sem("g_used")
        cur_ready = sem("cur_ready")
        e_in = [sem(f"decay_in{d}") for d in range(2)]
        diff = [sem(f"decay_diff{d}") for d in range(2)]
        e_exp = [sem(f"decay_exp{d}") for d in range(2)]
        xs_ready = sem("xs_ready")
        cb_mm = sem("cb_mm")
        cb_ready = sem("cb_masked")
        g_ready = sem("g_ready")
        off_mm = sem("off_mm")
        off_used = sem("off_used")
        zs_in = sem("zs_in")
        gated = sem("gated")
        y_sq = sem("y_sumsq")
        y_rst = sem("y_rstd")
        yn_ready = sem("yn_ready")
        yT_mm = sem("y_transposed")
        yT_ready = sem("yT_ready")
        x_back = sem("x_back")
        gate_in = sem("gate_in")
        wo_mm = sem("wo_mm")
        wo_added = sem("wo_added")
        BACK = ((1, None, 0), (0, 0, 3), (3, 3, 2))

        def over(v, n, at):
            return v.rearrange("p (h o) -> p h o", o=1).broadcast_to([P, v.shape[1], n])

        def heads(v):
            return v.rearrange("p (h e) -> p h e", h=HEADS)

        def per(v, c_, d_):
            return v[:, bass.ds(c_ * 64 + 32 * d_, HEADS)]

        def scan_pool_start(pool):
            pool.wait_ge(z_mm, 16)
            pool.memset(R[:, 1, :], 0.0).then_inc(cleared, 1)
            pool.wait_ge(z_stored[0], 128)
            pool.wait_ge(z_stored[1], 128)
            pool.wait_ge(acs_stored, 16)
            pool.memset(F, 0.0).then_inc(cleared, 1)

        def back_vector(v, step):
            v.wait_ge(dt_all, 1)
            v.wait_ge(z_mm, 16)
            for r, (c_, src, dst) in enumerate(BACK):
                if r == 2:
                    v.wait_ge(st_mm, 1)
                v.tensor_tensor(out=heads(XS[:, r % 2, :]), in0=heads(xtok[:, c_, :]), in1=over(per(wend, c_, 1), HD, 0),
                                op=ALU.mult).then_inc(xd_ready, 1)
                states = psum[:, 4:8, :].rearrange("p b n -> p (b n)")
                if src is None:
                    v.wait_ge(st_mm, r + 1)
                    v.tensor_copy(R[:, dst, :], states).then_inc(st_used, 1)
                else:
                    step(v.tensor_tensor(out=heads(R[:, dst, :]), in0=heads(R[:, src, :]), in1=over(per(dec, c_, 1), HD, 0),
                                         op=ALU.mult))
                    v.wait_ge(st_mm, r + 1)
                    v.tensor_tensor(out=R[:, dst, :], in0=R[:, dst, :], in1=states, op=ALU.add).then_inc(st_used, 1)
                v.wait_ge(st_used, r + 1)

        def back_tensor(pe):
            for r, (c_, src, dst) in enumerate(BACK):
                pe.wait_ge(xd_ready, r + 1)
                if r:
                    pe.wait_ge(st_used, r)
                for g in range(GROUPS):
                    m = pe.matmul(psum[:, 4 + g, :], Bt[:, c_, g * STATE:(g + 1) * STATE], XS[:, r % 2, g * NB:(g + 1) * NB],
                                  start=True, stop=True)
                    if r == 2 and g == 2:
                        m.then_inc(g_used, 1)
                m.then_inc(st_mm, 1)

        def scan_sync(sp):
            sp.wait_ge(acs_stored, 16)
            sp.wait_ge(mod_out, 192)
            with sp.Fori(0, TT) as c_:
                sp.wait_ge(g_used, c_ + 1)
                for d_ in range(2):
                    src = acs_d[bass.ds(c_, 1), 32 * d_:32 * d_ + 32, :].rearrange("o h l -> o (h l)").broadcast_to([P, HEADS * P])
                    sp.dma_start(E[d_].rearrange("p h l -> p (h l)"), src).then_inc(e_in[d_], 16)
                sp.wait_ge(g_ready, 2 * c_ + 2)
                sp.dma_start(zs, zs_d[bass.ds(c_, 1), :, :].rearrange("o p n -> (o p) n")).then_inc(zs_in, 16)

        def scan_pool(pool, step):
            with pool.Fori(0, TT) as c_:
                step.enter(c_, 2)
                pool.wait_ge(st_mm, c_ + 3)
                for n, src in enumerate((BC[:, 0:4, bass.ds(c_ * P, P)], BC[:, 4:8, bass.ds(c_ * P, P)],
                                         Bt[:, bass.ds(c_, 1), :].rearrange("p o (g n) -> p (o g) n", g=GROUPS))):
                    pool.tensor_copy(cur[:, n, :, :], src).then_inc(cur_ready, 1)
                pool.wait_ge(e_in[1], c_ * 16 + 16)
                pool.tensor_tensor(out=E[1], in0=E[1], in1=over(per(acs, c_, 1), P, 0), op=ALU.subtract).then_inc(diff[1], 1)
                pool.wait_ge(y_sq, c_ + 1)
                step(pool.tensor_tensor(out=ss[:, 0:1], in0=ss[:, 0:1], in1=inv_inner, op=ALU.mult))
                step(pool.tensor_tensor(out=ss[:, 0:1], in0=ss[:, 0:1], in1=eps_col, op=ALU.add))
                pool.tensor_tensor(out=rstd[:, 0:1], in0=ss[:, 0:1], in1=mhalf, op=ALU.pow).then_inc(y_rst, 1)
                step.leave_body()
            step.leave(TT)

        def scan_scalar(act):
            with act.Fori(0, TT) as c_:
                for d_ in range(2):
                    act.wait_ge(diff[d_], c_ + 1)
                    act.activation(E[d_], E[d_], ACT.Relu, scale=-1.0).then_inc(e_exp[d_], 1)
                    act.wait_ge(e_exp[d_], 2 * c_ + 1)
                    act.activation(E[d_], E[d_], ACT.Exp, scale=-1.0).then_inc(e_exp[d_], 1)
                act.wait_ge(gated, c_ + 1)
                act.activation(zs, y, ACT.Square, accum_out=ss[:, 0:1]).then_inc(y_sq, 1)

        def scan_vector(v, step):
            v.wait_ge(cleared, 2)
            with v.Fori(0, TT) as c_:
                step.enter(c_, 11)
                xc = xtok[:, bass.ds(c_, 1), :].rearrange("p o n -> p (o n)")
                v.wait_ge(e_in[0], c_ * 16 + 16)
                v.tensor_tensor(out=E[0], in0=E[0], in1=over(per(acs, c_, 0), P, 0), op=ALU.subtract).then_inc(diff[0], 1)
                v.wait_ge(st_mm, c_ + 3)
                for d_ in range(2):
                    v.tensor_tensor(out=heads(XS[:, d_, :]), in0=heads(xc), in1=over(per(dt, c_, d_), HD, 0),
                                    op=ALU.mult).then_inc(xs_ready, 1)
                v.wait_ge(cb_mm, c_ + 1)
                for d_, tri in ((0, tri_up), (1, tri_lo)):
                    v.tensor_tensor(out=cbm[:, d_, :].rearrange("p (g l) -> p g l", g=GROUPS),
                                    in0=psum[:, 4, :].rearrange("p (g l) -> p g l", g=GROUPS),
                                    in1=tri[:, :].rearrange("p (o l) -> p o l", o=1).broadcast_to([P, GROUPS, P]),
                                    op=ALU.mult).then_inc(cb_ready, 1)
                v.wait_ge(cb_ready, 2 * c_ + 2)
                for d_ in range(2):
                    v.wait_ge(e_exp[d_], 2 * c_ + 2)
                    e4 = E[d_].rearrange("p (g h) l -> p g h l", g=GROUPS)
                    v.tensor_tensor(out=e4, in0=e4, op=ALU.mult,
                                    in1=cbm[:, d_, :].rearrange("p (g o l) -> p g o l", g=GROUPS, o=1).broadcast_to([P, GROUPS, HPG, P]),
                                    ).then_inc(g_ready, 1)
                step(v.tensor_tensor(out=heads(y), in0=heads(xc), in1=over(d_skip, HD, 0), op=ALU.mult))
                for d_ in range(2):
                    v.wait_ge(off_mm, 2 * c_ + (d_ + 1))
                    for g in range(GROUPS):
                        yg = y[:, g * NB:(g + 1) * NB]
                        step(v.tensor_tensor(out=tmp.rearrange("p (h e) -> p h e", h=HPG),
                                             in0=psum[:, 4 + g, :].rearrange("p (h e) -> p h e", h=HPG),
                                             in1=over(eacs[:, bass.ds(c_ * 64 + (32 * d_ + HPG * g), HPG)], HD, 0), op=ALU.mult))
                        m = v.tensor_tensor(out=yg, in0=yg, in1=tmp, op=ALU.add).then_inc(off_used, 1)
                        v.wait_ge(off_used, c_ * 8 + (4 * d_ + g + 1))
                v.wait_ge(g_used, c_ + 2)
                v.tensor_tensor(out=heads(XS[:, 0, :]), in0=heads(xc), in1=over(per(wend, c_, 0), HD, 0),
                                op=ALU.mult).then_inc(xd_ready, 1)
                step(v.tensor_tensor(out=y, in0=y, in1=psum[:, 0:4, :].rearrange("p b n -> p (b n)"), op=ALU.add))
                v.wait_ge(zs_in, c_ * 16 + 16)
                v.tensor_tensor(out=y, in0=y, in1=zs, op=ALU.mult).then_inc(gated, 1)
                step(v.tensor_tensor(out=heads(F), in0=heads(F), in1=over(per(dec, c_, 0), HD, 0), op=ALU.mult))
                v.wait_ge(st_mm, c_ + 4)
                v.tensor_tensor(out=F, in0=F, in1=psum[:, 4:8, :].rearrange("p b n -> p (b n)"), op=ALU.add).then_inc(st_used, 1)
                v.wait_ge(st_used, c_ + 4)
                v.wait_ge(y_rst, c_ + 1)
                v.wait_ge(gated, c_ + 1)
                v.tensor_scalar(xc, y, rstd[:, 0:1], None, ALU.mult).then_inc(yn_ready, 1)
                step.leave_body()
            step.leave(TT)

        def scan_tensor(pe):
            pe.wait_ge(z_silu, 16)
            with pe.Fori(0, TT) as c_:
                pe.wait_ge(cur_ready, 3 * c_ + 3)
                pe.wait_ge(st_used, c_ + 3)
                for g in range(GROUPS):
                    m = pe.matmul(psum[:, 4, g * P:(g + 1) * P], cur[:, 0, g, :], cur[:, 1, g, :], start=True, stop=True)
                m.then_inc(cb_mm, 1)
                pe.wait_ge(cb_ready, 2 * c_ + 2)
                for d_ in range(2):
                    if d_:
                        pe.wait_ge(off_used, 8 * c_ + 4)
                    for g in range(GROUPS):
                        state = F[:, g * NB:(g + 1) * NB] if d_ == 0 else R[:, bass.ds(c_, 1), g * NB:(g + 1) * NB].rearrange("p o n -> p (o n)")
                        m = pe.matmul(psum[:, 4 + g, :], cur[:, 1, g, :], state, start=True, stop=True)
                    m.then_inc(off_mm, 1)
                pe.wait_ge(xs_ready, 2 * c_ + 2)
                pe.wait_ge(g_ready, 2 * c_ + 2)
                for h in range(HEADS):
                    for d_ in range(2):
                        m = pe.matmul(psum[:, h // HPG, (h % HPG) * HD:(h % HPG + 1) * HD], E[d_][:, h, :],
                                      XS[:, d_, h * HD:(h + 1) * HD], start=(d_ == 0), stop=(d_ == 1))
                m.then_inc(g_used, 1)
                pe.wait_ge(xd_ready, c_ + 4)
                pe.wait_ge(off_used, 8 * c_ + 8)
                for g in range(GROUPS):
                    m = pe.matmul(psum[:, 4 + g, :], cur[:, 2, g, :], XS[:, 0, g * NB:(g + 1) * NB], start=True, stop=True)
                m.then_inc(st_mm, 1)

        w_out = ssd_w_out[0]

        def wout_sync(sp):
            for half in range(2):
                for kk in range(2):
                    s_ = (4 + kk, kk)[half]
                    sp.wait_ge(*((xb_mm, 24), (st_mm, 7))[half])
                    load(sp, s_, w_out[kk * D:(kk + 1) * D, half * NB:(half + 1) * NB].rearrange("(k p) n -> p k n", p=P), KD)
                if half == 0:
                    yield
            sp.wait_ge(g_used, 5)
            load_x(sp, X, x_back)
            sp.wait_ge(st_used, 7)
            for cd in range(2):
                sp.dma_start(GB[:, cd, :], mod_row(0, 2, cd)).then_inc(gate_in, 16)

        def wout_tensor(pe):
            pe.wait_ge(st_used, 7)
            for t in range(TT):
                for half in range(2):
                    n = 2 * t + half
                    if n >= 2:
                        pe.wait_ge(yT_ready, 2 * (n - 1))
                    pe.wait_ge(yn_ready, t + 1)
                    for k in range(KD):
                        b = 2 * (n % 2) + k // 4
                        m = pe.transpose(psum[:, b, (k % 4) * P:(k % 4 + 1) * P],
                                         xtok[:, t, (half * KD + k) * P:(half * KD + k + 1) * P], ident[:, :])
                    m.then_inc(yT_mm, 1)
            for half in range(2):
                for kk in range(2):
                    s_ = (4 + kk, kk)[half]
                    wait_full(pe, s_, (3, 7)[half])
                for t in range(TT):
                    n = half * TT + t
                    pe.wait_ge(yT_ready, 4 * (t + 1))
                    if n >= 2:
                        pe.wait_ge(wo_added, n - 1)
                    for k in range(2 * KD):
                        m = pe.matmul(psum[:, 4 + n % 2, :], yT[:, k, t * P:(t + 1) * P], slot((4 + k // KD, k // KD)[half], KD)[:, k % KD, :],
                                      start=(k == 0), stop=(k == 2 * KD - 1))
                    m.then_inc(wo_mm, 1)

        def wout_vector(v, step):
            v.wait_ge(off_mm, 8)
            for n in range(2 * TT):
                v.wait_ge(yT_mm, n + 1)
                for b in range(2):
                    k0 = (n % 2) * KD + 4 * b
                    v.tensor_tensor(out=yT[:, k0:k0 + 4, (n // 2) * P:(n // 2 + 1) * P],
                                    in0=psum[:, 2 * (n % 2) + b, :].rearrange("p (k t) -> p k t", k=4),
                                    in1=over(cols[:, SN0 + k0:SN0 + k0 + 4], P, 0), op=ALU.mult).then_inc(yT_ready, 1)
            v.wait_ge(gate_in, 32)
            v.wait_ge(x_back, 32)
            for n in range(2 * TT):
                half, t = n // TT, n % TT
                v.wait_ge(wo_mm, n + 1)
                part = slice(half * NB, (half + 1) * NB)
                if n:
                    v.wait_ge(wo_added, n)
                step(v.tensor_tensor(out=tmp, in0=psum[:, 4 + n % 2, :], in1=GB[:, t // 2, part], op=ALU.mult))
                v.tensor_tensor(out=X[:, t, part], in0=X[:, t, part], in1=tmp, op=ALU.add).then_inc(wo_added, 1)

        hg = carve(arena, 8192, 2, D)
        hgT = carve(arena, 10240, 2, KD, P)
        u = carve(arena, 12288, 2, DE)
        uT = carve(arena, 13312, 2, DE // P, P)
        Yb = carve(arena, 14336, 2, D)
        GM = carve(arena, 0, 2, D)
        cg = carve(arena, 2048, 4, D)
        nA, nS = carve(arena, 0, 2, D), carve(arena, 2048, 2, D)
        ngb, nh, njunk = carve(arena, 4096, D), carve(arena, 5120, 2, D), carve(arena, 7168, D)
        KE = DE // P

        def carver(base, at):
            def take(*shape):
                nonlocal at
                v = carve(base, at, *shape)
                at += int(np.prod(shape))
                return v
            return take

        def expand(v, n):
            return v.rearrange("p a (b o) -> p a b o", o=1).broadcast_to([P, v.shape[1], v.shape[2], n])

        MOE_COUNTS = dict(router_in=32, table_zeroed=16, logits_mm=1, logitsT_mm=1, scores_ready=1, pool_const=4, consts=1,
                          rank_mm=1, pos_ready=1, scattered=32 * TT, idx_in=16, h_T_mm=NE, hgT_a=NE, hgT_b=NE, gate_mm=NE, silu=NE,
                          up_mm=NE, u_ready=NE, uT_mm=NE, uT_ready=NE, down_mm=NE, ya=NE + 1, yb=NE + 1, gates_in=32, combined=TT)

        class Moe:

            def __init__(self, tag, layer, tiles, order, fills, before, norm_before, norm_bufs):
                self.layer, self.tiles, self.nt, self.order, self.fills = layer, list(tiles), len(tiles), order, fills
                nt = self.nt
                self.conds = (0, 1) if nt == 4 else (1,)
                if before is None:
                    self.s = dict(**{n: sem(f"moe_{n}") for n in MOE_COUNTS})
                    self.at = dict(**{n: 0 for n in MOE_COUNTS}, rows=0, g_in=0, back_in=0)
                    self.row_stored = [sem(f"moe_rows_stored{j}") for j in range(2)]
                    self.g_in = [sem(f"moe_gathered{j}") for j in range(2)]
                    self.back_in = [sem(f"moe_back_in{j}") for j in range(2)]
                else:
                    self.s, self.row_stored, self.g_in, self.back_in = before.s, before.row_stored, before.g_in, before.back_in
                    self.at = dict(**MOE_COUNTS, rows=16 * (TT // 2 + NE // 2), g_in=16 * (NE // 2), back_in=16 * TT)
                self.o = dict(**{n: sem(f"{tag}_more_{n}") for n in "weights idx turn rows pe act dve stored".split()})
                self.h_d = nc.dram_tensor(f"{tag}_h_d", [P * nt, D], F32).ap()
                self.tok_d = nc.dram_tensor(f"{tag}_tok_d", [NE * P * nt, 1], I32).ap()
                self.y_d = nc.dram_tensor(f"{tag}_y_d", [NE * P * nt, D], F32).ap()
                self.y_rows = self.y_d[0:P * NE, :].rearrange("(p e) d -> e p d", e=NE)
                self.norm = Norm(f"{tag}_norm", X, layer, norm2_g[layer], 3, self.tiles, self.conds, norm_bufs, norm_before)
                self.norm.store, self.norm.stored, self.norm.stored_at, self.norm.h_d = True, self.row_stored, self.at["rows"], self.h_d
                k = carver(arena, 16384)
                self.rw = k(KD, NE)
                self.rb = k(NE)
                self.logT = k(T)
                self.iota = k(NE)
                self.sc, self.bi, self.m, self.pre, self.oh1, self.oh2, self.t16 = (k(nt, NE) for _ in range(7))
                self.pair = k(nt * NG, 6)
                self.gpad = k(nt, 8)
                self.top = k(nt, 8)
                self.topi = k(nt, 8).bitcast(U32)
                self.gi = k(nt, 1)
                self.e1 = k(nt, 2)
                self.gmask = k(nt, NG)
                self.w = k(2, nt)
                self.ws = k(nt)
                self.posf = k(2, nt)
                self.pos = k(2, nt).bitcast(I32)
                self.tok = k(nt).bitcast(I32)
                self.idx = k(NE).bitcast(I32)
                self.zero = k(NE * nt).bitcast(I32)
                self.iint = k(NE).bitcast(I32)
                self.strict = self.logT[:, 0:P]

            def fill(self, j, m):
                s_ = self.order[3 * j + m]
                return s_, self.fills[s_]

            def router_load(self, eng):
                eng.dma_start(self.rw, router_w.rearrange("(k p) e -> p k e", p=P)).then_inc(self.s["router_in"], 16)
                eng.dma_start(self.rb, row(router_b)).then_inc(self.s["router_in"], 16)

            def router_pool_start(self, pool, step):
                nt = self.nt
                pool.iota(self.iint, pattern=[[1, NE]], base=0, channel_multiplier=0).then_inc(self.s["pool_const"], 1)
                pool.iota(self.tok, pattern=[[P, nt]], base=0, channel_multiplier=1).then_inc(self.s["pool_const"], 1)
                pool.memset(self.zero, 0).then_inc(self.s["pool_const"], 1)
                pool.memset(self.gpad, -BIG).then_inc(self.s["pool_const"], 1)
                pool.wait_ge(self.s["pool_const"], self.at["pool_const"] + 4)
                pool.dma_start(self.tok_d.rearrange("(p n) o -> p (n o)", p=P), self.zero).then_inc(self.s["table_zeroed"], 16)
                pool.tensor_copy(self.iota, self.iint).then_inc(self.s["consts"], 1)

            def router_tensor(self, pe):
                s, at, nt, t0 = self.s, self.at, self.nt, self.tiles[0]
                pe.wait_ge(s["router_in"], at["router_in"] + 32)
                pe.wait_ge(self.norm.s["evac"], self.norm.at["evac"] + 2 * nt)
                for k in range(KD):
                    m = pe.matmul(psum[0:NE, 4, 0:nt * P], self.rw[:, k, :], hT[:, k, t0 * P:(t0 + nt) * P],
                                  start=(k == 0), stop=(k == KD - 1))
                m.then_inc(s["logits_mm"], 1)
                pe.wait_ge(s["ya"], at["ya"] + 1)
                for n in range(nt):
                    m = pe.transpose(psum[:, 5, n * NE:(n + 1) * NE], self.logT[0:NE, n * P:(n + 1) * P], ident[0:NE, 0:NE])
                m.then_inc(s["logitsT_mm"], 1)
                pe.wait_ge(s["yb"], at["yb"] + 1)
                flat = "p t e -> p (t e)"
                pe.matmul(psum[:, 6, 0:nt * NE], self.strict, self.m.rearrange(flat), start=True, stop=False)
                pe.matmul(psum[:, 6, 0:nt * NE], ones[:, :], self.pre.rearrange(flat), start=False, stop=True)
                pe.matmul(psum[:, 6, 128:128 + NE], ones[:, :], self.t16[:, 0, :], start=True, stop=True).then_inc(s["rank_mm"], 1)

            def router_scalar(self, act):
                s, at, nt = self.s, self.at, self.nt
                act.wait_ge(s["logits_mm"], at["logits_mm"] + 1)
                act.activation(self.logT[0:NE, 0:nt * P], psum[0:NE, 4, 0:nt * P], ACT.Copy).then_inc(s["ya"], 1)
                act.wait_ge(s["logitsT_mm"], at["logitsT_mm"] + 1)
                act.activation(self.sc.rearrange("p t e -> p (t e)"), psum[:, 5, 0:nt * NE], ACT.Sigmoid).then_inc(s["scores_ready"], 1)

            def router_vector(self, v, step):
                s, at, nt = self.s, self.at, self.nt
                tt = v.tensor_tensor

                def many(x_):
                    return x_.rearrange("p (o e) -> p o e", o=1).broadcast_to([P, nt, x_.shape[1]])

                v.wait_ge(s["consts"], at["consts"] + 1)
                v.wait_ge(s["router_in"], at["router_in"] + 32)
                v.wait_ge(s["scores_ready"], at["scores_ready"] + 1)
                step(tt(out=self.bi, in0=self.sc, in1=many(self.rb), op=ALU.add))
                b = self.bi.rearrange("p t (g e) -> p (t g) e", g=NG)
                step(tt(out=self.pair[:, :, 0:2], in0=b[:, :, 0:4:2], in1=b[:, :, 1:4:2], op=ALU.add))
                step(tt(out=self.pair[:, :, 2:4], in0=b[:, :, 0:2], in1=b[:, :, 2:4], op=ALU.add))
                step(tt(out=self.pair[:, :, 4:5], in0=b[:, :, 0:1], in1=b[:, :, 3:4], op=ALU.add))
                step(tt(out=self.pair[:, :, 5:6], in0=b[:, :, 1:2], in1=b[:, :, 2:3], op=ALU.add))
                step(v.tensor_reduce(out=self.gpad[:, :, 0:NG], in_=self.pair.rearrange("p (t g) s -> p t g s", g=NG), axis=AX.X, op=ALU.max))
                for n in range(nt):
                    step(v.max(self.top[:, n, :], self.gpad[:, n, :]))
                    step(v.max_index(self.topi[:, n, :], self.top[:, n, :], self.gpad[:, n, :]))
                step(v.tensor_copy(self.gi, self.topi[:, :, 0:1]))
                step(tt(out=self.gmask, in0=many(self.iota[:, 0:NG]), in1=self.gi.broadcast_to([P, nt, NG]), op=ALU.is_equal))
                g4 = expand(self.gmask, EPG)
                split = "p t (g e) -> p t g e"
                step(tt(out=self.bi.rearrange(split, g=NG), in0=self.bi.rearrange(split, g=NG), in1=g4, op=ALU.mult))
                step(v.tensor_scalar(self.gmask, self.gmask, -1.0, BIG, ALU.add, ALU.mult))
                step(tt(out=self.bi.rearrange(split, g=NG), in0=self.bi.rearrange(split, g=NG), in1=g4, op=ALU.add))
                for n in range(nt):
                    step(v.max(self.top[:, n, :], self.bi[:, n, :]))
                    step(v.max_index(self.topi[:, n, :], self.top[:, n, :], self.bi[:, n, :]))
                step(v.tensor_copy(self.e1, self.topi[:, :, 0:2]))
                for k, oh in enumerate((self.oh1, self.oh2)):
                    step(tt(out=oh, in0=many(self.iota), in1=self.e1[:, :, k:k + 1].broadcast_to([P, nt, NE]), op=ALU.is_equal))
                step(tt(out=self.m, in0=self.oh1, in1=self.oh2, op=ALU.add))
                step(v.memset(self.pre[:, 0, :], 0.0))
                for n in range(1, nt):
                    step(tt(out=self.pre[:, n, :], in0=self.pre[:, n - 1, :], in1=self.m[:, n - 1, :], op=ALU.add))
                step(tt(out=self.t16[:, 0, :], in0=self.pre[:, nt - 1, :], in1=self.m[:, nt - 1, :], op=ALU.add))
                tt(out=self.strict, in0=tri_up[:, :], in1=ident[:, :], op=ALU.subtract).then_inc(s["yb"], 1)
                for k, oh in enumerate((self.oh1, self.oh2)):
                    if k == 0:
                        v.wait_ge(s["rank_mm"], at["rank_mm"] + 1)
                    step(tt(out=self.t16, in0=oh, in1=self.sc, op=ALU.mult))
                    step(v.tensor_reduce(out=self.w[:, k, :], in_=self.t16, axis=AX.X, op=ALU.add))
                step(tt(out=self.ws, in0=self.w[:, 0, :], in1=self.w[:, 1, :], op=ALU.add))
                step(v.reciprocal(self.ws, self.ws))
                for k in range(2):
                    step(tt(out=self.w[:, k, :], in0=self.w[:, k, :], in1=self.ws, op=ALU.mult))
                step(v.tensor_scalar(self.bi, psum[:, 6, 0:nt * NE].rearrange("p (t e) -> p t e", t=nt), float(NE), None, ALU.mult))
                step(tt(out=self.bi, in0=self.bi, in1=many(self.iota), op=ALU.add))
                for k, oh in enumerate((self.oh1, self.oh2)):
                    step(tt(out=self.t16, in0=oh, in1=self.bi, op=ALU.mult))
                    step(v.tensor_reduce(out=self.posf[:, k, :], in_=self.t16, axis=AX.X, op=ALU.add))
                step(v.tensor_reduce(out=self.gi[:, 0, :], in_=psum[:, 6, 128:128 + NE], axis=AX.X, op=ALU.max))
                step(v.tensor_copy(most[:, :], self.gi[:, 0, :]))
                v.tensor_copy(self.pos, self.posf).then_inc(s["pos_ready"], 1)

            def router_pool(self, pool):
                s, at, nt = self.s, self.at, self.nt
                pool.wait_ge(s["table_zeroed"], at["table_zeroed"] + 16)
                pool.wait_ge(s["pos_ready"], at["pos_ready"] + 1)
                for k in range(2):
                    for n in range(nt):
                        pool.indirect_dma_start(out=self.tok_d, out_offset=bass.IndirectOffsetOnAxis(ap=self.pos[:, k, n:n + 1], axis=0),
                                                in_=self.tok[:, n:n + 1], in_offset=None).then_inc(s["scattered"], 16)
                pool.wait_ge(s["scattered"], at["scattered"] + 32 * nt)
                pool.dma_start(self.idx, self.tok_d[0:P * NE, :].rearrange("(p e) o -> p (e o)", e=NE)).then_inc(s["idx_in"], 16)
                pool.wait_ge(s["idx_in"], at["idx_in"] + 16)
                for j in range(2):
                    pool.wait_ge(self.row_stored[j], self.at["rows"] + 16 * (nt // 2))

            def gathers(self, pool):
                for e in range(NE):
                    if e >= 2:
                        pool.wait_ge(self.s["h_T_mm"], self.at["h_T_mm"] + e - 1)
                    pool.indirect_dma_start(out=hg[:, e % 2, :], out_offset=None, in_=self.h_d,
                                            in_offset=bass.IndirectOffsetOnAxis(ap=self.idx[:, e:e + 1], axis=0)).then_inc(self.g_in[e % 2], 16)

            def weights(self, e, m):
                if m < 2:
                    w_ = (moe_w_gate, moe_w_up)[m][self.layer, bass.ds(e, 1)].rearrange("o (k p) n -> p (o k) n", p=P)
                    return w_, KD
                return moe_w_down[self.layer, bass.ds(e, 1)].rearrange("o (k p) n -> p (o k) n", p=P), KE

            def sync_first(self, sp, waits):
                for j in range(2):
                    for m in range(3):
                        for w_ in waits[3 * j + m]:
                            sp.wait_ge(*w_)
                        src, a = self.weights(j, m)
                        load(sp, self.order[3 * j + m], src, a)

            def sync_rest(self, sp):
                with sp.Fori(1, NE // 2) as i:
                    for j in range(2):
                        for m, (done, at) in enumerate(((self.s["gate_mm"], self.at["gate_mm"]), (self.s["up_mm"], self.at["up_mm"]),
                                                        (self.s["down_mm"], self.at["down_mm"]))):
                            sp.wait_ge(done, 2 * i + (at + j - 1))
                            src, a = self.weights(2 * i + j, m)
                            load(sp, self.order[3 * j + m], src, a)

            def gate_or_up(self, pe, n, i, j, m):
                s_, f = self.fill(j, m)
                pe.wait_ge(full[s_], 16 * i + (16 * f + 16))
                for k in range(KD):
                    mm = pe.matmul(psum[:, 2 + m, :], hgT[:, j, k, :], slot(s_, KD)[:, k, :], start=(k == 0), stop=(k == KD - 1))
                mm.then_inc((self.s["gate_mm"], self.s["up_mm"])[m], 1)

            def u_transpose(self, pe, n, j):
                pe.wait_ge(self.s["u_ready"], self.at["u_ready"] + n + 1)
                for k in range(KE):
                    m = pe.transpose(psum[:, 4, k * P:(k + 1) * P], u[:, j, k * P:(k + 1) * P], ident[:, :])
                m.then_inc(self.s["uT_mm"], 1)

            def down(self, pe, n, i, j):
                s_, f = self.fill(j, 2)
                pe.wait_ge(full[s_], 16 * i + (16 * f + 16))
                pe.wait_ge(self.s["uT_ready"], self.at["uT_ready"] + n + 1)
                pe.wait_ge(self.s["ya"], self.at["ya"] + n + 1)
                pe.wait_ge(self.s["yb"], self.at["yb"] + n + 1)
                for half in range(2):
                    for k in range(KE):
                        m = pe.matmul(psum[:, 5 + half, :], uT[:, j, k, :], slot(s_, KE)[:, k, half * NB:(half + 1) * NB],
                                      start=(k == 0), stop=(k == KE - 1))
                m.then_inc(self.s["down_mm"], 1)

            def tokens_transpose(self, pe, n, i, j, first):
                pe.wait_ge(self.g_in[j], self.at["g_in"] + 16 * i + 16)
                if not first:
                    pe.wait_ge(self.s["hgT_a"], self.at["hgT_a"] + n)
                    pe.wait_ge(self.s["hgT_b"], self.at["hgT_b"] + n)
                for k in range(KD):
                    m = pe.transpose(psum[:, k // 4, (k % 4) * P:(k % 4 + 1) * P], hg[:, j, k * P:(k + 1) * P], ident[:, :])
                m.then_inc(self.s["h_T_mm"], 1)

            def tensor(self, pe):
                s, at = self.s, self.at
                self.tokens_transpose(pe, 0, 0, 0, True)
                pe.wait_ge(s["hgT_a"], at["hgT_a"] + 1)
                pe.wait_ge(s["hgT_b"], at["hgT_b"] + 1)
                self.gate_or_up(pe, 0, 0, 0, 0)
                self.gate_or_up(pe, 0, 0, 0, 1)
                self.tokens_transpose(pe, 1, 0, 1, False)

                def step_(n, i, j, tokens):
                    i1 = i + j
                    pe.wait_ge(s["hgT_a"], at["hgT_a"] + n + 2)
                    pe.wait_ge(s["hgT_b"], at["hgT_b"] + n + 2)
                    pe.wait_ge(s["silu"], at["silu"] + n + 1)
                    self.gate_or_up(pe, n + 1, i1, 1 - j, 0)
                    self.u_transpose(pe, n, j)
                    self.gate_or_up(pe, n + 1, i1, 1 - j, 1)
                    self.down(pe, n, i, j)
                    if tokens:
                        self.tokens_transpose(pe, n + 2, i + 1, j, False)

                with pe.Fori(0, NE // 2 - 1) as i:
                    for j in range(2):
                        step_(2 * i + j, i, j, True)
                last = NE // 2 - 1
                step_(NE - 2, last, 0, False)
                self.u_transpose(pe, NE - 1, 1)
                self.down(pe, NE - 1, last, 1)

            def copy_tokens(self, eng, n, j, half, first):
                s, at = self.s, self.at
                eng.wait_ge(s["h_T_mm"], at["h_T_mm"] + n + 1)
                if not first:
                    eng.wait_ge(s["up_mm"], at["up_mm"] + n - 1)
                return (hgT[:, j, 4 * half:4 * half + 4, :], psum[:, half, :].rearrange("p (k c) -> p k c", k=4))

            def scalar(self, act):
                s, at = self.s, self.at

                def tokens(n, j, first=False):
                    dst, src = self.copy_tokens(act, n, j, 0, first)
                    act.activation(dst, src, ACT.Copy).then_inc(s["hgT_a"], 1)

                def silu(n, j):
                    act.wait_ge(s["gate_mm"], at["gate_mm"] + n + 1)
                    act.activation(u[:, j, :], psum[:, 2, :], ACT.Silu).then_inc(s["silu"], 1)

                def rows_out(n, i, j):
                    act.wait_ge(s["down_mm"], at["down_mm"] + n + 1)
                    act.wait_ge(self.row_stored[j], self.at["rows"] + 16 * i + 16 * (self.nt // 2))
                    act.activation(Yb[:, j, 0:NB], psum[:, 5, :], ACT.Copy).then_inc(s["ya"], 1)
                    act.wait_ge(s["ya"], at["ya"] + n + 2)
                    act.wait_ge(s["yb"], at["yb"] + n + 2)
                    act.dma_start(self.y_rows[bass.ds(n, 1), :, :].rearrange("o p d -> (o p) d"), Yb[:, j, :]).then_inc(self.row_stored[j], 16)

                tokens(0, 0, True)
                silu(0, 0)
                tokens(1, 1, True)
                with act.Fori(0, NE // 2 - 1) as i:
                    for j in range(2):
                        n = 2 * i + j
                        silu(n + 1, 1 - j)
                        rows_out(n, i, j)
                        tokens(n + 2, j)
                last = NE // 2 - 1
                silu(NE - 1, 1)
                rows_out(NE - 2, last, 0)
                rows_out(NE - 1, last, 1)

            def vector(self, v):
                s, at = self.s, self.at

                def tokens(n, j, first=False):
                    dst, src = self.copy_tokens(v, n, j, 1, first)
                    v.tensor_copy(dst, src).then_inc(s["hgT_b"], 1)

                def gated_(n, j):
                    v.wait_ge(s["up_mm"], at["up_mm"] + n + 1)
                    v.wait_ge(s["silu"], at["silu"] + n + 1)
                    v.tensor_tensor(out=u[:, j, :], in0=u[:, j, :], in1=psum[:, 3, :], op=ALU.mult).then_inc(s["u_ready"], 1)

                def body(n, i, j, more):
                    v.wait_ge(s["uT_mm"], at["uT_mm"] + n + 1)
                    v.tensor_copy(uT[:, j, :, :], psum[:, 4, :].rearrange("p (k c) -> p k c", k=KE)).then_inc(s["uT_ready"], 1)
                    if more:
                        gated_(n + 1, 1 - j)
                    v.wait_ge(s["down_mm"], at["down_mm"] + n + 1)
                    v.wait_ge(self.row_stored[j], self.at["rows"] + 16 * i + 16 * (self.nt // 2))
                    v.tensor_copy(Yb[:, j, NB:D], psum[:, 6, :]).then_inc(s["yb"], 1)

                tokens(0, 0, True)
                gated_(0, 0)
                tokens(1, 1, True)
                with v.Fori(0, NE // 2 - 1) as i:
                    for j in range(2):
                        body(2 * i + j, i, j, True)
                        tokens(2 * i + (j + 2), j)
                last = NE // 2 - 1
                body(NE - 2, last, 0, True)
                body(NE - 1, last, 1, False)

            def crowded(self, eng):
                eng.wait_ge(self.s["pos_ready"], self.at["pos_ready"] + 1)
                return eng.value_load(most[0:1, 0:1], min_val=0, max_val=T) > CAP

            def more(self, eng, body):
                with eng.Fori(0, NE) as e:
                    with eng.Fori(1, self.nt) as r:
                        body(e, r, e * (self.nt - 1) + (r - 1))

            def sync_more(self, sp):
                with sp.If(self.crowded(sp)):
                    with sp.Fori(0, NE) as e:
                        sp.wait_ge(self.o["pe"], 4 * (self.nt - 1) * e + 1)
                        for m in range(3):
                            src, a = self.weights(e, m)
                            sp.dma_start(slot(self.order[m], a), src).then_inc(self.o["weights"], 16)
                    sp.wait_ge(self.o["pe"], 4 * (self.nt - 1) * NE + 1)

            def pool_more(self, pool):
                o = self.o

                def body(e, r, n):
                    pool.wait_ge(o["pe"], 4 * n + 1)
                    pool.dma_start(self.idx[:, 0:1], self.tok_d.rearrange("(r p e) o -> r e p o", e=NE, p=P)[bass.ds(r, 1), bass.ds(e, 1)]
                                   .rearrange("a b p o -> (a b p) o"), allow_slow_non_contiguous=True).then_inc(o["idx"], 16)
                    pool.wait_ge(o["idx"], 16 * n + 16)
                    pool.sem_inc(o["turn"], 1)
                    pool.indirect_dma_start(out=hg[:, 0, :], out_offset=None, in_=self.h_d,
                                            in_offset=bass.IndirectOffsetOnAxis(ap=self.idx[:, 0:1], axis=0)).then_inc(o["rows"], 16)

                with pool.If(self.crowded(pool)):
                    self.more(pool, body)
                    pool.wait_ge(o["turn"], (self.nt - 1) * NE)
                    pool.wait_ge(o["stored"], 16 * (self.nt - 1) * NE)
                    self.combine_pool(pool, self.y_d)
                with pool.Else():
                    self.combine_pool(pool, self.y_d[0:NE * P, :])

            def tensor_more(self, pe):
                o = self.o

                def body(e, r, n):
                    pe.wait_ge(o["rows"], 16 * n + 16)
                    for k in range(KD):
                        m = pe.transpose(psum[:, k // 4, (k % 4) * P:(k % 4 + 1) * P], hg[:, 0, k * P:(k + 1) * P], ident[:, :])
                    m.then_inc(o["pe"], 1)
                    pe.wait_ge(o["act"], 6 * n + 2)
                    pe.wait_ge(o["weights"], 48 * e + 48)
                    for m in range(2):
                        for k in range(KD):
                            mm = pe.matmul(psum[:, 2 + m, :], hgT[:, 0, k, :], slot(self.order[m], KD)[:, k, :], start=(k == 0), stop=(k == KD - 1))
                    mm.then_inc(o["pe"], 1)
                    pe.wait_ge(o["dve"], n + 1)
                    for k in range(KE):
                        m = pe.transpose(psum[:, 4, k * P:(k + 1) * P], u[:, 0, k * P:(k + 1) * P], ident[:, :])
                    m.then_inc(o["pe"], 1)
                    pe.wait_ge(o["act"], 6 * n + 4)
                    for half in range(2):
                        for k in range(KE):
                            m = pe.matmul(psum[:, 5 + half, :], uT[:, 0, k, :], slot(self.order[2], KE)[:, k, half * NB:(half + 1) * NB],
                                          start=(k == 0), stop=(k == KE - 1))
                    m.then_inc(o["pe"], 1)

                with pe.If(self.crowded(pe)):
                    pe.wait_ge(self.s["ya"], self.at["ya"] + NE + 1)
                    pe.wait_ge(self.s["yb"], self.at["yb"] + NE + 1)
                    pe.transpose(psum[:, 0, 0:P], ident[:, :], ident[:, :]).then_inc(o["pe"], 1)
                    self.more(pe, body)

            def scalar_more(self, act):
                o = self.o

                def body(e, r, n):
                    act.wait_ge(o["pe"], 4 * n + 2)
                    for half in range(2):
                        act.activation(hgT[:, 0, 4 * half:4 * half + 4, :], psum[:, half, :].rearrange("p (k c) -> p k c", k=4),
                                       ACT.Copy).then_inc(o["act"], 1)
                    act.wait_ge(o["pe"], 4 * n + 3)
                    act.activation(u[:, 0, :], psum[:, 2, :], ACT.Silu).then_inc(o["act"], 1)
                    act.wait_ge(o["pe"], 4 * n + 4)
                    act.activation(uT[:, 0, :, :], psum[:, 4, :].rearrange("p (k c) -> p k c", k=KE), ACT.Copy).then_inc(o["act"], 1)
                    act.wait_ge(o["pe"], 4 * n + 5)
                    for half in range(2):
                        act.activation(Yb[:, 0, half * NB:(half + 1) * NB], psum[:, 5 + half, :], ACT.Copy).then_inc(o["act"], 1)
                    act.wait_ge(o["act"], 6 * n + 6)
                    act.dma_start(self.y_d.rearrange("(r p e) d -> r e p d", e=NE, p=P)[bass.ds(r, 1), bass.ds(e, 1)]
                                  .rearrange("a b p d -> (a b p) d"), Yb[:, 0, :]).then_inc(o["stored"], 16)
                    act.wait_ge(o["stored"], 16 * n + 16)

                with act.If(self.crowded(act)):
                    act.wait_ge(self.row_stored[0], self.at["rows"] + 16 * (self.nt // 2 + NE // 2))
                    self.more(act, body)

            def vector_more(self, v):
                o = self.o

                def body(e, r, n):
                    v.wait_ge(o["pe"], 4 * n + 3)
                    v.wait_ge(o["act"], 6 * n + 3)
                    v.tensor_tensor(out=u[:, 0, :], in0=u[:, 0, :], in1=psum[:, 3, :], op=ALU.mult).then_inc(o["dve"], 1)

                with v.If(self.crowded(v)):
                    self.more(v, body)

            def combine_pool(self, pool, table):
                s, at = self.s, self.at
                for j in range(2):
                    pool.wait_ge(self.row_stored[j], self.at["rows"] + 16 * (self.nt // 2 + NE // 2))
                for n in range(self.nt):
                    if n >= 2:
                        pool.wait_ge(s["combined"], at["combined"] + n - 1)
                    for k in range(2):
                        pool.indirect_dma_start(out=cg[:, 2 * (n % 2) + k, :], out_offset=None, in_=table,
                                                in_offset=bass.IndirectOffsetOnAxis(ap=self.pos[:, k, n:n + 1], axis=0)).then_inc(self.back_in[n % 2], 16)

            def gates_load(self, eng):
                eng.wait_ge(self.norm.s["h_T"], self.norm.at["h_T"] + self.nt)
                eng.wait_ge(self.norm.s["h_ready"], self.norm.at["h_ready"] + self.nt)
                for cd in self.conds:
                    eng.dma_start(GM[:, cd, :], mod_row(self.layer, 5, cd)).then_inc(self.s["gates_in"], 16)

            def combine_vector(self, v, step):
                s, at = self.s, self.at
                v.wait_ge(s["gates_in"], at["gates_in"] + 16 * len(self.conds))
                for n, t in enumerate(self.tiles):
                    v.wait_ge(self.back_in[n % 2], self.at["back_in"] + 32 * (n // 2 + 1))
                    c0, c1 = cg[:, 2 * (n % 2), :], cg[:, 2 * (n % 2) + 1, :]
                    step(v.tensor_scalar(c0, c0, self.w[:, 0, n:n + 1], None, ALU.mult))
                    step(v.scalar_tensor_tensor(out=c0, in0=c1, scalar=self.w[:, 1, n:n + 1], in1=c0, op0=ALU.mult, op1=ALU.add))
                    step(v.tensor_tensor(out=c0, in0=c0, in1=GM[:, 0 if t < 2 else 1, :], op=ALU.mult))
                    v.tensor_tensor(out=X[:, t, :], in0=X[:, t, :], in1=c0, op=ALU.add).then_inc(s["combined"], 1)

        most = sb("most", [P, 1], I32)
        moe0 = Moe("moe0", 0, range(TT), (4, 5, 0, 1, 2, 3), (8, 8, 7, 7, 4, 4), None, norm_a, (nA, nS, ngb, nh, njunk))

        LT = 2
        q_tok = carve(arena, 0, LT, D)
        k_tok = carve(arena, 2048, TT, D)
        v_tok = carve(arena, 6144, TT, D)
        qT = carve(arena, 10240, KD, LT * P)
        kT = carve(arena, 12288, KD, T)
        sq = psum[:, 6:8, :].rearrange("p b n -> p (b n)")
        rot = carve(arena, 17408, D)
        bA, bS = carve(arena, 8192, 2, D), carve(arena, 10240, 2, D)
        bg, bh, bj = carve(arena, 12288, D), carve(arena, 13312, 2, D), carve(arena, 15360, D)
        norm_b = Norm("norm_b", X, 1, norm1_g[1], 0, range(TT), (0, 1), (bA, bS, bg, bh, bj), moe0.norm)
        norm_b.src_ready = [(moe0.s["combined"], n + 1) for n in range(TT)]
        kk = carver(arena, 16384)
        rope = kk(LT, 2, DA_D)
        gains = kk(2, 2, DA_D)
        sub_g = kk(DA_V)
        lqk = kk(2, 2 * DA_D)
        lam2 = kk(2)
        nlam = kk(1)
        rs = kk(2 * DA_H)
        mhalf16 = kk(2 * DA_H)
        pk = carver(hflat, 0)
        pr = [pk(2, T) for _ in range(2)]
        attT = [pk(TT, P) for _ in range(2)]
        o_tok = carve(arena, 0, LT, D)
        osq = carve(arena, 2048, D)
        oT = carve(arena, 3072, KD, LT * P)
        GA = carve(arena, 5120, D)
        wtmp = pk(NB)
        stat = [pk(8) for _ in range(2)]

        A = dict(**{n: sem(f"att_{n}") for n in
                               ("small_in lam_exp lam_exp2 const qkv_mm qkv_copied squared rms normed_q normed_k T_mm T_copied s_mm max_ready "
                                "exp_done mixed p_T p_copied o_mm o_copied o_sq o_rms o_normed oT_mm oT_copied out_mm out_added gate_in").split()})
        QKV = [(n, t) for n in range(6) for t in (range(2, TT) if n < 2 else range(TT))]
        qkv_fill = {4: 12, 5: 12, 0: 16, 1: 16, 2: 15, 3: 15}
        qkv_slot = (4, 5, 0, 1, 2, 3)

        def att_sync(sp):
            s = moe0.s
            for n, (done, count) in enumerate(((s["gate_mm"], 15), (s["up_mm"], 15), (s["down_mm"], 15), (s["gate_mm"], 16), (s["up_mm"], 16), (s["down_mm"], 16))):
                sp.wait_ge(done, count)
                load(sp, qkv_slot[n], blocks(da_w_in[0], n * NB), KD)
            for j in range(2):
                sp.wait_ge(moe0.row_stored[j], 16 * (2 + NE // 2))
            norm_b.load(sp, lambda e: None)
            sp.wait_ge(moe0.s["combined"], TT)
            for dst, src in ((rope.rearrange("p t a d -> p t (a d)"), rope_d.rearrange("(t p) a d -> p t (a d)", p=P)),
                             (gains[:, 0].rearrange("p m d -> p (m d)"), row(da_q_norm[0].rearrange("m d -> (m d)"))),
                             (gains[:, 1].rearrange("p m d -> p (m d)"), row(da_k_norm[0].rearrange("m d -> (m d)"))),
                             (sub_g, row(da_sub_norm[0])),
                             (lqk[:, 0, :], row(da_lam_q[0].rearrange("m d -> (m d)"))),
                             (lqk[:, 1, :], row(da_lam_k[0].rearrange("m d -> (m d)")))):
                sp.dma_start(dst, src).then_inc(A["small_in"], 16)
            for n in range(2):
                sp.wait_ge(A["qkv_mm"], (2, 4)[n])
                load(sp, 4 + n, blocks(da_w_out[0], n * NB), KD)
            sp.wait_ge(A["T_mm"], 12)
            sp.dma_start(GA, mod_row(1, 2, 1)).then_inc(A["gate_in"], 16)

        def att_pool(pool, step):
            pool.wait_ge(A["small_in"], 96)
            pool.memset(mhalf16, -0.5).then_inc(A["const"], 1)
            pool.wait_ge(A["const"], 1)
            for n in range(6):
                pool.wait_ge(A["squared"], n + 1)
                step(pool.tensor_scalar(rs, rs, 1.0 / DA_D, EPS, ALU.mult, ALU.add))
                pool.tensor_tensor(out=rs, in0=rs, in1=mhalf16, op=ALU.pow).then_inc(A["rms"], 1)
            for n in range(LT):
                pool.wait_ge(A["o_sq"], n + 1)
                step(pool.tensor_scalar(rs[:, 0:DA_H], rs[:, 0:DA_H], 1.0 / DA_V, EPS, ALU.mult, ALU.add))
                pool.tensor_tensor(out=rs[:, 0:DA_H], in0=rs[:, 0:DA_H], in1=mhalf16[:, 0:DA_H], op=ALU.pow).then_inc(A["o_rms"], 1)

        def att_tensor(pe):
            pe.wait_ge(norm_b.s["evac"], norm_b.at["evac"] + 2 * TT)
            for m_, (n, t) in enumerate(QKV):
                if t == QKV[0][1] or m_ == 0 or QKV[m_ - 1][0] != n:
                    wait_full(pe, qkv_slot[n], qkv_fill[qkv_slot[n]])
                if m_ >= 4:
                    pe.wait_ge(A["qkv_copied"], m_ - 3)
                for k in range(KD):
                    mm = pe.matmul(psum[:, m_ % 4, :], hT[:, k, t * P:(t + 1) * P], slot(qkv_slot[n], KD)[:, k, :],
                                   start=(k == 0), stop=(k == KD - 1))
                mm.then_inc(A["qkv_mm"], 1)
            for n in range(6):
                pe.wait_ge(*((A["normed_q"], n + 1) if n < 2 else (A["normed_k"], n - 1)))
                src = q_tok[:, n, :] if n < 2 else k_tok[:, n - 2, :]
                for half in range(2):
                    m_ = 2 * n + half
                    if m_ >= 2:
                        pe.wait_ge(A["T_copied"], m_ - 1)
                    for b in range(4):
                        mm = pe.transpose(psum[:, 4 + m_ % 2, b * P:(b + 1) * P], src[:, (4 * half + b) * P:(4 * half + b + 1) * P], ident[:, :])
                    mm.then_inc(A["T_mm"], 1)
            pe.wait_ge(A["T_copied"], 12)
            pe.wait_ge(A["qkv_copied"], len(QKV))

            def scores(n):
                t, h = n // DA_H, n % DA_H
                if n >= 2:
                    pe.wait_ge(A["exp_done"], 2 * (n - 1))
                r = 64 * (h % 2)
                for m in range(2):
                    b = 4 * m + h // 2
                    mm = pe.matmul(psum[:, 2 * (n % 2) + m, :], qT[r:r + 64, b, t * P:(t + 1) * P], kT[r:r + 64, b, :],
                                   start=True, stop=True)
                mm.then_inc(A["s_mm"], 1)

            def values(n):
                t, h = n // DA_H, n % DA_H
                pe.wait_ge(A["mixed"], n + 1)
                if n >= 2:
                    pe.wait_ge(A["p_copied"], n - 1)
                for k in range(TT):
                    mm = pe.transpose(psum[:, 4 + n % 2, k * P:(k + 1) * P], pr[n % 2][:, 0, k * P:(k + 1) * P], ident[:, :])
                mm.then_inc(A["p_T"], 1)

            def product(n):
                t, h = n // DA_H, n % DA_H
                pe.wait_ge(A["p_copied"], n + 1)
                if n % 4 == 0 and n >= 8:
                    pe.wait_ge(A["o_copied"], n // 4 - 1)
                for k in range(TT):
                    mm = pe.matmul(psum[:, 6 + (n // 4) % 2, (h % 4) * P:(h % 4 + 1) * P], attT[n % 2][:, k, :],
                                   v_tok[:, k, h * DA_V:(h + 1) * DA_V], start=(k == 0), stop=(k == TT - 1))
                mm.then_inc(A["o_mm"], 1)

            N = LT * DA_H
            scores(0)
            for n in range(N + 1):
                if n + 1 < N:
                    scores(n + 1)
                if n < N:
                    values(n)
                if n:
                    product(n - 1)
            for t in range(LT):
                pe.wait_ge(A["o_normed"], t + 1)
                for half in range(2):
                    for b in range(4):
                        mm = pe.transpose(psum[:, 2 * (t % 2) + half, b * P:(b + 1) * P],
                                          o_tok[:, t, (4 * half + b) * P:(4 * half + b + 1) * P], ident[:, :])
                    mm.then_inc(A["oT_mm"], 1)
            for n in range(2):
                wait_full(pe, 4 + n, 13)
                for t in range(LT):
                    pe.wait_ge(A["oT_copied"], 2 * t + 2)
                    for k in range(KD):
                        mm = pe.matmul(psum[:, 4 + 2 * n + t, :], oT[:, k, t * P:(t + 1) * P], slot(4 + n, KD)[:, k, :],
                                       start=(k == 0), stop=(k == KD - 1))
                    mm.then_inc(A["out_mm"], 1)

        def att_scalar(act):
            act.wait_ge(A["lam_exp"], 1)
            act.activation(lam2, lam2, ACT.Exp).then_inc(A["lam_exp2"], 1)
            for m_, (n, t) in enumerate(QKV):
                act.wait_ge(A["qkv_mm"], m_ + 1)
                dst = (q_tok[:, t - 2, n * NB:(n + 1) * NB] if n < 2 else k_tok[:, t, (n - 2) * NB:(n - 1) * NB] if n < 4
                       else v_tok[:, t, (n - 4) * NB:(n - 3) * NB])
                act.activation(dst, psum[:, m_ % 4, :], ACT.Copy).then_inc(A["qkv_copied"], 1)
            for n in range(6):
                for half in range(2):
                    act.wait_ge(A["T_mm"], 2 * n + half + 1)
                    dst = (qT if n < 2 else kT)[:, 4 * half:4 * half + 4, (n % 2 if n < 2 else n - 2) * P:(n % 2 + 1 if n < 2 else n - 1) * P]
                    act.activation(dst, psum[:, 4 + half, :].rearrange("p (b t) -> p b t", b=4), ACT.Copy).then_inc(A["T_copied"], 1)
            N = LT * DA_H
            for n in range(N + 1):
                if n < N:
                    act.wait_ge(A["max_ready"], n + 1)
                    if n >= 2:
                        act.wait_ge(A["p_T"], n - 1)
                    for m in range(2):
                        act.activation(pr[n % 2][:, m, :], psum[:, 2 * (n % 2) + m, :], ACT.Exp, bias=stat[n % 2][:, m:m + 1],
                                       scale=DA_D ** -0.5, accum_out=stat[n % 2][:, 2 + m:3 + m]).then_inc(A["exp_done"], 1)
                if n:
                    act.wait_ge(A["p_T"], n)
                    act.activation(attT[(n - 1) % 2], psum[:, 4 + (n - 1) % 2, :].rearrange("p (k t) -> p k t", k=TT), ACT.Copy).then_inc(A["p_copied"], 1)
            for m_ in range(2 * LT):
                act.wait_ge(A["oT_mm"], m_ + 1)
                act.activation(oT[:, 4 * (m_ % 2):4 * (m_ % 2) + 4, (m_ // 2) * P:(m_ // 2 + 1) * P],
                               psum[:, m_, :].rearrange("p (b t) -> p b t", b=4), ACT.Copy).then_inc(A["oT_copied"], 1)

        def att_vector(v, step):
            tt = v.tensor_tensor
            v.wait_ge(A["small_in"], 96)
            step(tt(out=lqk[:, 0, :], in0=lqk[:, 0, :], in1=lqk[:, 1, :], op=ALU.mult))
            v.tensor_reduce(out=lam2, in_=lqk[:, 0, :].rearrange("p (m d) -> p m d", m=2), axis=AX.X, op=ALU.add).then_inc(A["lam_exp"], 1)
            v.wait_ge(A["lam_exp2"], 1)
            step(v.scalar_tensor_tensor(out=nlam, in0=lam2[:, 1:2], scalar=-LAM_INIT, in1=lam2[:, 0:1], op0=ALU.add, op1=ALU.subtract))
            for n in range(6):
                w_ = 0 if n < 2 else 1
                tok = q_tok[:, n, :] if n < 2 else k_tok[:, n - 2, :]
                v.wait_ge(A["qkv_copied"], (n + 3) if n < 2 else (4 + 4 + n - 1))
                mh = tok.rearrange("p (x d) -> p x d", d=DA_D)
                step(tt(out=sq, in0=tok, in1=tok, op=ALU.mult))
                v.tensor_reduce(out=rs, in_=sq.rearrange("p (x d) -> p x d", d=DA_D), axis=AX.X, op=ALU.add).then_inc(A["squared"], 1)
                v.wait_ge(A["rms"], n + 1)
                step(tt(out=mh, in0=mh, in1=rs.rearrange("p (x o) -> p x o", o=1).broadcast_to([P, 2 * DA_H, DA_D]), op=ALU.mult))
                done = A["normed_q"] if n < 2 else A["normed_k"]
                m4 = tok.rearrange("p (m h d) -> p m h d", m=2, h=DA_H)
                ins = tt(out=m4, in0=m4, in1=gains[:, w_].rearrange("p m (o d) -> p m o d", o=1).broadcast_to([P, 2, DA_H, DA_D]), op=ALU.mult)
                t = n if n < 2 else n - 4
                if n in (2, 3):
                    ins.then_inc(done, 1)
                    continue
                step(ins)
                half = "p (x f s) -> p x f s"
                F4 = DA_D // 4
                xa_, ra_ = tok.rearrange(half, f=2, s=F4), rot.rearrange(half, f=2, s=F4)
                r_c, r_s = rope[:, t, 0, :], rope[:, t, 1, :]
                for f in range(2):
                    src = xa_[:, :, 1 - f, :].rearrange("p (x a) s -> p x a s", a=2)
                    dst = ra_[:, :, f, :].rearrange("p (x a) s -> p x a s", a=2)
                    sn = r_s.rearrange("p (o a f s) -> p o a f s", o=1, f=2, s=F4)[:, :, :, f, :].broadcast_to([P, 2 * DA_H, 2, F4])
                    step(tt(out=dst, in0=src, in1=sn, op=ALU.mult))
                step(tt(out=mh, in0=mh, in1=r_c.rearrange("p (o d) -> p o d", o=1).broadcast_to([P, 2 * DA_H, DA_D]), op=ALU.mult))
                tt(out=tok, in0=tok, in1=rot, op=ALU.add).then_inc(done, 1)
            N = LT * DA_H

            def maxes(n):
                v.wait_ge(A["s_mm"], n + 1)
                st = stat[n % 2]
                step(v.tensor_reduce(out=st[:, 0:2], in_=psum[:, 2 * (n % 2):2 * (n % 2) + 2, :], axis=AX.X, op=ALU.max))
                v.tensor_scalar(st[:, 0:2], st[:, 0:2], -(DA_D ** -0.5), None, ALU.mult).then_inc(A["max_ready"], 1)

            v.wait_ge(A["T_copied"], 12)
            maxes(0)
            for n in range(N):
                st = stat[n % 2]
                if n + 1 < N:
                    maxes(n + 1)
                v.wait_ge(A["exp_done"], 2 * n + 2)
                step(v.reciprocal(st[:, 4:6], st[:, 2:4]))
                step(tt(out=st[:, 5:6], in0=st[:, 5:6], in1=nlam, op=ALU.mult))
                step(v.tensor_scalar(pr[n % 2][:, 0, :], pr[n % 2][:, 0, :], st[:, 4:5], None, ALU.mult))
                v.scalar_tensor_tensor(out=pr[n % 2][:, 0, :], in0=pr[n % 2][:, 1, :], scalar=st[:, 5:6], in1=pr[n % 2][:, 0, :],
                                       op0=ALU.mult, op1=ALU.add).then_inc(A["mixed"], 1)
                if n % 4 == 1 and n > 4:
                    o_copy(v, n // 4 - 1)
                if n == 10:
                    o_norm(v, step, 0)
            o_copy(v, 3)
            o_norm(v, step, 1)
            v.wait_ge(A["gate_in"], 16)
            for m_ in range(4):
                n, t = m_ // LT, m_ % LT
                v.wait_ge(A["out_mm"], m_ + 1)
                part = slice(n * NB, (n + 1) * NB)
                step(tt(out=wtmp, in0=psum[:, 4 + 2 * n + t, :], in1=GA[:, part], op=ALU.mult))
                ins = tt(out=X[:, 2 + t, part], in0=X[:, 2 + t, part], in1=wtmp, op=ALU.add).then_inc(A["out_added"], 1)
                v.wait_ge(A["out_added"], m_ + 1)

        def o_copy(v, g):
            v.wait_ge(A["o_mm"], 4 * g + 4)
            v.tensor_copy(o_tok[:, g // 2, (g % 2) * NB:(g % 2 + 1) * NB], psum[:, 6 + g % 2, :]).then_inc(A["o_copied"], 1)

        def o_norm(v, step, t):
            v.wait_ge(A["o_copied"], 2 * t + 2)
            o = o_tok[:, t, :]
            oh = o.rearrange("p (h e) -> p h e", h=DA_H)
            step(v.tensor_tensor(out=osq, in0=o, in1=o, op=ALU.mult))
            v.tensor_reduce(out=rs[:, 0:DA_H], in_=osq.rearrange("p (h e) -> p h e", h=DA_H), axis=AX.X, op=ALU.add).then_inc(A["o_sq"], 1)
            v.wait_ge(A["o_rms"], t + 1)
            step(v.tensor_tensor(out=oh, in0=oh, in1=rs[:, 0:DA_H].rearrange("p (h o) -> p h o", o=1).broadcast_to([P, DA_H, DA_V]), op=ALU.mult))
            v.scalar_tensor_tensor(out=oh, in0=oh, scalar=1.0 - LAM_INIT, op0=ALU.mult, op1=ALU.mult,
                                   in1=sub_g.rearrange("p (o e) -> p o e", o=1).broadcast_to([P, DA_H, DA_V])).then_inc(A["o_normed"], 1)

        moe1 = Moe("moe1", 1, range(2, TT), (0, 1, 2, 3, 4, 5), (17, 17, 16, 16, 14, 14), moe0, norm_b,
                   (carve(arena, 10240, 1, D), carve(arena, 11264, 1, D), carve(arena, 12288, D), carve(arena, 13312, 2, D), carve(arena, 15360, D)))
        moe1.norm.src_ready = [(A["out_added"], 3 + n) for n in range(LT)]
        out_stored = sem("out_stored")

        block = es.enter_context(nc.Block())

        @block.sync
        def _(sp):
            setup_sync(sp)
            ada_sync(sp, 0)
            norm_a.load(sp, lambda e: e.wait_ge(mod_out, 32))
            proj_sync(sp)
            wo = wout_sync(sp)
            next(wo)
            scan_sync(sp)
            for _ in wo:
                pass
            sp.wait_ge(yT_mm, 8)
            moe0.norm.load(sp, lambda e: None)
            moe0.router_load(sp)
            moe0.sync_first(sp, ([(wo_mm, 4)], [(wo_mm, 4)], [(wo_mm, 8)], [], [], []))
            moe0.gates_load(sp)
            moe0.sync_rest(sp)
            moe0.sync_more(sp)
            att_sync(sp)
            sp.wait_ge(A["o_mm"], LT * DA_H)
            moe1.norm.load(sp, lambda e: None)
            moe1.router_load(sp)
            k_used = (A["qkv_mm"], 20)
            moe1.sync_first(sp, ([k_used], [k_used], [k_used], [k_used], [(A["out_mm"], 2)], [(A["out_mm"], 4)]))
            moe1.gates_load(sp)
            moe1.sync_rest(sp)
            moe1.sync_more(sp)
            for n in range(LT):
                sp.wait_ge(moe1.s["combined"], moe1.at["combined"] + n + 1)
                sp.dma_start(out[0, n * P:(n + 1) * P, :], X[:, 2 + n, :]).then_inc(out_stored, 16)
            sp.wait_ge(out_stored, 16 * LT)

        @block.gpsimd
        def _(pool):
            step = Chain(pool, pool_step)
            setup_pool(pool)
            norm_a.pool(pool, step)
            pool.wait_ge(norm_a.s["h_ready"], TT)
            pool.memset(U, 0.0).then_inc(pads_set, 1)
            scan_pool_start(pool)
            scan_pool(pool, step)
            pool.wait_ge(st_mm, 7)
            moe0.router_pool_start(pool, step)
            moe0.norm.pool(pool, step)
            moe0.router_pool(pool)
            moe0.gathers(pool)
            moe0.pool_more(pool)
            norm_b.pool(pool, step)
            att_pool(pool, step)
            moe1.router_pool_start(pool, step)
            moe1.norm.pool(pool, step)
            moe1.router_pool(pool)
            moe1.gathers(pool)
            moe1.pool_more(pool)

        @block.scalar
        def _(act):
            act.dma_start(ada_row[0:1, :], ada_bias(0)).then_inc(adab_in, 16)
            load_x(act, xa, x_in)
            act.dma_start(w_dt, w_in[:, IN_DT:IN_DT + 64].rearrange("(k p) n -> p k n", p=P)).then_inc(w_dt_in, 16)
            act.wait_ge(pool_set, 6)
            act.dma_start(dt_b, ssd_dt_bias[0].rearrange("d (h o) -> (d h) o", o=1)).then_inc(w_dt_in, 16)
            setup_scalar(act)
            ada_scalar(act, 0)
            norm_a.scalar(act, lambda e: e.wait_ge(x_in, 32))
            act.wait_ge(pads_set, 1)
            proj_scalar(act)
            scan_scalar(act)
            moe0.norm.src_ready = [(wo_added, TT + n + 1) for n in range(TT)]
            moe0.norm.scalar(act, lambda e: None)
            moe0.router_scalar(act)
            moe0.scalar(act)
            moe0.scalar_more(act)
            norm_b.scalar(act, lambda e: None)
            att_scalar(act)
            moe1.norm.scalar(act, lambda e: None)
            moe1.router_scalar(act)
            moe1.scalar(act)
            moe1.scalar_more(act)

        @block.vector
        def _(v):
            step = Chain(v, dve_step)
            setup_vector(v, step)
            norm_a.vector(v, step)
            proj_vector(v, step)
            back_vector(v, step)
            scan_vector(v, step)
            wout_vector(v, step)
            moe0.norm.vector(v, step)
            moe0.router_vector(v, step)
            moe0.vector(v)
            moe0.vector_more(v)
            moe0.combine_vector(v, step)
            norm_b.vector(v, step)
            att_vector(v, step)
            moe1.norm.vector(v, step)
            moe1.router_vector(v, step)
            moe1.vector(v)
            moe1.vector_more(v)
            moe1.combine_vector(v, step)

        @block.tensor
        def _(pe):
            setup_tensor(pe)
            pe.wait_ge(pool_set, 1)
            ada_tensor(pe, 0)
            norm_a.tensor(pe)
            proj_tensor(pe)
            back_tensor(pe)
            scan_tensor(pe)
            wout_tensor(pe)
            moe0.norm.tensor(pe)
            moe0.router_tensor(pe)
            moe0.tensor(pe)
            moe0.tensor_more(pe)
            norm_b.tensor(pe)
            att_tensor(pe)
            moe1.norm.tensor(pe)
            moe1.router_tensor(pe)
            moe1.tensor(pe)
            moe1.tensor_more(pe)


_INS = ["x", "c", "ctx", "c_ctx", "ada_w", "ada_b", "norm1_g", "norm2_g",
        "ssd_w_in", "ssd_conv_w", "ssd_conv_b", "ssd_dt_bias", "ssd_a_log", "ssd_d", "ssd_norm_g", "ssd_w_out",
        "da_w_in", "da_q_norm", "da_k_norm", "da_lam_q", "da_lam_k", "da_sub_norm", "da_w_out",
        "router_w", "router_b", "moe_w_gate", "moe_w_up", "moe_w_down"]


def kernel(**inputs):
    import concourse.bacc as bacc
    from concourse.bass_utils import run_bass_kernel_spmd

    nc = bacc.Bacc("TRN2", target_bir_lowering=False, num_devices=1)
    arrays, aps = {}, {}
    for name in _INS:
        a = np.ascontiguousarray(inputs[name])
        arrays[f"in_{name}"] = a
        aps[name] = nc.dram_tensor(f"in_{name}", a.shape, mybir.dt.from_np(a.dtype), kind="ExternalInput").ap()
    aps["out"] = nc.dram_tensor("out_latent", (1, SEG, D), F32, kind="ExternalOutput").ap()
    backbone(nc, **aps)
    r = run_bass_kernel_spmd(nc, [arrays], core_ids=[0])
    return r.results[0]["out_latent"]
```

```python
import math
from contextlib import ExitStack

import numpy as np
import concourse.bass as bass
from concourse import mybir

F32 = mybir.dt.float32
I32 = mybir.dt.int32
U32 = mybir.dt.uint32
ALU = mybir.AluOpType
ACT = mybir.ActivationFunctionType
AX = mybir.AxisListType

P = 128
D = 1024
KD = D // P
TT = 4
T = TT * P
NB = 512
EPS = 1e-6
SLOTS = 6
SLOT = 4096

INNER = 2048
HEADS = 32
HD = 64
GROUPS = 4
HPG = HEADS // GROUPS
STATE = 128
TAPS = 5
CONV = INNER + 2 * GROUPS * STATE
PAD = TAPS // 2
SEG = 2 * P
IN_DT = INNER + CONV

DA_H = 8
DA_D = 64
DA_V = 128
LAM_INIT = 0.8 - 0.6 * math.exp(-0.3 * 1)

NE = 16
NG = 4
EPG = NE // NG
DE = D // 2
CAP = P
BIG = 1.0e30


class Chain:

    def __init__(self, eng, sem):
        self.eng, self.sem, self.at, self.k = eng, sem, 0, 0

    def __call__(self, ins):
        ins.then_inc(self.sem, 1)
        self.k += 1
        self.eng.wait_ge(self.sem, self.at + self.k)
        return ins

    def enter(self, i, per):
        self.start = self.at + self.k
        self.at, self.k, self.per = i * per + self.start, 0, per

    def leave_body(self):
        assert self.k == self.per, self.k

    def leave(self, n):
        self.at, self.k = 0, self.start + n * self.per


def rope_tables():
    t = np.arange(SEG)
    pos = np.stack([t // 64, t % 64], -1).astype(np.float32)
    n_freq = DA_D // 4
    inv = (10000.0 ** (-np.arange(n_freq, dtype=np.float32) / n_freq)).astype(np.float32)
    ang = pos[..., None] * inv
    cos, sin = np.cos(ang).astype(np.float32), np.sin(ang).astype(np.float32)
    c = np.stack([cos, cos], 2).reshape(SEG, DA_D)
    s = np.stack([-sin, sin], 2).reshape(SEG, DA_D)
    return np.stack([c, s], 1)


def backbone(nc, x, c, ctx, c_ctx, ada_w, ada_b, norm1_g, norm2_g,
             ssd_w_in, ssd_conv_w, ssd_conv_b, ssd_dt_bias, ssd_a_log, ssd_d, ssd_norm_g, ssd_w_out,
             da_w_in, da_q_norm, da_k_norm, da_lam_q, da_lam_k, da_sub_norm, da_w_out,
             router_w, router_b, moe_w_gate, moe_w_up, moe_w_down, out):
    es = ExitStack()
    with es:
        def sb(name, shape, dt=F32):
            return es.enter_context(nc.sbuf_tensor(name, shape, dt))

        def sem(name):
            return es.enter_context(nc.semaphore(name))

        ring = sb("ring", [P, SLOTS, SLOT])
        X = sb("X", [P, TT, D])
        hT = sb("hT", [P, KD, T])
        ARENA = 18432
        arena = sb("arena", [P, ARENA])
        ident = sb("ident", [P, P])
        tri_up = sb("tri_up", [P, P])
        tri_lo = sb("tri_lo", [P, P])
        ones = sb("ones", [P, P])
        cols = sb("cols", [P, 176])
        small = sb("small", [P, 32])
        psum = es.enter_context(nc.psum_tensor("psum", [P, 8, NB], F32))
        dts = sb("dts", [P, 5, 4 * 64])
        mhalf = small[:, 0:1]
        ss = small[:, 1:5]
        rstd = small[:, 8:12]

        def carve(base, at, *shape):
            n = int(np.prod(shape))
            v = base[:, at:at + n]
            if len(shape) == 2:
                v = v.rearrange("p (a b) -> p a b", a=shape[0])
            if len(shape) == 3:
                v = v.rearrange("p (a b c) -> p a b c", a=shape[0], b=shape[1])
            return v

        def slot(s, a):
            return ring[:, s, :].rearrange("p (a b) -> p a b", a=a)

        mod_d = nc.dram_tensor("mod_d", [6, 2, 2 * D], F32).ap()
        acs_d = nc.dram_tensor("acs_d", [TT, 2 * HEADS, P], F32).ap()
        zs_d = nc.dram_tensor("zs_d", [TT, P, INNER], F32).ap()
        id_d = nc.inline_tensor(np.eye(P, dtype=np.float32), "id_d").ap()
        up_d = nc.inline_tensor(np.triu(np.ones((P, P), np.float32)), "up_d").ap()
        lo_d = nc.inline_tensor(np.tril(np.ones((P, P), np.float32)), "lo_d").ap()
        rope_d = nc.inline_tensor(rope_tables(), "rope_d").ap()

        full = [sem(f"slot{s}_full") for s in range(SLOTS)]

        def load(eng, s, src, a):
            eng.dma_start(slot(s, a), src).then_inc(full[s], 16)

        def wait_full(pe, s, fill):
            pe.wait_ge(full[s], fill * 16 + 16)

        def row(v):
            return v.rearrange("(o n) -> o n", o=1).broadcast_to([P, v.shape[0]])

        def mod_row(layer, v, cond):
            q = 3 * layer + v // 2
            return row(mod_d[q, cond, (v % 2) * D:(v % 2 + 1) * D])

        def blocks(w, c0, n=NB):
            return w[:, c0:c0 + n].rearrange("(k p) n -> p k n", p=P)

        Xflat = X[:, :, :].rearrange("p t n -> p (t n)")
        hflat = hT[:, :, :].rearrange("p k t -> p (k t)")
        xa = carve(arena, 0, TT, D)
        rows1 = carve(arena, 12288, P)
        rows2 = carve(arena, 12288 + P, P)
        N1, N2 = TAPS * CONV // P, 24 + 16 + 8 + 8
        TAP0, CB0, SN0, CC0 = 0, N1, N1 + 24, N1 + 40
        c_sil = carve(Xflat, 0, KD, 32)
        ada_row = carve(Xflat, 256, 2 * D)
        mod_sb = carve(Xflat, 2304, NB)
        w_dt = carve(Xflat, 2816, KD, 64)
        Abc = carve(arena, 4096, 2, D)
        Sbc = carve(arena, 6144, 2, D)
        gbc = carve(arena, 8192, D)
        hbuf = carve(arena, 9216, 2, D)
        junk = carve(arena, 11264, D)

        consts_in = sem("consts_in")
        rows_in = sem("rows_in")
        x_in = sem("x_in")
        pool_set = sem("pool_set")
        rows_T = sem("rows_transposed")
        cols_ready = sem("cols_ready")
        csil_ready = sem("csil_ready")
        adab_in = sem("adab_in")
        ada_done = sem("ada_psum_done")
        ada_copied = sem("ada_copied")
        mod_out = sem("mod_out")
        dve_step = sem("dve_step")
        pool_step = sem("pool_step")

        def setup_sync(sp):
            for dst, src in ((ident, id_d), (tri_up, up_d), (tri_lo, lo_d)):
                sp.dma_start(dst[:, :], src).then_inc(consts_in, 16)
            sp.dma_start(rows1[0:N1, :], ssd_conv_w[0].rearrange("j (t c) -> (j t) c", c=P)).then_inc(rows_in, 16)
            for r, v in ((0, ssd_conv_b[0]), (24, ssd_norm_g[0]), (40, c[0]), (48, c_ctx)):
                n = v.shape[0] // P
                sp.dma_start(rows2[r:r + n, :], v.rearrange("(t c) -> t c", c=P)).then_inc(rows_in, 16)

        def load_x(eng, dst, signal):
            for half, src in ((0, ctx), (2, x)):
                eng.dma_start(dst[:, half:half + 2, :], src[0].rearrange("(t p) n -> p t n", p=P)).then_inc(signal, 16)

        def setup_pool(pool):
            pool.memset(ones[:, :], 1.0).then_inc(pool_set, 1)
            pool.memset(small[:, :], 0.0).then_inc(pool_set, 1)
            pool.memset(Xflat[:, 0:256], 0.0).then_inc(pool_set, 1)
            pool.wait_ge(pool_set, 3)
            pool.memset(mhalf, -0.5).then_inc(pool_set, 1)
            pool.wait_ge(pool_set, 4)

        def setup_tensor(pe):
            pe.wait_ge(consts_in, 48)
            pe.wait_ge(rows_in, 80)
            pe.transpose(psum[:, 6, 0:N1], rows1[0:N1, :], ident[0:N1, 0:N1])
            pe.transpose(psum[:, 6, N1:N1 + N2], rows2[0:N2, :], ident[0:N2, 0:N2]).then_inc(rows_T, 1)

        def setup_vector(v, step):
            v.wait_ge(rows_T, 1)
            v.tensor_copy(cols[:, 0:N1 + N2], psum[:, 6, 0:N1 + N2]).then_inc(cols_ready, 1)

        def setup_scalar(act):
            act.wait_ge(cols_ready, 1)
            act.wait_ge(pool_set, 4)
            for cond, at in ((0, CC0 + 8), (1, CC0)):
                act.activation(c_sil[:, :, cond], cols[:, at:at + KD], ACT.Silu).then_inc(csil_ready, 1)

        def ada_sync(sp, q):
            if q:
                sp.wait_ge(ada_done, q)
            for j in range(4):
                load(sp, j, blocks(ada_w[q // 3, 2 * P * j:2 * P * (j + 1)], (q % 3) * 2 * D, 2 * D), 2)

        def ada_tensor(pe, q):
            pe.wait_ge(adab_in, 16 * q + 16)
            if q:
                pe.wait_ge(ada_copied, q)
            else:
                pe.wait_ge(csil_ready, 2)
            for j in range(4):
                pe.matmul(psum[32 * j:32 * j + 32, 7, :], ones[0:1, 0:32], ada_row[0:1, j * NB:(j + 1) * NB],
                          start=True, stop=False)
            for k in range(KD):
                if k % 2 == 0:
                    wait_full(pe, k // 2, q)
                for j in range(4):
                    m = pe.matmul(psum[32 * j:32 * j + 32, 7, :], c_sil[:, k, :], slot(k // 2, 2)[:, k % 2, j * NB:(j + 1) * NB],
                                  start=False, stop=(k == KD - 1))
            m.then_inc(ada_done, 1)

        def ada_scalar(act, q):
            act.wait_ge(ada_done, q + 1)
            if q:
                act.wait_ge(mod_out, 32 * q)
            act.activation(mod_sb, psum[:, 7, :], ACT.Copy).then_inc(ada_copied, 1)
            act.wait_ge(ada_copied, q + 1)
            for cond in range(2):
                act.dma_start(mod_d[q, cond, :].rearrange("(j n) -> j n", j=4),
                              mod_sb[cond:cond + 97:32, :]).then_inc(mod_out, 16)
            if q < 5:
                act.dma_start(ada_row[0:1, :], ada_bias(q + 1)).then_inc(adab_in, 16)

        def ada_bias(q):
            return ada_b[q // 3:q // 3 + 1, (q % 3) * 2 * D:(q % 3 + 1) * 2 * D]

        class Norm:

            def __init__(self, tag, src, layer, g, v_shift, tiles, conds, base, before):
                self.src = src
                self.layer, self.g, self.vs, self.tiles, self.conds = layer, g, v_shift, tiles, conds
                if before is None:
                    self.s = dict(**{n: sem(f"norm_{n}") for n in "par_in sumsq rst h_ready h_T evac".split()})
                    self.at = dict(par_in=0, sumsq=0, rst=0, h_ready=0, h_T=0, evac=0)
                else:
                    b, n = before.at, len(before.tiles)
                    self.s = before.s
                    self.at = dict(par_in=b["par_in"] + 16 * (1 + 2 * len(before.conds)), sumsq=b["sumsq"] + n, rst=b["rst"] + n,
                                              h_ready=b["h_ready"] + n, h_T=b["h_T"] + n, evac=b["evac"] + 2 * n)
                self.A, self.S, self.gb, self.h, self.junk = base

            def load(self, eng, wait):
                eng.dma_start(self.gb, row(self.g)).then_inc(self.s["par_in"], 16)
                wait(eng)
                for cd in self.conds:
                    eng.dma_start(self.A[:, cd - self.conds[0], :], mod_row(self.layer, self.vs + 1, cd)).then_inc(self.s["par_in"], 16)
                    eng.dma_start(self.S[:, cd - self.conds[0], :], mod_row(self.layer, self.vs, cd)).then_inc(self.s["par_in"], 16)

            def scalar(self, act, wait):
                wait(act)
                for n in range(len(self.tiles) + 2):
                    if n < len(self.tiles):
                        self.square(act, n)
                    if n >= 2:
                        self.transposed_out(act, n - 2)

            def square(self, act, n):
                t = self.tiles[n]
                if self.src_ready:
                    act.wait_ge(*self.src_ready[n])
                act.activation(self.junk, self.src[:, t, :], ACT.Square, accum_out=ss[:, t:t + 1]).then_inc(self.s["sumsq"], 1)
                act.wait_ge(self.s["sumsq"], self.at["sumsq"] + n + 1)

            def transposed_out(self, act, n):
                t = self.tiles[n]
                if self.store:
                    act.wait_ge(self.s["h_ready"], self.at["h_ready"] + n + 1)
                    act.dma_start(self.h_d[n * P:(n + 1) * P, :], self.h[:, n % 2, :]).then_inc(self.stored[n % 2], 16)
                act.wait_ge(self.s["h_T"], self.at["h_T"] + n + 1)
                for hf in range(2):
                    act.activation(hT[:, 4 * hf:4 * hf + 4, t * P:(t + 1) * P],
                                   psum[:, 2 * (n % 2) + hf, :].rearrange("p (k t) -> p k t", k=4),
                                   ACT.Copy).then_inc(self.s["evac"], 1)

            def pool(self, pool, step):
                for n, t in enumerate(self.tiles):
                    pool.wait_ge(self.s["sumsq"], self.at["sumsq"] + n + 1)
                    step(pool.tensor_scalar(ss[:, t:t + 1], ss[:, t:t + 1], 1.0 / D, EPS, ALU.mult, ALU.add))
                    pool.tensor_tensor(out=rstd[:, t:t + 1], in0=ss[:, t:t + 1], in1=mhalf, op=ALU.pow).then_inc(self.s["rst"], 1)

            def vector(self, v, step):
                self.prepare(v, step)
                for n in range(len(self.tiles)):
                    self.tile(v, step, n)

            def prepare(self, v, step):
                v.wait_ge(self.s["par_in"], self.at["par_in"] + 16 * (1 + 2 * len(self.conds)))
                for cd in self.conds:
                    step(v.scalar_tensor_tensor(out=self.A[:, cd - self.conds[0], :], in0=self.A[:, cd - self.conds[0], :], scalar=1.0,
                                                in1=self.gb, op0=ALU.add, op1=ALU.mult))

            def tile(self, v, step, n):
                t = self.tiles[n]
                cd = 0 if t < 2 else 1
                v.wait_ge(self.s["rst"], self.at["rst"] + n + 1)
                if n >= 2:
                    v.wait_ge(self.s["h_T"], self.at["h_T"] + n - 1)
                    if self.store:
                        v.wait_ge(self.stored[n % 2], self.stored_at + 16 * (n // 2))
                step(v.scalar_tensor_tensor(out=self.h[:, n % 2, :], in0=self.src[:, t, :], scalar=rstd[:, t:t + 1],
                                            in1=self.A[:, cd - self.conds[0], :], op0=ALU.mult, op1=ALU.mult))
                v.tensor_tensor(out=self.h[:, n % 2, :], in0=self.h[:, n % 2, :], in1=self.S[:, cd - self.conds[0], :],
                                op=ALU.add).then_inc(self.s["h_ready"], 1)

            store = False
            src_ready = None

            def tensor(self, pe, part=None):
                for n in part or range(len(self.tiles)):
                    pe.wait_ge(self.s["h_ready"], self.at["h_ready"] + n + 1)
                    if n >= 2:
                        pe.wait_ge(self.s["evac"], self.at["evac"] + 2 * (n - 1))
                    for k in range(KD):
                        m = pe.transpose(psum[:, 2 * (n % 2) + k // 4, (k % 4) * P:(k % 4 + 1) * P],
                                         self.h[:, n % 2, k * P:(k + 1) * P], ident[:, :])
                    m.then_inc(self.s["h_T"], 1)

        norm_a = Norm("norm_a", xa, 0, norm1_g[0], 0, range(TT), (0, 1), (Abc, Sbc, gbc, hbuf, junk), None)

        xtok = carve(arena, 0, TT, INNER)
        BC = carve(arena, 8192, 8, T)
        Bt = carve(arena, 12288, TT, GROUPS * STATE)
        U = carve(arena, 14336, 2, 2, SEG + 2 * PAD)
        conv = carve(arena, 14336 + 1040, 2, T)
        xs = carve(arena, 14336 + 1040 + 1024, 2, T)
        v_dt = carve(arena, 12288, T)
        e_dt = carve(arena, 12800, T)
        dtT = carve(arena, 17424, T)
        dt_b = small[0:64, 12:13]
        expA = cols[:, 0:64]
        d_skip = cols[:, 64:96]
        dt, acs, eacs, wend, dec = (dts[:, n, :] for n in range(5))

        w_dt_in = sem("w_dt_in")
        pads_set = sem("pads_set")
        dt_mm = sem("dt_mm")
        dt_neg = sem("dt_neg")
        dt_ln = sem("dt_ln")
        dt_T = sem("dt_T")
        heads_in = sem("heads_in")
        expa_ready = sem("expa_ready")
        a_ready = sem("a_ready")
        acs_copied = sem("acs_copied")
        acs_exp = sem("acs_exp")
        acs_stored = sem("acs_stored")
        acsT_ready = sem("acsT_ready")
        dt_all = sem("dt_all")
        xb_mm = sem("conv_in_psum")
        xb_copied = sem("conv_in_copied")
        xb_conv = sem("conv_done")
        xb_silu = sem("conv_silu")
        xb_T = sem("conv_transposed")
        xb_out = sem("conv_tok_ready")
        z_mm = sem("z_mm")
        z_silu = sem("z_silu")
        z_stored = [sem(f"z_stored{n}") for n in range(2)]

        w_in = ssd_w_in[0]

        def dt_tensor(pe):
            pe.wait_ge(w_dt_in, 32)
            pe.wait_ge(norm_a.s["evac"], 2 * TT)
            for k in range(KD):
                m = pe.matmul(psum[0:64, 4, :], w_dt[:, k, :], hT[:, k, :], start=(k == 0), stop=(k == KD - 1))
            m.then_inc(dt_mm, 1)

        def dt_vector(v, step):
            v.wait_ge(dt_mm, 1)
            step(v.tensor_scalar(v_dt[0:64, :], psum[0:64, 4, :], dt_b, None, ALU.add))
            v.scalar_tensor_tensor(out=e_dt[0:64, :], in0=v_dt[0:64, :], scalar=-1.0, in1=v_dt[0:64, :],
                                   op0=ALU.mult, op1=ALU.min).then_inc(dt_neg, 1)
            v.wait_ge(dt_ln, 2)
            v.scalar_tensor_tensor(out=dtT[0:64, :], in0=v_dt[0:64, :], scalar=0.0, in1=e_dt[0:64, :],
                                   op0=ALU.max, op1=ALU.add).then_inc(dt_T, 1)

        def dt_scalar(act):
            act.wait_ge(dt_neg, 1)
            act.activation(e_dt[0:64, :], e_dt[0:64, :], ACT.Exp).then_inc(dt_ln, 1)
            act.wait_ge(dt_ln, 1)
            act.activation(e_dt[0:64, :], e_dt[0:64, :], ACT.Ln, bias=1.0).then_inc(dt_ln, 1)

        def xb_project(pe, n, slot_, ct, j):
            if n >= 2:
                pe.wait_ge(xb_copied, n - 1)
            for k in range(KD):
                m = pe.matmul(psum[:, j, :], slot(slot_, KD)[:, k, ct * P:(ct + 1) * P], hT[:, k, :],
                              start=(k == 0), stop=(k == KD - 1))
            m.then_inc(xb_mm, 1)

        def xb_transpose(pe, n, j, src):
            pe.wait_ge(xb_silu, n + 1)
            if n >= 2:
                pe.wait_ge(xb_out, n - 1)
            for t in range(TT):
                m = pe.transpose(psum[:, 2 + j, t * P:(t + 1) * P], src[:, t * P:(t + 1) * P], ident[:, :])
            m.then_inc(xb_T, 1)

        def xb_scalar(act, n, j, post):
            act.wait_ge(xb_conv, n + 1)
            dst = xs[:, j, :] if post == "x" else BC[:, n - 16, :]
            act.activation(dst, conv[:, j, :], ACT.Silu).then_inc(xb_silu, 1)
            if n < 23:
                xb_copy(act, n + 1, 1 - j)
            if post == "C":
                return
            act.wait_ge(xb_T, n + 1)
            src = psum[:, 2 + j, :].rearrange("p (t c) -> p t c", t=TT)
            dst = xtok[:, :, bass.ds(n * P, P)] if post == "x" else Bt[:, :, (n - 16) * P:(n - 15) * P]
            act.activation(dst, src, ACT.Copy).then_inc(xb_out, 1)

        def xb_copy(act, n, j):
            act.wait_ge(xb_mm, n + 1)
            act.activation(U[:, j, :, PAD:PAD + SEG], psum[:, j, :].rearrange("p (s t) -> p s t", s=2),
                           ACT.Copy).then_inc(xb_copied, 1)

        def xb_vector(v, n, j, step):
            v.wait_ge(xb_copied, n + 1)
            if n >= 2:
                v.wait_ge(xb_silu, n - 1)
            o = conv[:, j, :].rearrange("p (s t) -> p s t", s=2)
            step(v.tensor_scalar(o, U[:, j, :, 0:SEG], cols[:, bass.ds(TAP0 + n, 1)], cols[:, bass.ds(CB0 + n, 1)],
                                 ALU.mult, ALU.add))
            for tap in range(1, TAPS):
                m = v.scalar_tensor_tensor(out=o, in0=U[:, j, :, tap:tap + SEG], scalar=cols[:, bass.ds(TAP0 + 24 * tap + n, 1)],
                                           in1=o, op0=ALU.mult, op1=ALU.add)
                if tap < TAPS - 1:
                    step(m)
                else:
                    m.then_inc(xb_conv, 1)

        def xb_load(sp, i, odd, wait):
            if wait is not None:
                sp.wait_ge(xb_mm, wait)
            load(sp, 4 + odd, w_in[:, bass.ds(i * NB + INNER, NB)].rearrange("(k p) n -> p k n", p=P), KD)

        def proj_sync(sp):
            xb_load(sp, 0, 0, None)
            xb_load(sp, 1, 1, None)
            for i in range(2, 6):
                ada_sync(sp, i - 1)
                xb_load(sp, i, i % 2, 4 * (i - 1))
            ada_sync(sp, 5)
            sp.wait_ge(ada_done, 6)
            for n in range(4):
                load(sp, n, blocks(w_in, n * NB), KD)
            for n in range(4):
                for t in range(TT):
                    m = n * TT + t
                    sp.wait_ge(z_silu, m + 1)
                    sp.dma_start(zs_d[t, :, n * NB:(n + 1) * NB], xs[:, m % 2, :]).then_inc(z_stored[m % 2], 16)
                if n == 0:
                    sp.wait_ge(acsT_ready, 1)
                    sp.dma_start(acs_d.rearrange("c r l -> r c l"), dtT[0:64, :].rearrange("r (c l) -> r c l", c=TT)).then_inc(acs_stored, 16)

        def proj_tensor(pe):
            dt_tensor(pe)
            wait_full(pe, 4, 0)
            xb_project(pe, 0, 4, 0, 0)
            wait_full(pe, 5, 0)
            for i in range(6):
                for ct in range(4):
                    n = 4 * i + ct
                    if n < 23:
                        if ct == 3:
                            wait_full(pe, 4 + (i + 1) % 2, (i + 1) // 2)
                        xb_project(pe, n + 1, 4 + ((n + 1) // 4) % 2, (n + 1) % 4, (n + 1) % 2)
                    if n < 20:
                        xb_transpose(pe, n, n % 2, xs[:, n % 2, :] if n < 16 else BC[:, n - 16, :])
                if i < 5:
                    ada_tensor(pe, i + 1)
            pe.wait_ge(dt_T, 1)
            for t in range(TT):
                m = pe.transpose(psum[:, 5, t * 64:(t + 1) * 64], dtT[0:64, t * P:(t + 1) * P], ident[0:64, 0:64])
            m.then_inc(dt_mm, 1)
            for n in range(4):
                for t in range(TT):
                    m_ = n * TT + t
                    if t == 0:
                        wait_full(pe, n, 6)
                    if m_ >= 2:
                        pe.wait_ge(z_silu, m_ - 1)
                    else:
                        pe.wait_ge(xb_copied, 24)
                    for k in range(KD):
                        m = pe.matmul(psum[:, m_ % 2, :], hT[:, k, t * P:(t + 1) * P], slot(n, KD)[:, k, :],
                                      start=(k == 0), stop=(k == KD - 1))
                    m.then_inc(z_mm, 1)
                if n == 0:
                    acs_tensor(pe)

        def acs_tensor(pe):
            pe.wait_ge(a_ready, 1)
            a4 = dec.rearrange("p (c r) -> p c r", c=TT)
            pe.matmul(psum[:, 4, 0:128].rearrange("p (c r) -> p c r", c=TT), tri_up[:, :], a4[:, :, 0:HEADS], start=True, stop=True)
            pe.matmul(psum[:, 4, 128:256].rearrange("p (c r) -> p c r", c=TT), tri_lo[:, :], a4[:, :, HEADS:64], start=True, stop=True)
            pe.matmul(psum[:, 4, 256:512], ones[:, :], dec, start=True, stop=True)
            for c_ in range(TT):
                for d_, tri in ((0, tri_up), (1, tri_lo)):
                    m = pe.matmul(psum[32 * d_:32 * d_ + 32, 5, c_ * P:(c_ + 1) * P], a4[:, c_, 32 * d_:32 * d_ + 32], tri[:, :],
                                  start=True, stop=True)
            m.then_inc(dt_mm, 1)

        def proj_scalar(act):
            dt_scalar(act)
            xb_copy(act, 0, 0)
            for i in range(6):
                for ct in range(4):
                    n = 4 * i + ct
                    xb_scalar(act, n, n % 2, "x" if n < 16 else "B" if n < 20 else "C")
                if i < 5:
                    ada_scalar(act, i + 1)
            act.wait_ge(xb_conv, 24)
            act.dma_start(expA, row(ssd_a_log[0].rearrange("d h -> (d h)"))).then_inc(heads_in, 16)
            act.dma_start(d_skip, row(ssd_d[0])).then_inc(heads_in, 16)
            act.wait_ge(heads_in, 32)
            act.activation(expA, expA, ACT.Exp).then_inc(expa_ready, 1)
            for n in range(4):
                for t in range(TT):
                    m = n * TT + t
                    act.wait_ge(z_mm, m + 1)
                    if m >= 2:
                        act.wait_ge(z_stored[m % 2], 16 * (m // 2))
                    else:
                        act.wait_ge(xb_T, 20)
                    act.activation(xs[:, m % 2, :], psum[:, m % 2, :], ACT.Silu).then_inc(z_silu, 1)
            act.wait_ge(acs_copied, 1)
            for n, (dst, src) in enumerate(((eacs, acs), (wend, wend), (dec, dec))):
                act.activation(dst, src, ACT.Exp).then_inc(acs_exp, 1)

        def proj_vector(v, step):
            dt_vector(v, step)
            for n in range(24):
                xb_vector(v, n, n % 2, step)
            v.wait_ge(dt_mm, 2)
            v.wait_ge(expa_ready, 1)
            step(v.tensor_copy(dt, psum[:, 5, 0:256]))
            v.scalar_tensor_tensor(out=dec.rearrange("p (c r) -> p c r", c=TT), in0=dt.rearrange("p (c r) -> p c r", c=TT),
                                   scalar=-1.0, in1=expA.rearrange("p (o r) -> p o r", o=1).broadcast_to([P, TT, 64]),
                                   op0=ALU.mult, op1=ALU.mult).then_inc(a_ready, 1)
            v.wait_ge(dt_mm, 3)
            a4 = acs.rearrange("p (c r) -> p c r", c=TT)
            v.tensor_copy(dtT[0:64, :], psum[0:64, 5, :]).then_inc(acsT_ready, 1)
            step(v.tensor_copy(a4[:, :, 0:HEADS], psum[:, 4, 0:128].rearrange("p (c r) -> p c r", c=TT)))
            step(v.tensor_copy(a4[:, :, HEADS:64], psum[:, 4, 128:256].rearrange("p (c r) -> p c r", c=TT)))
            step(v.tensor_copy(dec, psum[:, 4, 256:512]))
            v.tensor_tensor(out=wend, in0=dec, in1=acs, op=ALU.subtract).then_inc(acs_copied, 1)
            v.wait_ge(acs_exp, 3)
            v.tensor_tensor(out=wend, in0=wend, in1=dt, op=ALU.mult).then_inc(dt_all, 1)

        ringflat = ring[:, :, :].rearrange("p s n -> p (s n)")
        R = carve(ringflat, 2 * SLOT, TT, INNER)
        E = [carve(ringflat, 0, HEADS, P), carve(Xflat, 0, HEADS, P)]
        XS = carve(ringflat, SLOT, 2, INNER)
        y = carve(hflat, 0, INNER)
        zs = carve(hflat, INNER, INNER)
        F = carve(arena, 14336, INNER)
        cbm = carve(arena, 16384, 2, GROUPS * P)
        tmp2 = carve(arena, 17408, 2 * NB)
        tmp = carve(arena, 17920, NB)
        GB = carve(arena, 14336, 2, D)
        yT = carve(ringflat, 2 * SLOT, KD * 2, T)
        HALF = HEADS // 2

        xd_ready = sem("xd_ready")
        xe_ready = sem("xe_ready")
        y_begun = sem("y_begun")
        st_mm = sem("state_mm")
        st_used = sem("state_used")
        g_used = sem("g_used")
        e_in = [[sem(f"decay_in{h_}{d}") for d in range(2)] for h_ in range(2)]
        diff = sem("decay_diff")
        e_exp = [sem(f"decay_exp{d}") for d in range(2)]
        xs_ready = [sem(f"xs_ready{d}") for d in range(2)]
        cb_mm = sem("cb_mm")
        cb_ready = sem("cb_masked")
        g_ready = sem("g_ready")
        off_mm = sem("off_mm")
        off_used = sem("off_used")
        diag_used = sem("diag_used")
        zs_in = sem("zs_in")
        gated = sem("gated")
        y_sq = sem("y_sumsq")
        y_rst = sem("y_rstd")
        yn_ready = sem("yn_ready")
        yT_mm = sem("y_transposed")
        yT_ready = sem("yT_ready")
        x_back = sem("x_back")
        gate_in = sem("gate_in")
        wo_mm = sem("wo_mm")
        wo_added = sem("wo_added")
        BACK = ((1, None, 0), (0, 0, 3), (3, 3, 2))
        OFFS = ((0, 1), (1, 0), (2, 0), (2, 1), (3, 0), (3, 1))
        NBACK = len(BACK)

        def offs_done(c_, d_):
            return sum(1 for x_ in OFFS if x_ <= (c_, d_))

        def over(v, n):
            return v.rearrange("p (h o) -> p h o", o=1).broadcast_to([P, v.shape[1], n])

        def heads(v):
            return v.rearrange("p (h e) -> p h e", e=HD)

        def per(v, c_, d_):
            return v[:, c_ * 64 + 32 * d_:c_ * 64 + 32 * d_ + HEADS]

        def banks(a):
            return psum[:, a:a + 4, :].rearrange("p b n -> p (b n)")

        def back_banks(r):
            return 0 if r == 1 else 4

        def mask_cb(v, c_):
            v.wait_ge(cb_mm, c_ + 1)
            for d_, tri in ((0, tri_up), (1, tri_lo)):
                v.tensor_tensor(out=cbm[:, d_, :].rearrange("p (g l) -> p g l", g=GROUPS),
                                in0=psum[:, 4 if c_ else 3, :].rearrange("p (g l) -> p g l", g=GROUPS),
                                in1=tri[:, :].rearrange("p (o l) -> p o l", o=1).broadcast_to([P, GROUPS, P]),
                                op=ALU.mult).then_inc(cb_ready, 1)

        def back_vector(v, step):
            v.wait_ge(dt_all, 1)
            v.wait_ge(z_mm, 16)
            for r, (c_, src, dst) in enumerate(BACK):
                if r == 2:
                    v.wait_ge(st_mm, 1)
                v.tensor_tensor(out=heads(XS[:, r % 2, :]), in0=heads(xtok[:, c_, :]), in1=over(per(wend, c_, 1), HD),
                                op=ALU.mult).then_inc(xd_ready, 1)
                if r == 0:
                    for n in range(2):
                        v.wait_ge(z_stored[n], 128)
                    mask_cb(v, 0)
            for r, (c_, src, dst) in enumerate(BACK):
                states = banks(back_banks(r))
                if src is None:
                    v.wait_ge(st_mm, r + 1)
                    v.tensor_copy(R[:, dst, :], states).then_inc(st_used, 1)
                else:
                    step(v.tensor_tensor(out=heads(R[:, dst, :]), in0=heads(R[:, src, :]), in1=over(per(dec, c_, 1), HD),
                                         op=ALU.mult))
                    v.wait_ge(st_mm, r + 1)
                    v.tensor_tensor(out=R[:, dst, :], in0=R[:, dst, :], in1=states, op=ALU.add).then_inc(st_used, 1)
                v.wait_ge(st_used, r + 1)
                if r == 0:
                    xs_vector(v, 0)

        def back_tensor(pe):
            pe.wait_ge(xb_out, 20)
            pe.wait_ge(xb_silu, 24)
            cb_tensor(pe, 0)
            pe.wait_ge(z_silu, 16)
            for r, (c_, src, dst) in enumerate(BACK):
                pe.wait_ge(xd_ready, r + 1)
                if r == 1:
                    pe.wait_ge(cb_ready, 2)
                if r == 2:
                    pe.wait_ge(st_used, 1)
                for g in range(GROUPS):
                    m = pe.matmul(psum[:, back_banks(r) + g, :], Bt[:, c_, g * STATE:(g + 1) * STATE], XS[:, r % 2, g * NB:(g + 1) * NB],
                                  start=True, stop=True)
                m.then_inc(st_mm, 1)

        def scan_sync(sp):
            sp.wait_ge(acs_stored, 16)
            sp.wait_ge(mod_out, 192)
            sp.wait_ge(dt_mm, 1)
            sp.wait_ge(z_mm, TT)
            for c_ in range(TT):
                for hh in range(2):
                    if c_:
                        sp.wait_ge(g_used, 2 * c_ + hh - 1)
                    for d_ in range(2):
                        r0 = 32 * d_ + HALF * hh
                        src = acs_d[c_:c_ + 1, r0:r0 + HALF, :].rearrange("o h l -> o (h l)").broadcast_to([P, HALF * P])
                        sp.dma_start(E[d_][:, HALF * hh:HALF * hh + HALF, :].rearrange("p h l -> p (h l)"), src).then_inc(e_in[hh][d_], 16)
                if c_:
                    sp.wait_ge(y_sq, c_)
                else:
                    sp.wait_ge(z_mm, 16)
                    for n in range(2):
                        sp.wait_ge(z_stored[n], 128)
                sp.dma_start(zs, zs_d[c_, :, :]).then_inc(zs_in, 16)

        def scan_pool(pool, step):
            def gate(c_):
                pool.wait_ge(zs_in, 16 * c_ + 16)
                pool.wait_ge(diag_used, c_ + 1)
                if c_ < TT - 1:
                    pool.wait_ge(xe_ready, 2 * c_ + 1)
                else:
                    pool.wait_ge(y_begun, TT)
                pool.tensor_tensor(out=xtok[:, c_, :], in0=y, in1=zs, op=ALU.mult).then_inc(gated, 1)

            def begin_y(c_):
                if c_:
                    pool.wait_ge(gated, c_)
                else:
                    pool.wait_ge(z_mm, 16)
                pool.tensor_tensor(out=heads(y), in0=heads(xtok[:, c_, :]), in1=over(d_skip, HD), op=ALU.mult).then_inc(y_begun, 1)

            for c_ in range(TT):
                for hh in range(2):
                    half = slice(HALF * hh, HALF * hh + HALF)
                    pool.wait_ge(e_in[hh][1], 16 * c_ + 16)
                    if c_ == 0 and hh == 0:
                        pool.wait_ge(dt_all, 1)
                    pool.tensor_tensor(out=E[1][:, half, :], in0=E[1][:, half, :], in1=over(per(acs, c_, 1)[:, half], P),
                                       op=ALU.subtract).then_inc(diff, 1)
                    if hh == 0:
                        if c_:
                            pool.wait_ge(g_used, 2 * c_)
                        else:
                            pool.wait_ge(st_mm, 2)
                        pool.tensor_tensor(out=heads(XS[:, 1, :]), in0=heads(xtok[:, c_, :]), in1=over(per(dt, c_, 1), HD),
                                           op=ALU.mult).then_inc(xs_ready[1], 1)
                        if c_:
                            gate(c_ - 1)
                        begin_y(c_)
                if 0 < c_ < TT - 1:
                    pool.wait_ge(off_mm, offs_done(c_, 0))
                    pool.tensor_tensor(out=heads(F), in0=heads(F), in1=over(per(dec, c_, 0), HD), op=ALU.mult).then_inc(xe_ready, 1)
                if c_ < TT - 1:
                    pool.wait_ge(off_mm, offs_done(c_, 1))
                    pool.tensor_tensor(out=heads(R[:, c_, :]), in0=heads(xtok[:, c_, :]), in1=over(per(wend, c_, 0), HD),
                                       op=ALU.mult).then_inc(xe_ready, 1)
                if c_:
                    y_rstd(pool, step, c_ - 1)
            gate(TT - 1)
            y_rstd(pool, step, TT - 1)

        def y_rstd(pool, step, c_):
            pool.wait_ge(y_sq, c_ + 1)
            step(pool.tensor_scalar(ss[:, c_:c_ + 1], ss[:, c_:c_ + 1], 1.0 / INNER, EPS, ALU.mult, ALU.add))
            pool.tensor_tensor(out=rstd[:, c_:c_ + 1], in0=ss[:, c_:c_ + 1], in1=mhalf, op=ALU.pow).then_inc(y_rst, 1)

        def scan_scalar(act):
            def y_square(c_):
                act.wait_ge(gated, c_ + 1)
                act.activation(zs, xtok[:, c_, :], ACT.Square, accum_out=ss[:, c_:c_ + 1]).then_inc(y_sq, 1)

            for c_ in range(TT):
                for hh in range(2):
                    n = 4 * c_ + 2 * hh
                    half = slice(HALF * hh, HALF * hh + HALF)
                    act.wait_ge(e_in[hh][0], 16 * c_ + 16)
                    for h in range(HALF * hh, HALF * hh + HALF):
                        m = act.activation(E[0][:, h, :], E[0][:, h, :], ACT.Relu, scale=-1.0, bias=per(acs, c_, 0)[:, h:h + 1])
                    m.then_inc(e_exp[0], 1)
                    for d_ in range(2):
                        if d_:
                            act.wait_ge(diff, 2 * c_ + hh + 1)
                            act.activation(E[1][:, half, :], E[1][:, half, :], ACT.Relu, scale=-1.0).then_inc(e_exp[1], 1)
                        act.wait_ge(e_exp[d_], n + 1)
                        act.activation(E[d_][:, half, :], E[d_][:, half, :], ACT.Exp, scale=-1.0).then_inc(e_exp[d_], 1)
                if c_:
                    y_square(c_ - 1)
            y_square(TT - 1)

        def xs_vector(v, c_):
            if c_:
                v.wait_ge(g_used, 2 * c_)
            else:
                v.wait_ge(st_mm, NBACK)
            v.tensor_tensor(out=heads(XS[:, 0, :]), in0=heads(xtok[:, c_, :]), in1=over(per(dt, c_, 0), HD),
                            op=ALU.mult).then_inc(xs_ready[0], 1)

        def times_cb(v, c_, hh):
            v.wait_ge(cb_ready, 2 * c_ + 2)
            for d_ in range(2):
                v.wait_ge(e_exp[d_], 4 * c_ + 2 * hh + 2)
                e4 = E[d_][:, HALF * hh:HALF * hh + HALF, :].rearrange("p (g h) l -> p g h l", g=GROUPS // 2)
                cb = cbm[:, d_, hh * 2 * P:(hh + 1) * 2 * P].rearrange("p (g o l) -> p g o l", g=GROUPS // 2, o=1)
                v.tensor_tensor(out=e4, in0=e4, op=ALU.mult,
                                in1=cb.broadcast_to([P, GROUPS // 2, HPG, P])).then_inc(g_ready, 1)

        def off_vector(v, step, c_, d_):
            n = offs_done(c_, d_)
            v.wait_ge(off_mm, n)
            for b in range(2):
                step(v.tensor_tensor(out=heads(tmp2), in0=heads(psum[:, 4 + 2 * b:6 + 2 * b, :].rearrange("p b n -> p (b n)")),
                                     in1=over(per(eacs, c_, d_)[:, HALF * b:HALF * b + HALF], HD), op=ALU.mult))
                yb = y[:, b * D:(b + 1) * D]
                v.tensor_tensor(out=yb, in0=yb, in1=tmp2, op=ALU.add).then_inc(off_used, 1)
                v.wait_ge(off_used, 2 * n - 1 + b)

        def scan_vector(v, step):
            times_cb(v, 0, 0)
            for c_ in range(TT):
                v.wait_ge(y_begun, c_ + 1)
                if (c_, 0) in OFFS:
                    off_vector(v, step, c_, 0)
                times_cb(v, c_, 1)
                if (c_, 1) in OFFS:
                    off_vector(v, step, c_, 1)
                if c_ < TT - 1:
                    mask_cb(v, c_ + 1)
                if c_:
                    y_norm(v, c_ - 1)
                v.wait_ge(g_used, 2 * c_ + 2)
                v.tensor_tensor(out=y, in0=y, in1=banks(0), op=ALU.add).then_inc(diag_used, 1)
                if c_ < TT - 1:
                    xs_vector(v, c_ + 1)
                    v.wait_ge(st_mm, NBACK + c_ + 1)
                    if c_:
                        v.wait_ge(xe_ready, 2 * c_)
                        v.tensor_tensor(out=F, in0=F, in1=banks(4), op=ALU.add).then_inc(st_used, 1)
                    else:
                        v.tensor_copy(F, banks(4)).then_inc(st_used, 1)
                    v.wait_ge(st_used, NBACK + c_ + 1)
                    times_cb(v, c_ + 1, 0)

        def y_norm(v, c_):
            v.wait_ge(y_rst, c_ + 1)
            v.tensor_scalar(xtok[:, c_, :], xtok[:, c_, :], rstd[:, c_:c_ + 1], None, ALU.mult).then_inc(yn_ready, 1)

        def cb_tensor(pe, c_):
            for g in range(GROUPS):
                m = pe.matmul(psum[:, 4 if c_ else 3, g * P:(g + 1) * P], BC[:, g, c_ * P:(c_ + 1) * P],
                              BC[:, GROUPS + g, c_ * P:(c_ + 1) * P], start=True, stop=True)
            m.then_inc(cb_mm, 1)

        def scan_tensor(pe):
            def off(c_, d_):
                if d_ == 0 or c_ == 0:
                    pe.wait_ge(st_used, NBACK + c_)
                for g in range(GROUPS):
                    if d_ and c_:
                        pe.wait_ge(off_used, 2 * offs_done(c_, 0) - 1 + g // 2)
                    state = (F if d_ == 0 else R[:, c_, :])[:, g * NB:(g + 1) * NB]
                    m = pe.matmul(psum[:, 4 + g, :], BC[:, GROUPS + g, c_ * P:(c_ + 1) * P], state, start=True, stop=True)
                m.then_inc(off_mm, 1)

            def diagonal(c_, h0, n):
                for h in range(h0, h0 + n):
                    for d_ in range(2):
                        m = pe.matmul(psum[:, h // HPG, (h % HPG) * HD:(h % HPG + 1) * HD], E[d_][:, h, :],
                                      XS[:, d_, h * HD:(h + 1) * HD], start=(d_ == 0), stop=(d_ == 1))
                return m

            for c_ in range(TT):
                if (c_, 0) in OFFS:
                    off(c_, 0)
                for d_ in range(2):
                    pe.wait_ge(xs_ready[d_], c_ + 1)
                if c_:
                    pe.wait_ge(diag_used, c_)
                else:
                    pe.wait_ge(st_used, 2)
                pe.wait_ge(g_ready, 4 * c_ + 2)
                diagonal(c_, 0, HALF).then_inc(g_used, 1)
                if (c_, 1) in OFFS:
                    off(c_, 1)
                pe.wait_ge(g_ready, 4 * c_ + 4)
                diagonal(c_, HALF, HPG)
                if c_ < TT - 1:
                    pe.wait_ge(off_used, 2 * offs_done(c_, 1))
                    cb_tensor(pe, c_ + 1)
                diagonal(c_, HALF + HPG, HPG).then_inc(g_used, 1)
                if c_ < TT - 1:
                    pe.wait_ge(xe_ready, 2 * c_ + 1)
                    pe.wait_ge(cb_ready, 2 * c_ + 4)
                    for g in range(GROUPS):
                        m = pe.matmul(psum[:, 4 + g, :], Bt[:, c_, g * STATE:(g + 1) * STATE], R[:, c_, g * NB:(g + 1) * NB],
                                      start=True, stop=True)
                    m.then_inc(st_mm, 1)

        w_out = ssd_w_out[0]

        def wout_sync(sp):
            for half in range(2):
                for kk in range(2):
                    s_ = (4 + kk, kk)[half]
                    sp.wait_ge(*((xb_mm, 24), (g_used, 2 * TT))[half])
                    load(sp, s_, w_out[kk * D:(kk + 1) * D, half * NB:(half + 1) * NB].rearrange("(k p) n -> p k n", p=P), KD)
                if half == 0:
                    yield
            load_x(sp, X, x_back)
            sp.wait_ge(off_mm, len(OFFS))
            for cd in range(2):
                sp.dma_start(GB[:, cd, :], mod_row(0, 2, cd)).then_inc(gate_in, 16)

        def wout_tensor(pe):
            pe.wait_ge(diag_used, TT)
            for t in range(TT):
                for half in range(2):
                    n = 2 * t + half
                    if n >= 2:
                        pe.wait_ge(yT_ready, 2 * (n - 1))
                    pe.wait_ge(yn_ready, t + 1)
                    for k in range(KD):
                        b = 2 * (n % 2) + k // 4
                        m = pe.transpose(psum[:, b, (k % 4) * P:(k % 4 + 1) * P],
                                         xtok[:, t, (half * KD + k) * P:(half * KD + k + 1) * P], ident[:, :])
                    m.then_inc(yT_mm, 1)
            for half in range(2):
                for kk in range(2):
                    s_ = (4 + kk, kk)[half]
                    wait_full(pe, s_, (3, 7)[half])
                for t in range(TT):
                    n = half * TT + t
                    pe.wait_ge(yT_ready, 4 * (t + 1))
                    if n >= 2:
                        pe.wait_ge(wo_added, n - 1)
                    for k in range(2 * KD):
                        m = pe.matmul(psum[:, 4 + n % 2, :], yT[:, k, t * P:(t + 1) * P], slot((4 + k // KD, k // KD)[half], KD)[:, k % KD, :],
                                      start=(k == 0), stop=(k == 2 * KD - 1))
                    m.then_inc(wo_mm, 1)

        def wout_vector(v, step):
            v.wait_ge(off_mm, len(OFFS))
            for n in range(2 * TT):
                if n == TT:
                    y_norm(v, TT - 1)
                v.wait_ge(yT_mm, n + 1)
                for b in range(2):
                    k0 = (n % 2) * KD + 4 * b
                    v.tensor_tensor(out=yT[:, k0:k0 + 4, (n // 2) * P:(n // 2 + 1) * P],
                                    in0=psum[:, 2 * (n % 2) + b, :].rearrange("p (k t) -> p k t", k=4),
                                    in1=over(cols[:, SN0 + k0:SN0 + k0 + 4], P), op=ALU.mult).then_inc(yT_ready, 1)
            v.wait_ge(gate_in, 32)
            v.wait_ge(x_back, 32)
            for n in range(2 * TT):
                half, t = n // TT, n % TT
                v.wait_ge(wo_mm, n + 1)
                part = slice(half * NB, (half + 1) * NB)
                if n:
                    v.wait_ge(wo_added, n)
                step(v.tensor_tensor(out=tmp, in0=psum[:, 4 + n % 2, :], in1=GB[:, t // 2, part], op=ALU.mult))
                v.tensor_tensor(out=X[:, t, part], in0=X[:, t, part], in1=tmp, op=ALU.add).then_inc(wo_added, 1)
                if n == 2 * TT - 2:
                    moe0.norm.prepare(v, step)
                    for m in range(2):
                        moe0.norm.tile(v, step, m)
            for m in range(2, TT):
                moe0.norm.tile(v, step, m)

        hg = carve(arena, 8192, 2, D)
        hgT = carve(arena, 10240, 2, KD, P)
        u = carve(arena, 12288, 2, DE)
        uT = carve(arena, 13312, 2, DE // P, P)
        Yb = carve(arena, 14336, 2, D)
        GM = carve(arena, 2048, 2, D)
        cg = carve(arena, 8192, 4, D)
        nA, nS = carve(arena, 0, 2, D), carve(arena, 2048, 2, D)
        ngb, nh, njunk = carve(arena, 4096, D), carve(arena, 5120, 2, D), carve(arena, 7168, D)
        KE = DE // P

        def carver(base, at):
            def take(*shape):
                nonlocal at
                v = carve(base, at, *shape)
                at += int(np.prod(shape))
                return v
            return take

        def expand(v, n):
            return v.rearrange("p a (b o) -> p a b o", o=1).broadcast_to([P, v.shape[1], v.shape[2], n])

        MOE_COUNTS = dict(router_in=32, table_zeroed=16, logits_mm=1, pool_const=4, consts=1,
                          rank_mm=1, pos_ready=1, scattered=32 * TT, idx_in=16, h_T_mm=NE, hgT_a=NE, hgT_b=NE, gate_mm=NE, silu=NE,
                          up_mm=NE, u_ready=NE, uT_mm=NE, uT_ready=NE, down_mm=NE, ya=NE + 1, yb=NE + 1, gates_in=32, combined=TT)

        class Moe:

            def __init__(self, tag, layer, tiles, order, fills, before, norm_before, norm_bufs):
                self.bank = 7 if len(tiles) == TT else 5
                self.back_order = (2, 3, 0, 1) if len(tiles) == TT else (0, 1)
                self.layer, self.tiles, self.nt, self.order, self.fills = layer, list(tiles), len(tiles), order, fills
                nt = self.nt
                self.conds = (0, 1) if nt == 4 else (1,)
                if before is None:
                    self.s = dict(**{n: sem(f"moe_{n}") for n in MOE_COUNTS})
                    self.at = dict(**{n: 0 for n in MOE_COUNTS}, rows=0, g_in=0, back_in=0)
                    self.row_stored = [sem(f"moe_rows_stored{j}") for j in range(2)]
                    self.g_in = [sem(f"moe_gathered{j}") for j in range(2)]
                    self.back_in = [sem(f"moe_back_in{j}") for j in range(2)]
                else:
                    self.s, self.row_stored, self.g_in, self.back_in = before.s, before.row_stored, before.g_in, before.back_in
                    self.at = dict(**MOE_COUNTS, rows=16 * (TT // 2 + NE // 2), g_in=16 * (NE // 2), back_in=16 * TT)
                self.o = dict(**{n: sem(f"{tag}_more_{n}") for n in "weights idx turn rows pe act dve stored".split()})
                self.h_d = nc.dram_tensor(f"{tag}_h_d", [P * nt, D], F32).ap()
                self.tok_d = nc.dram_tensor(f"{tag}_tok_d", [NE * P * nt, 1], I32).ap()
                self.y_d = nc.dram_tensor(f"{tag}_y_d", [NE * P * nt, D], F32).ap()
                self.y_rows = self.y_d[0:P * NE, :].rearrange("(p e) d -> e p d", e=NE)
                self.norm = Norm(f"{tag}_norm", X, layer, norm2_g[layer], 3, self.tiles, self.conds, norm_bufs, norm_before)
                self.norm.store, self.norm.stored, self.norm.stored_at, self.norm.h_d = True, self.row_stored, self.at["rows"], self.h_d
                k = carver(arena, 16384)
                self.rw = k(KD, NE)
                self.rb = k(NE)
                self.strict = k(P)
                self.iota = k(NE)
                self.sc, self.bi, self.m, self.pre, self.oh1, self.oh2, self.t16 = (k(nt, NE) for _ in range(7))
                self.pair = k(nt * NG, 6)
                self.gpad = k(nt, 8)
                self.top = k(nt, 8)
                self.topi = k(nt, 8).bitcast(U32)
                self.gi = k(nt, 1)
                self.e1 = k(nt, 2)
                self.gmask = k(nt, NG)
                self.w = k(2, nt)
                self.ws = k(nt)
                self.posf = k(2, nt)
                self.pos = k(2, nt).bitcast(I32)
                self.tok = k(nt).bitcast(I32)
                self.idx = k(NE).bitcast(I32)
                self.zero = k(NE * nt).bitcast(I32)
                self.iint = k(NE).bitcast(I32)

            def fill(self, j, m):
                s_ = self.order[3 * j + m]
                return s_, self.fills[s_]

            def router_load(self, eng):
                eng.dma_start(self.rw, router_w.rearrange("(k p) e -> p k e", p=P)).then_inc(self.s["router_in"], 16)
                eng.dma_start(self.rb, row(router_b)).then_inc(self.s["router_in"], 16)

            def router_pool_start(self, pool, step):
                nt = self.nt
                pool.iota(self.iint, pattern=[[1, NE]], base=0, channel_multiplier=0).then_inc(self.s["pool_const"], 1)
                pool.iota(self.tok, pattern=[[P, nt]], base=0, channel_multiplier=1).then_inc(self.s["pool_const"], 1)
                pool.memset(self.zero, 0).then_inc(self.s["pool_const"], 1)
                pool.memset(self.gpad, -BIG).then_inc(self.s["pool_const"], 1)
                pool.wait_ge(self.s["pool_const"], self.at["pool_const"] + 4)
                pool.dma_start(self.tok_d.rearrange("(p n) o -> p (n o)", p=P), self.zero).then_inc(self.s["table_zeroed"], 16)
                pool.tensor_copy(self.iota, self.iint).then_inc(self.s["consts"], 1)

            def router_tensor(self, pe):
                s, at, nt, t0 = self.s, self.at, self.nt, self.tiles[0]
                pe.wait_ge(s["router_in"], at["router_in"] + 32)
                for n in range(nt + 1):
                    if n < nt:
                        self.norm.tensor(pe, (n,))
                    if n:
                        pe.wait_ge(self.norm.s["evac"], self.norm.at["evac"] + 2 * n)
                        for k in range(KD):
                            m = pe.matmul(psum[:, self.bank, (n - 1) * NE:n * NE], hT[:, k, (t0 + n - 1) * P:(t0 + n) * P], self.rw[:, k, :],
                                          start=(k == 0), stop=(k == KD - 1))
                m.then_inc(s["logits_mm"], 1)
                pe.wait_ge(s["yb"], at["yb"] + 1)
                flat = "p t e -> p (t e)"
                pe.matmul(psum[:, 6, 0:nt * NE], self.strict, self.m.rearrange(flat), start=True, stop=False)
                pe.matmul(psum[:, 6, 0:nt * NE], ones[:, :], self.pre.rearrange(flat), start=False, stop=True)
                pe.matmul(psum[:, 6, 128:128 + NE], ones[:, :], self.t16[:, 0, :], start=True, stop=True).then_inc(s["rank_mm"], 1)

            def router_scalar(self, act):
                s, at, nt = self.s, self.at, self.nt
                act.wait_ge(s["logits_mm"], at["logits_mm"] + 1)
                act.activation(self.sc.rearrange("p t e -> p (t e)"), psum[:, self.bank, 0:nt * NE], ACT.Sigmoid).then_inc(s["ya"], 1)

            def router_vector(self, v, step):
                s, at, nt = self.s, self.at, self.nt
                tt = v.tensor_tensor

                def many(x_):
                    return x_.rearrange("p (o e) -> p o e", o=1).broadcast_to([P, nt, x_.shape[1]])

                v.wait_ge(s["consts"], at["consts"] + 1)
                v.wait_ge(s["router_in"], at["router_in"] + 32)
                v.wait_ge(s["ya"], at["ya"] + 1)
                step(tt(out=self.bi, in0=self.sc, in1=many(self.rb), op=ALU.add))
                b = self.bi.rearrange("p t (g e) -> p (t g) e", g=NG)
                step(tt(out=self.pair[:, :, 0:2], in0=b[:, :, 0:4:2], in1=b[:, :, 1:4:2], op=ALU.add))
                step(tt(out=self.pair[:, :, 2:4], in0=b[:, :, 0:2], in1=b[:, :, 2:4], op=ALU.add))
                step(tt(out=self.pair[:, :, 4:5], in0=b[:, :, 0:1], in1=b[:, :, 3:4], op=ALU.add))
                step(tt(out=self.pair[:, :, 5:6], in0=b[:, :, 1:2], in1=b[:, :, 2:3], op=ALU.add))
                step(v.tensor_reduce(out=self.gpad[:, :, 0:NG], in_=self.pair.rearrange("p (t g) s -> p t g s", g=NG), axis=AX.X, op=ALU.max))
                for n in range(nt):
                    step(v.max(self.top[:, n, :], self.gpad[:, n, :]))
                    step(v.max_index(self.topi[:, n, :], self.top[:, n, :], self.gpad[:, n, :]))
                step(v.tensor_copy(self.gi, self.topi[:, :, 0:1]))
                step(tt(out=self.gmask, in0=many(self.iota[:, 0:NG]), in1=self.gi.broadcast_to([P, nt, NG]), op=ALU.is_equal))
                g4 = expand(self.gmask, EPG)
                split = "p t (g e) -> p t g e"
                step(tt(out=self.bi.rearrange(split, g=NG), in0=self.bi.rearrange(split, g=NG), in1=g4, op=ALU.mult))
                step(v.tensor_scalar(self.gmask, self.gmask, -1.0, BIG, ALU.add, ALU.mult))
                step(tt(out=self.bi.rearrange(split, g=NG), in0=self.bi.rearrange(split, g=NG), in1=g4, op=ALU.add))
                for n in range(nt):
                    step(v.max(self.top[:, n, :], self.bi[:, n, :]))
                    step(v.max_index(self.topi[:, n, :], self.top[:, n, :], self.bi[:, n, :]))
                step(v.tensor_copy(self.e1, self.topi[:, :, 0:2]))
                for k, oh in enumerate((self.oh1, self.oh2)):
                    step(tt(out=oh, in0=many(self.iota), in1=self.e1[:, :, k:k + 1].broadcast_to([P, nt, NE]), op=ALU.is_equal))
                step(tt(out=self.m, in0=self.oh1, in1=self.oh2, op=ALU.add))
                step(v.memset(self.pre[:, 0, :], 0.0))
                for n in range(1, nt):
                    step(tt(out=self.pre[:, n, :], in0=self.pre[:, n - 1, :], in1=self.m[:, n - 1, :], op=ALU.add))
                step(tt(out=self.t16[:, 0, :], in0=self.pre[:, nt - 1, :], in1=self.m[:, nt - 1, :], op=ALU.add))
                tt(out=self.strict, in0=tri_up[:, :], in1=ident[:, :], op=ALU.subtract).then_inc(s["yb"], 1)
                for k, oh in enumerate((self.oh1, self.oh2)):
                    if k == 0:
                        v.wait_ge(s["rank_mm"], at["rank_mm"] + 1)
                    step(tt(out=self.t16, in0=oh, in1=self.sc, op=ALU.mult))
                    step(v.tensor_reduce(out=self.w[:, k, :], in_=self.t16, axis=AX.X, op=ALU.add))
                step(tt(out=self.ws, in0=self.w[:, 0, :], in1=self.w[:, 1, :], op=ALU.add))
                step(v.reciprocal(self.ws, self.ws))
                for k in range(2):
                    step(tt(out=self.w[:, k, :], in0=self.w[:, k, :], in1=self.ws, op=ALU.mult))
                step(v.tensor_scalar(self.bi, psum[:, 6, 0:nt * NE].rearrange("p (t e) -> p t e", t=nt), float(NE), None, ALU.mult))
                step(tt(out=self.bi, in0=self.bi, in1=many(self.iota), op=ALU.add))
                for k, oh in enumerate((self.oh1, self.oh2)):
                    step(tt(out=self.t16, in0=oh, in1=self.bi, op=ALU.mult))
                    step(v.tensor_reduce(out=self.posf[:, k, :], in_=self.t16, axis=AX.X, op=ALU.add))
                step(v.tensor_reduce(out=self.gi[:, 0, :], in_=psum[:, 6, 128:128 + NE], axis=AX.X, op=ALU.max))
                step(v.tensor_copy(most[:, :], self.gi[:, 0, :]))
                v.tensor_copy(self.pos, self.posf).then_inc(s["pos_ready"], 1)

            def router_pool(self, pool):
                s, at, nt = self.s, self.at, self.nt
                pool.wait_ge(s["table_zeroed"], at["table_zeroed"] + 16)
                pool.wait_ge(s["pos_ready"], at["pos_ready"] + 1)
                for k in range(2):
                    for n in range(nt):
                        pool.indirect_dma_start(out=self.tok_d, out_offset=bass.IndirectOffsetOnAxis(ap=self.pos[:, k, n:n + 1], axis=0),
                                                in_=self.tok[:, n:n + 1], in_offset=None).then_inc(s["scattered"], 16)
                pool.wait_ge(s["scattered"], at["scattered"] + 32 * nt)
                pool.dma_start(self.idx, self.tok_d[0:P * NE, :].rearrange("(p e) o -> p (e o)", e=NE)).then_inc(s["idx_in"], 16)
                pool.wait_ge(s["idx_in"], at["idx_in"] + 16)
                for j in range(2):
                    pool.wait_ge(self.row_stored[j], self.at["rows"] + 16 * (nt // 2))

            def gathers(self, pool):
                for e in range(NE):
                    if e >= 2:
                        pool.wait_ge(self.s["h_T_mm"], self.at["h_T_mm"] + e - 1)
                    pool.indirect_dma_start(out=hg[:, e % 2, :], out_offset=None, in_=self.h_d,
                                            in_offset=bass.IndirectOffsetOnAxis(ap=self.idx[:, e:e + 1], axis=0)).then_inc(self.g_in[e % 2], 16)

            def weights(self, e, m):
                if m < 2:
                    w_ = (moe_w_gate, moe_w_up)[m][self.layer, bass.ds(e, 1)].rearrange("o (k p) n -> p (o k) n", p=P)
                    return w_, KD
                return moe_w_down[self.layer, bass.ds(e, 1)].rearrange("o (k p) n -> p (o k) n", p=P), KE

            def sync_first(self, sp, waits):
                for j in range(2):
                    for m in range(3):
                        for w_ in waits[3 * j + m]:
                            sp.wait_ge(*w_)
                        src, a = self.weights(j, m)
                        load(sp, self.order[3 * j + m], src, a)

            def sync_rest(self, sp):
                with sp.Fori(1, NE // 2) as i:
                    for j in range(2):
                        for m, (done, at) in enumerate(((self.s["gate_mm"], self.at["gate_mm"]), (self.s["up_mm"], self.at["up_mm"]),
                                                        (self.s["down_mm"], self.at["down_mm"]))):
                            sp.wait_ge(done, 2 * i + (at + j - 1))
                            src, a = self.weights(2 * i + j, m)
                            load(sp, self.order[3 * j + m], src, a)

            def gate_or_up(self, pe, n, i, j, m):
                s_, f = self.fill(j, m)
                pe.wait_ge(full[s_], 16 * i + (16 * f + 16))
                for k in range(KD):
                    mm = pe.matmul(psum[:, 2 + m, :], hgT[:, j, k, :], slot(s_, KD)[:, k, :], start=(k == 0), stop=(k == KD - 1))
                mm.then_inc((self.s["gate_mm"], self.s["up_mm"])[m], 1)

            def u_transpose(self, pe, n, j):
                pe.wait_ge(self.s["u_ready"], self.at["u_ready"] + n + 1)
                for k in range(KE):
                    m = pe.transpose(psum[:, 4, k * P:(k + 1) * P], u[:, j, k * P:(k + 1) * P], ident[:, :])
                m.then_inc(self.s["uT_mm"], 1)

            def down(self, pe, n, i, j):
                s_, f = self.fill(j, 2)
                pe.wait_ge(full[s_], 16 * i + (16 * f + 16))
                pe.wait_ge(self.s["uT_ready"], self.at["uT_ready"] + n + 1)
                pe.wait_ge(self.s["ya"], self.at["ya"] + n + 1)
                pe.wait_ge(self.s["yb"], self.at["yb"] + n + 1)
                for half in range(2):
                    for k in range(KE):
                        m = pe.matmul(psum[:, 5 + half, :], uT[:, j, k, :], slot(s_, KE)[:, k, half * NB:(half + 1) * NB],
                                      start=(k == 0), stop=(k == KE - 1))
                m.then_inc(self.s["down_mm"], 1)

            def tokens_transpose(self, pe, n, i, j, first):
                pe.wait_ge(self.g_in[j], self.at["g_in"] + 16 * i + 16)
                if not first:
                    pe.wait_ge(self.s["hgT_a"], self.at["hgT_a"] + n)
                    pe.wait_ge(self.s["hgT_b"], self.at["hgT_b"] + n)
                for k in range(KD):
                    m = pe.transpose(psum[:, k // 4, (k % 4) * P:(k % 4 + 1) * P], hg[:, j, k * P:(k + 1) * P], ident[:, :])
                m.then_inc(self.s["h_T_mm"], 1)

            def tensor(self, pe):
                s, at = self.s, self.at
                self.tokens_transpose(pe, 0, 0, 0, True)
                pe.wait_ge(s["hgT_a"], at["hgT_a"] + 1)
                pe.wait_ge(s["hgT_b"], at["hgT_b"] + 1)
                self.gate_or_up(pe, 0, 0, 0, 0)
                self.gate_or_up(pe, 0, 0, 0, 1)
                self.tokens_transpose(pe, 1, 0, 1, False)

                def step_(n, i, j, tokens):
                    i1 = i + j
                    pe.wait_ge(s["hgT_a"], at["hgT_a"] + n + 2)
                    pe.wait_ge(s["hgT_b"], at["hgT_b"] + n + 2)
                    pe.wait_ge(s["silu"], at["silu"] + n + 1)
                    self.gate_or_up(pe, n + 1, i1, 1 - j, 0)
                    self.u_transpose(pe, n, j)
                    self.gate_or_up(pe, n + 1, i1, 1 - j, 1)
                    self.down(pe, n, i, j)
                    if tokens:
                        self.tokens_transpose(pe, n + 2, i + 1, j, False)

                with pe.Fori(0, NE // 2 - 1) as i:
                    for j in range(2):
                        step_(2 * i + j, i, j, True)
                last = NE // 2 - 1
                step_(NE - 2, last, 0, False)
                self.u_transpose(pe, NE - 1, 1)
                self.down(pe, NE - 1, last, 1)

            def copy_tokens(self, eng, n, j, half, first):
                s, at = self.s, self.at
                eng.wait_ge(s["h_T_mm"], at["h_T_mm"] + n + 1)
                if not first:
                    eng.wait_ge(s["up_mm"], at["up_mm"] + n - 1)
                return (hgT[:, j, 4 * half:4 * half + 4, :], psum[:, half, :].rearrange("p (k c) -> p k c", k=4))

            def scalar(self, act):
                s, at = self.s, self.at

                def tokens(n, j, first=False):
                    dst, src = self.copy_tokens(act, n, j, 0, first)
                    act.activation(dst, src, ACT.Copy).then_inc(s["hgT_a"], 1)

                def silu(n, j):
                    act.wait_ge(s["gate_mm"], at["gate_mm"] + n + 1)
                    act.activation(u[:, j, :], psum[:, 2, :], ACT.Silu).then_inc(s["silu"], 1)

                def rows_out(n, i, j):
                    act.wait_ge(s["down_mm"], at["down_mm"] + n + 1)
                    act.wait_ge(self.row_stored[j], self.at["rows"] + 16 * i + 16 * (self.nt // 2))
                    act.activation(Yb[:, j, 0:NB], psum[:, 5, :], ACT.Copy).then_inc(s["ya"], 1)
                    act.wait_ge(s["ya"], at["ya"] + n + 2)
                    act.wait_ge(s["yb"], at["yb"] + n + 2)
                    act.dma_start(self.y_rows[bass.ds(n, 1), :, :].rearrange("o p d -> (o p) d"), Yb[:, j, :]).then_inc(self.row_stored[j], 16)

                tokens(0, 0, True)
                silu(0, 0)
                tokens(1, 1, True)
                with act.Fori(0, NE // 2 - 1) as i:
                    for j in range(2):
                        n = 2 * i + j
                        silu(n + 1, 1 - j)
                        rows_out(n, i, j)
                        tokens(n + 2, j)
                last = NE // 2 - 1
                silu(NE - 1, 1)
                rows_out(NE - 2, last, 0)
                rows_out(NE - 1, last, 1)

            def vector(self, v):
                s, at = self.s, self.at

                def tokens(n, j, first=False):
                    dst, src = self.copy_tokens(v, n, j, 1, first)
                    v.tensor_copy(dst, src).then_inc(s["hgT_b"], 1)

                def gated_(n, j):
                    v.wait_ge(s["up_mm"], at["up_mm"] + n + 1)
                    v.wait_ge(s["silu"], at["silu"] + n + 1)
                    v.tensor_tensor(out=u[:, j, :], in0=u[:, j, :], in1=psum[:, 3, :], op=ALU.mult).then_inc(s["u_ready"], 1)

                def body(n, i, j, more):
                    v.wait_ge(s["uT_mm"], at["uT_mm"] + n + 1)
                    v.tensor_copy(uT[:, j, :, :], psum[:, 4, :].rearrange("p (k c) -> p k c", k=KE)).then_inc(s["uT_ready"], 1)
                    if more:
                        gated_(n + 1, 1 - j)
                    v.wait_ge(s["down_mm"], at["down_mm"] + n + 1)
                    v.wait_ge(self.row_stored[j], self.at["rows"] + 16 * i + 16 * (self.nt // 2))
                    v.tensor_copy(Yb[:, j, NB:D], psum[:, 6, :]).then_inc(s["yb"], 1)

                tokens(0, 0, True)
                gated_(0, 0)
                tokens(1, 1, True)
                with v.Fori(0, NE // 2 - 1) as i:
                    for j in range(2):
                        body(2 * i + j, i, j, True)
                        tokens(2 * i + (j + 2), j)
                last = NE // 2 - 1
                body(NE - 2, last, 0, True)
                body(NE - 1, last, 1, False)

            def crowded(self, eng):
                eng.wait_ge(self.s["pos_ready"], self.at["pos_ready"] + 1)
                return eng.value_load(most[0:1, 0:1], min_val=0, max_val=T) > CAP

            def more(self, eng, body):
                with eng.Fori(0, NE) as e:
                    with eng.Fori(1, self.nt) as r:
                        body(e, r, e * (self.nt - 1) + (r - 1))

            def sync_more(self, sp):
                with sp.If(self.crowded(sp)):
                    with sp.Fori(0, NE) as e:
                        sp.wait_ge(self.o["pe"], 4 * (self.nt - 1) * e + 1)
                        for m in range(3):
                            src, a = self.weights(e, m)
                            sp.dma_start(slot(self.order[m], a), src).then_inc(self.o["weights"], 16)
                    sp.wait_ge(self.o["pe"], 4 * (self.nt - 1) * NE + 1)

            def pool_more(self, pool):
                o = self.o

                def body(e, r, n):
                    pool.wait_ge(o["pe"], 4 * n + 1)
                    pool.dma_start(self.idx[:, 0:1], self.tok_d.rearrange("(r p e) o -> r e p o", e=NE, p=P)[bass.ds(r, 1), bass.ds(e, 1)]
                                   .rearrange("a b p o -> (a b p) o"), allow_slow_non_contiguous=True).then_inc(o["idx"], 16)
                    pool.wait_ge(o["idx"], 16 * n + 16)
                    pool.sem_inc(o["turn"], 1)
                    pool.indirect_dma_start(out=hg[:, 0, :], out_offset=None, in_=self.h_d,
                                            in_offset=bass.IndirectOffsetOnAxis(ap=self.idx[:, 0:1], axis=0)).then_inc(o["rows"], 16)

                with pool.If(self.crowded(pool)):
                    self.more(pool, body)
                    pool.wait_ge(o["turn"], (self.nt - 1) * NE)
                    pool.wait_ge(o["stored"], 16 * (self.nt - 1) * NE)
                    self.combine_pool(pool, self.y_d)
                with pool.Else():
                    self.combine_pool(pool, self.y_d[0:NE * P, :])

            def tensor_more(self, pe):
                o = self.o

                def body(e, r, n):
                    pe.wait_ge(o["rows"], 16 * n + 16)
                    for k in range(KD):
                        m = pe.transpose(psum[:, k // 4, (k % 4) * P:(k % 4 + 1) * P], hg[:, 0, k * P:(k + 1) * P], ident[:, :])
                    m.then_inc(o["pe"], 1)
                    pe.wait_ge(o["act"], 6 * n + 2)
                    pe.wait_ge(o["weights"], 48 * e + 48)
                    for m in range(2):
                        for k in range(KD):
                            mm = pe.matmul(psum[:, 2 + m, :], hgT[:, 0, k, :], slot(self.order[m], KD)[:, k, :], start=(k == 0), stop=(k == KD - 1))
                    mm.then_inc(o["pe"], 1)
                    pe.wait_ge(o["dve"], n + 1)
                    for k in range(KE):
                        m = pe.transpose(psum[:, 4, k * P:(k + 1) * P], u[:, 0, k * P:(k + 1) * P], ident[:, :])
                    m.then_inc(o["pe"], 1)
                    pe.wait_ge(o["act"], 6 * n + 4)
                    for half in range(2):
                        for k in range(KE):
                            m = pe.matmul(psum[:, 5 + half, :], uT[:, 0, k, :], slot(self.order[2], KE)[:, k, half * NB:(half + 1) * NB],
                                          start=(k == 0), stop=(k == KE - 1))
                    m.then_inc(o["pe"], 1)

                with pe.If(self.crowded(pe)):
                    pe.wait_ge(self.s["ya"], self.at["ya"] + NE + 1)
                    pe.wait_ge(self.s["yb"], self.at["yb"] + NE + 1)
                    pe.transpose(psum[:, 0, 0:P], ident[:, :], ident[:, :]).then_inc(o["pe"], 1)
                    self.more(pe, body)

            def scalar_more(self, act):
                o = self.o

                def body(e, r, n):
                    act.wait_ge(o["pe"], 4 * n + 2)
                    for half in range(2):
                        act.activation(hgT[:, 0, 4 * half:4 * half + 4, :], psum[:, half, :].rearrange("p (k c) -> p k c", k=4),
                                       ACT.Copy).then_inc(o["act"], 1)
                    act.wait_ge(o["pe"], 4 * n + 3)
                    act.activation(u[:, 0, :], psum[:, 2, :], ACT.Silu).then_inc(o["act"], 1)
                    act.wait_ge(o["pe"], 4 * n + 4)
                    act.activation(uT[:, 0, :, :], psum[:, 4, :].rearrange("p (k c) -> p k c", k=KE), ACT.Copy).then_inc(o["act"], 1)
                    act.wait_ge(o["pe"], 4 * n + 5)
                    for half in range(2):
                        act.activation(Yb[:, 0, half * NB:(half + 1) * NB], psum[:, 5 + half, :], ACT.Copy).then_inc(o["act"], 1)
                    act.wait_ge(o["act"], 6 * n + 6)
                    act.dma_start(self.y_d.rearrange("(r p e) d -> r e p d", e=NE, p=P)[bass.ds(r, 1), bass.ds(e, 1)]
                                  .rearrange("a b p d -> (a b p) d"), Yb[:, 0, :]).then_inc(o["stored"], 16)
                    act.wait_ge(o["stored"], 16 * n + 16)

                with act.If(self.crowded(act)):
                    act.wait_ge(self.row_stored[0], self.at["rows"] + 16 * (self.nt // 2 + NE // 2))
                    self.more(act, body)

            def vector_more(self, v):
                o = self.o

                def body(e, r, n):
                    v.wait_ge(o["pe"], 4 * n + 3)
                    v.wait_ge(o["act"], 6 * n + 3)
                    v.tensor_tensor(out=u[:, 0, :], in0=u[:, 0, :], in1=psum[:, 3, :], op=ALU.mult).then_inc(o["dve"], 1)

                with v.If(self.crowded(v)):
                    self.more(v, body)

            def combine_pool(self, pool, table):
                s, at = self.s, self.at
                for j in range(2):
                    pool.wait_ge(self.row_stored[j], self.at["rows"] + 16 * (self.nt // 2 + NE // 2))
                for m, n in enumerate(self.back_order):
                    if m >= 2:
                        pool.wait_ge(s["combined"], at["combined"] + m - 1)
                    for k in range(2):
                        pool.indirect_dma_start(out=cg[:, 2 * (m % 2) + k, :], out_offset=None, in_=table,
                                                in_offset=bass.IndirectOffsetOnAxis(ap=self.pos[:, k, n:n + 1], axis=0)).then_inc(self.back_in[m % 2], 16)

            def gates_load(self, eng):
                eng.wait_ge(self.s["logits_mm"], self.at["logits_mm"] + 1)
                for cd in self.conds:
                    eng.dma_start(GM[:, cd, :], mod_row(self.layer, 5, cd)).then_inc(self.s["gates_in"], 16)

            def combine_vector(self, v, step, m):
                s, at = self.s, self.at
                n = self.back_order[m]
                t = self.tiles[n]
                if m == 0:
                    v.wait_ge(s["gates_in"], at["gates_in"] + 16 * len(self.conds))
                v.wait_ge(self.back_in[m % 2], self.at["back_in"] + 32 * (m // 2 + 1))
                c0, c1 = cg[:, 2 * (m % 2), :], cg[:, 2 * (m % 2) + 1, :]
                step(v.tensor_scalar(c0, c0, self.w[:, 0, n:n + 1], None, ALU.mult))
                step(v.scalar_tensor_tensor(out=c0, in0=c1, scalar=self.w[:, 1, n:n + 1], in1=c0, op0=ALU.mult, op1=ALU.add))
                step(v.tensor_tensor(out=c0, in0=c0, in1=GM[:, 0 if t < 2 else 1, :], op=ALU.mult))
                v.tensor_tensor(out=X[:, t, :], in0=X[:, t, :], in1=c0, op=ALU.add).then_inc(s["combined"], 1)

        most = sb("most", [P, 1], I32)
        moe0 = Moe("moe0", 0, range(TT), (4, 5, 0, 1, 2, 3), (8, 8, 7, 7, 4, 4), None, norm_a, (nA, nS, ngb, nh, njunk))

        LT = 2
        q_tok = carve(arena, 0, LT, D)
        k_tok = carve(arena, 2048, TT, D)
        v_tok = carve(arena, 6144, TT, D)
        qT = carve(arena, 10240, KD, LT * P)
        kT = carve(arena, 12288, KD, T)
        sq = psum[:, 6:8, :].rearrange("p b n -> p (b n)")
        rot = carve(arena, 17408, D)
        bA, bS = carve(arena, 6144, 2, D), carve(arena, 4096, 2, D)
        bg, bh, bj = carve(hflat, 2048, D), carve(arena, 13312, 2, D), carve(arena, 15360, D)
        norm_b = Norm("norm_b", X, 1, norm1_g[1], 0, (2, 3, 0, 1), (0, 1), (bA, bS, bg, bh, bj), moe0.norm)
        norm_b.src_ready = [(moe0.s["combined"], n + 1) for n in range(TT)]
        kk = carver(arena, 16384)
        rope = kk(LT, 2, DA_D)
        gains = kk(2, 2, DA_D)
        sub_g = kk(DA_V)
        lqk = kk(2, 2 * DA_D)
        lam2 = kk(2)
        nlam = kk(1)
        rs = kk(2 * DA_H)
        mhalf16 = kk(2 * DA_H)
        pk = carver(hflat, 0)
        pr = [pk(2, T) for _ in range(2)]
        attT = [pk(TT, P) for _ in range(2)]
        o_tok = carve(arena, 0, LT, D)
        osq = carve(arena, 2048, D)
        oT = carve(arena, 3072, KD, LT * P)
        GA = carve(arena, 5120, D)
        wtmp = pk(NB)
        stat = [pk(8) for _ in range(2)]

        A = dict(**{n: sem(f"att_{n}") for n in
                               ("small_in lam_exp lam_exp2 const qkv_mm qkv_copied squared rms normed_q normed_k T_mm T_copied s_mm max_ready "
                                "exp_done mixed p_T p_copied o_mm o_copied o_sq o_rms o_normed oT_mm oT_copied out_mm out_added gate_in").split()})
        QKV = [(n, t) for n in range(6) for t in (range(2, TT) if n < 2 else range(TT))]
        qkv_fill = {4: 12, 5: 12, 0: 16, 1: 16, 2: 15, 3: 15}
        qkv_slot = (4, 5, 0, 1, 2, 3)

        def att_sync(sp):
            s = moe0.s
            for n, (done, count) in enumerate(((s["gate_mm"], 15), (s["up_mm"], 15), (s["down_mm"], 15), (s["gate_mm"], 16), (s["up_mm"], 16), (s["down_mm"], 16))):
                if n == 2:
                    sp.wait_ge(moe0.s["combined"], 3)
                sp.wait_ge(done, count)
                load(sp, qkv_slot[n], blocks(da_w_in[0], n * NB), KD)
            sp.wait_ge(moe0.s["combined"], TT)
            for dst, src in ((rope.rearrange("p t a d -> p t (a d)"), rope_d.rearrange("(t p) a d -> p t (a d)", p=P)),
                             (gains[:, 0].rearrange("p m d -> p (m d)"), row(da_q_norm[0].rearrange("m d -> (m d)"))),
                             (gains[:, 1].rearrange("p m d -> p (m d)"), row(da_k_norm[0].rearrange("m d -> (m d)"))),
                             (sub_g, row(da_sub_norm[0])),
                             (lqk[:, 0, :], row(da_lam_q[0].rearrange("m d -> (m d)"))),
                             (lqk[:, 1, :], row(da_lam_k[0].rearrange("m d -> (m d)")))):
                sp.dma_start(dst, src).then_inc(A["small_in"], 16)
            for n in range(2):
                sp.wait_ge(A["qkv_mm"], (2, 4)[n])
                load(sp, 4 + n, blocks(da_w_out[0], n * NB), KD)
            sp.wait_ge(A["T_mm"], 12)
            sp.dma_start(GA, mod_row(1, 2, 1)).then_inc(A["gate_in"], 16)

        def att_pool(pool, step):
            pool.wait_ge(A["small_in"], 96)
            pool.memset(mhalf16, -0.5).then_inc(A["const"], 1)
            pool.wait_ge(A["const"], 1)
            for n in range(6):
                pool.wait_ge(A["squared"], n + 1)
                step(pool.tensor_scalar(rs, rs, 1.0 / DA_D, EPS, ALU.mult, ALU.add))
                pool.tensor_tensor(out=rs, in0=rs, in1=mhalf16, op=ALU.pow).then_inc(A["rms"], 1)
            for n in range(LT):
                pool.wait_ge(A["o_sq"], n + 1)
                step(pool.tensor_scalar(rs[:, 0:DA_H], rs[:, 0:DA_H], 1.0 / DA_V, EPS, ALU.mult, ALU.add))
                pool.tensor_tensor(out=rs[:, 0:DA_H], in0=rs[:, 0:DA_H], in1=mhalf16[:, 0:DA_H], op=ALU.pow).then_inc(A["o_rms"], 1)

        def att_tensor(pe):
            for m_, (n, t) in enumerate(QKV):
                if m_ == LT:
                    norm_b.tensor(pe, range(LT, TT))
                elif m_ == 2 * LT:
                    pe.wait_ge(norm_b.s["evac"], norm_b.at["evac"] + 2 * TT)
                elif m_ < LT:
                    pe.wait_ge(norm_b.s["evac"], norm_b.at["evac"] + 2 * (m_ + 1))
                if t == QKV[0][1] or m_ == 0 or QKV[m_ - 1][0] != n:
                    wait_full(pe, qkv_slot[n], qkv_fill[qkv_slot[n]])
                if m_ >= 2:
                    pe.wait_ge(A["qkv_copied"], m_ - 1)
                for k in range(KD):
                    mm = pe.matmul(psum[:, 4 + m_ % 2, :], hT[:, k, t * P:(t + 1) * P], slot(qkv_slot[n], KD)[:, k, :],
                                   start=(k == 0), stop=(k == KD - 1))
                mm.then_inc(A["qkv_mm"], 1)
            pe.wait_ge(A["qkv_copied"], len(QKV))
            for n in range(6):
                pe.wait_ge(*((A["normed_q"], n + 1) if n < 2 else (A["normed_k"], n - 1)))
                src = q_tok[:, n, :] if n < 2 else k_tok[:, n - 2, :]
                for half in range(2):
                    m_ = 2 * n + half
                    if m_ >= 2:
                        pe.wait_ge(A["T_copied"], m_ - 1)
                    for b in range(4):
                        mm = pe.transpose(psum[:, 4 + m_ % 2, b * P:(b + 1) * P], src[:, (4 * half + b) * P:(4 * half + b + 1) * P], ident[:, :])
                    mm.then_inc(A["T_mm"], 1)
            pe.wait_ge(A["T_copied"], 12)

            def scores(n):
                t, h = n // DA_H, n % DA_H
                if n >= 2:
                    pe.wait_ge(A["exp_done"], 2 * (n - 1))
                r = 64 * (h % 2)
                for m in range(2):
                    b = 4 * m + h // 2
                    mm = pe.matmul(psum[:, 2 * (n % 2) + m, :], qT[r:r + 64, b, t * P:(t + 1) * P], kT[r:r + 64, b, :],
                                   start=True, stop=True)
                mm.then_inc(A["s_mm"], 1)

            def values(n):
                t, h = n // DA_H, n % DA_H
                pe.wait_ge(A["mixed"], n + 1)
                if n >= 2:
                    pe.wait_ge(A["p_copied"], n - 1)
                for k in range(TT):
                    mm = pe.transpose(psum[:, 4 + n % 2, k * P:(k + 1) * P], pr[n % 2][:, 0, k * P:(k + 1) * P], ident[:, :])
                mm.then_inc(A["p_T"], 1)

            def product(n):
                t, h = n // DA_H, n % DA_H
                pe.wait_ge(A["p_copied"], n + 1)
                if n % 4 == 0 and n >= 8:
                    pe.wait_ge(A["o_copied"], n // 4 - 1)
                for k in range(TT):
                    mm = pe.matmul(psum[:, 6 + (n // 4) % 2, (h % 4) * P:(h % 4 + 1) * P], attT[n % 2][:, k, :],
                                   v_tok[:, k, h * DA_V:(h + 1) * DA_V], start=(k == 0), stop=(k == TT - 1))
                mm.then_inc(A["o_mm"], 1)

            N = LT * DA_H
            scores(0)
            scores(1)
            for n in range(N + 1):
                if n + 2 < N:
                    scores(n + 2)
                if n < N:
                    values(n)
                if n:
                    product(n - 1)
            for t in range(LT):
                pe.wait_ge(A["o_normed"], t + 1)
                for half in range(2):
                    for b in range(4):
                        mm = pe.transpose(psum[:, 2 * (t % 2) + half, b * P:(b + 1) * P],
                                          o_tok[:, t, (4 * half + b) * P:(4 * half + b + 1) * P], ident[:, :])
                    mm.then_inc(A["oT_mm"], 1)
            for t in range(LT):
                for n in range(2):
                    if t == 0:
                        wait_full(pe, 4 + n, 13)
                    pe.wait_ge(A["oT_copied"], 2 * t + 2)
                    for k in range(KD):
                        mm = pe.matmul(psum[:, 4 + 2 * n + t, :], oT[:, k, t * P:(t + 1) * P], slot(4 + n, KD)[:, k, :],
                                       start=(k == 0), stop=(k == KD - 1))
                    mm.then_inc(A["out_mm"], 1)

        def att_scalar(act):
            act.wait_ge(A["lam_exp"], 1)
            act.activation(lam2, lam2, ACT.Exp).then_inc(A["lam_exp2"], 1)
            for m_, (n, t) in enumerate(QKV):
                act.wait_ge(A["qkv_mm"], m_ + 1)
                dst = (q_tok[:, t - 2, n * NB:(n + 1) * NB] if n < 2 else k_tok[:, t, (n - 2) * NB:(n - 1) * NB] if n < 4
                       else v_tok[:, t, (n - 4) * NB:(n - 3) * NB])
                act.activation(dst, psum[:, 4 + m_ % 2, :], ACT.Copy).then_inc(A["qkv_copied"], 1)
            for n in range(6):
                for half in range(2):
                    act.wait_ge(A["T_mm"], 2 * n + half + 1)
                    dst = (qT if n < 2 else kT)[:, 4 * half:4 * half + 4, (n % 2 if n < 2 else n - 2) * P:(n % 2 + 1 if n < 2 else n - 1) * P]
                    act.activation(dst, psum[:, 4 + half, :].rearrange("p (b t) -> p b t", b=4), ACT.Copy).then_inc(A["T_copied"], 1)
            N = LT * DA_H
            for n in range(N + 1):
                if n < N:
                    act.wait_ge(A["max_ready"], n + 1)
                    if n >= 2:
                        act.wait_ge(A["p_T"], n - 1)
                    for m in range(2):
                        act.activation(pr[n % 2][:, m, :], psum[:, 2 * (n % 2) + m, :], ACT.Exp, bias=stat[n % 2][:, m:m + 1],
                                       scale=DA_D ** -0.5, accum_out=stat[n % 2][:, 2 + m:3 + m]).then_inc(A["exp_done"], 1)
                if n:
                    act.wait_ge(A["p_T"], n)
                    act.activation(attT[(n - 1) % 2], psum[:, 4 + (n - 1) % 2, :].rearrange("p (k t) -> p k t", k=TT), ACT.Copy).then_inc(A["p_copied"], 1)
            for m_ in range(2 * LT):
                act.wait_ge(A["oT_mm"], m_ + 1)
                act.activation(oT[:, 4 * (m_ % 2):4 * (m_ % 2) + 4, (m_ // 2) * P:(m_ // 2 + 1) * P],
                               psum[:, m_, :].rearrange("p (b t) -> p b t", b=4), ACT.Copy).then_inc(A["oT_copied"], 1)

        def att_vector(v, step):
            tt = v.tensor_tensor
            v.wait_ge(A["small_in"], 96)
            step(tt(out=lqk[:, 0, :], in0=lqk[:, 0, :], in1=lqk[:, 1, :], op=ALU.mult))
            v.tensor_reduce(out=lam2, in_=lqk[:, 0, :].rearrange("p (m d) -> p m d", m=2), axis=AX.X, op=ALU.add).then_inc(A["lam_exp"], 1)
            v.wait_ge(A["lam_exp2"], 1)
            step(v.scalar_tensor_tensor(out=nlam, in0=lam2[:, 1:2], scalar=-LAM_INIT, in1=lam2[:, 0:1], op0=ALU.add, op1=ALU.subtract))
            for n in range(6):
                w_ = 0 if n < 2 else 1
                tok = q_tok[:, n, :] if n < 2 else k_tok[:, n - 2, :]
                v.wait_ge(A["qkv_copied"], (n + 3) if n < 2 else (4 + 4 + n - 1))
                mh = tok.rearrange("p (x d) -> p x d", d=DA_D)
                step(tt(out=sq, in0=tok, in1=tok, op=ALU.mult))
                v.tensor_reduce(out=rs, in_=sq.rearrange("p (x d) -> p x d", d=DA_D), axis=AX.X, op=ALU.add).then_inc(A["squared"], 1)
                v.wait_ge(A["rms"], n + 1)
                step(tt(out=mh, in0=mh, in1=rs.rearrange("p (x o) -> p x o", o=1).broadcast_to([P, 2 * DA_H, DA_D]), op=ALU.mult))
                done = A["normed_q"] if n < 2 else A["normed_k"]
                m4 = tok.rearrange("p (m h d) -> p m h d", m=2, h=DA_H)
                ins = tt(out=m4, in0=m4, in1=gains[:, w_].rearrange("p m (o d) -> p m o d", o=1).broadcast_to([P, 2, DA_H, DA_D]), op=ALU.mult)
                t = n if n < 2 else n - 4
                if n in (2, 3):
                    ins.then_inc(done, 1)
                    continue
                step(ins)
                half = "p (x f s) -> p x f s"
                F4 = DA_D // 4
                xa_, ra_ = tok.rearrange(half, f=2, s=F4), rot.rearrange(half, f=2, s=F4)
                r_c, r_s = rope[:, t, 0, :], rope[:, t, 1, :]
                for f in range(2):
                    src = xa_[:, :, 1 - f, :].rearrange("p (x a) s -> p x a s", a=2)
                    dst = ra_[:, :, f, :].rearrange("p (x a) s -> p x a s", a=2)
                    sn = r_s.rearrange("p (o a f s) -> p o a f s", o=1, f=2, s=F4)[:, :, :, f, :].broadcast_to([P, 2 * DA_H, 2, F4])
                    step(tt(out=dst, in0=src, in1=sn, op=ALU.mult))
                step(tt(out=mh, in0=mh, in1=r_c.rearrange("p (o d) -> p o d", o=1).broadcast_to([P, 2 * DA_H, DA_D]), op=ALU.mult))
                tt(out=tok, in0=tok, in1=rot, op=ALU.add).then_inc(done, 1)
            N = LT * DA_H

            def maxes(n):
                v.wait_ge(A["s_mm"], n + 1)
                st = stat[n % 2]
                step(v.tensor_reduce(out=st[:, 0:2], in_=psum[:, 2 * (n % 2):2 * (n % 2) + 2, :], axis=AX.X, op=ALU.max))
                v.tensor_scalar(st[:, 0:2], st[:, 0:2], -(DA_D ** -0.5), None, ALU.mult).then_inc(A["max_ready"], 1)

            v.wait_ge(A["T_copied"], 12)
            maxes(0)
            maxes(1)
            for n in range(N):
                st = stat[n % 2]
                v.wait_ge(A["exp_done"], 2 * n + 2)
                step(v.reciprocal(st[:, 4:6], st[:, 2:4]))
                step(tt(out=st[:, 5:6], in0=st[:, 5:6], in1=nlam, op=ALU.mult))
                step(v.tensor_scalar(pr[n % 2][:, 0, :], pr[n % 2][:, 0, :], st[:, 4:5], None, ALU.mult))
                v.scalar_tensor_tensor(out=pr[n % 2][:, 0, :], in0=pr[n % 2][:, 1, :], scalar=st[:, 5:6], in1=pr[n % 2][:, 0, :],
                                       op0=ALU.mult, op1=ALU.add).then_inc(A["mixed"], 1)
                if n + 2 < N:
                    maxes(n + 2)
                if n % 4 == 1 and n > 4:
                    o_copy(v, n // 4 - 1)
                if n == 10:
                    o_norm(v, step, 0)
            o_copy(v, 3)
            o_norm(v, step, 1)
            v.wait_ge(A["gate_in"], 16)
            for m_ in range(4):
                t, n = m_ // 2, m_ % 2
                v.wait_ge(A["out_mm"], m_ + 1)
                part = slice(n * NB, (n + 1) * NB)
                step(tt(out=wtmp, in0=psum[:, 4 + 2 * n + t, :], in1=GA[:, part], op=ALU.mult))
                ins = tt(out=X[:, 2 + t, part], in0=X[:, 2 + t, part], in1=wtmp, op=ALU.add).then_inc(A["out_added"], 1)
                v.wait_ge(A["out_added"], m_ + 1)
                if n:
                    if t == 0:
                        moe1.norm.prepare(v, step)
                    moe1.norm.tile(v, step, t)

        def o_copy(v, g):
            v.wait_ge(A["o_mm"], 4 * g + 4)
            v.tensor_copy(o_tok[:, g // 2, (g % 2) * NB:(g % 2 + 1) * NB], psum[:, 6 + g % 2, :]).then_inc(A["o_copied"], 1)

        def o_norm(v, step, t):
            v.wait_ge(A["o_copied"], 2 * t + 2)
            o = o_tok[:, t, :]
            oh = o.rearrange("p (h e) -> p h e", h=DA_H)
            step(v.tensor_tensor(out=osq, in0=o, in1=o, op=ALU.mult))
            v.tensor_reduce(out=rs[:, 0:DA_H], in_=osq.rearrange("p (h e) -> p h e", h=DA_H), axis=AX.X, op=ALU.add).then_inc(A["o_sq"], 1)
            v.wait_ge(A["o_rms"], t + 1)
            step(v.tensor_tensor(out=oh, in0=oh, in1=rs[:, 0:DA_H].rearrange("p (h o) -> p h o", o=1).broadcast_to([P, DA_H, DA_V]), op=ALU.mult))
            v.scalar_tensor_tensor(out=oh, in0=oh, scalar=1.0 - LAM_INIT, op0=ALU.mult, op1=ALU.mult,
                                   in1=sub_g.rearrange("p (o e) -> p o e", o=1).broadcast_to([P, DA_H, DA_V])).then_inc(A["o_normed"], 1)

        moe1 = Moe("moe1", 1, range(2, TT), (0, 1, 2, 3, 4, 5), (17, 17, 16, 16, 14, 14), moe0, norm_b,
                   (carve(arena, 10240, 1, D), carve(arena, 11264, 1, D), carve(arena, 12288, D), carve(arena, 13312, 2, D), carve(arena, 15360, D)))
        moe1.norm.src_ready = [(A["out_added"], 2 * n + 2) for n in range(LT)]
        out_stored = sem("out_stored")

        block = es.enter_context(nc.Block())

        @block.sync
        def _(sp):
            setup_sync(sp)
            ada_sync(sp, 0)
            norm_a.load(sp, lambda e: e.wait_ge(mod_out, 32))
            proj_sync(sp)
            wo = wout_sync(sp)
            next(wo)
            scan_sync(sp)
            for _ in wo:
                pass
            sp.wait_ge(yT_mm, 8)
            moe0.norm.load(sp, lambda e: None)
            moe0.router_load(sp)
            stored = [(moe0.row_stored[j], 16 * (TT // 2)) for j in range(2)]
            moe0.sync_first(sp, ([(wo_mm, 4)], [(wo_mm, 4)], [(wo_mm, 8)] + stored, [], [], []))
            moe0.sync_rest(sp)
            moe0.gates_load(sp)
            norm_b.load(sp, lambda e: None)
            moe0.sync_more(sp)
            att_sync(sp)
            sp.wait_ge(A["o_mm"], LT * DA_H)
            moe1.norm.load(sp, lambda e: None)
            moe1.router_load(sp)
            k_used = (A["qkv_mm"], 20)
            moe1.sync_first(sp, ([k_used], [k_used], [k_used], [k_used], [(A["out_mm"], 3)], [(A["out_mm"], 4)]))
            moe1.sync_rest(sp)
            moe1.gates_load(sp)
            moe1.sync_more(sp)
            for n in range(LT):
                sp.wait_ge(moe1.s["combined"], moe1.at["combined"] + n + 1)
                sp.dma_start(out[0, n * P:(n + 1) * P, :], X[:, 2 + n, :]).then_inc(out_stored, 16)
            sp.wait_ge(out_stored, 16 * LT)

        @block.gpsimd
        def _(pool):
            step = Chain(pool, pool_step)
            setup_pool(pool)
            norm_a.pool(pool, step)
            pool.wait_ge(norm_a.s["h_ready"], TT)
            pool.memset(U, 0.0).then_inc(pads_set, 1)
            scan_pool(pool, step)
            pool.wait_ge(g_ready, 4 * TT)
            moe0.router_pool_start(pool, step)
            moe0.norm.pool(pool, step)
            moe0.router_pool(pool)
            moe0.gathers(pool)
            moe0.pool_more(pool)
            norm_b.pool(pool, step)
            att_pool(pool, step)
            pool.wait_ge(A["o_normed"], LT)
            moe1.router_pool_start(pool, step)
            moe1.norm.pool(pool, step)
            moe1.router_pool(pool)
            moe1.gathers(pool)
            moe1.pool_more(pool)

        @block.scalar
        def _(act):
            act.dma_start(ada_row[0:1, :], ada_bias(0)).then_inc(adab_in, 16)
            act.wait_ge(full[0], 16)
            load_x(act, xa, x_in)
            act.dma_start(w_dt, w_in[:, IN_DT:IN_DT + 64].rearrange("(k p) n -> p k n", p=P)).then_inc(w_dt_in, 16)
            act.wait_ge(pool_set, 4)
            act.dma_start(dt_b, ssd_dt_bias[0].rearrange("d (h o) -> (d h) o", o=1)).then_inc(w_dt_in, 16)
            setup_scalar(act)
            ada_scalar(act, 0)
            norm_a.scalar(act, lambda e: e.wait_ge(x_in, 32))
            act.wait_ge(pads_set, 1)
            proj_scalar(act)
            scan_scalar(act)
            moe0.norm.src_ready = [(wo_added, TT + n + 1) for n in range(TT)]
            moe0.norm.scalar(act, lambda e: None)
            moe0.router_scalar(act)
            moe0.scalar(act)
            moe0.scalar_more(act)
            norm_b.scalar(act, lambda e: None)
            att_scalar(act)
            moe1.norm.scalar(act, lambda e: None)
            moe1.router_scalar(act)
            moe1.scalar(act)
            moe1.scalar_more(act)

        @block.vector
        def _(v):
            step = Chain(v, dve_step)
            setup_vector(v, step)
            norm_a.vector(v, step)
            proj_vector(v, step)
            back_vector(v, step)
            scan_vector(v, step)
            wout_vector(v, step)
            moe0.router_vector(v, step)
            moe0.vector(v)
            moe0.vector_more(v)
            norm_b.prepare(v, step)
            for m in range(TT):
                moe0.combine_vector(v, step, m)
                if m:
                    norm_b.tile(v, step, m - 1)
            norm_b.tile(v, step, TT - 1)
            att_vector(v, step)
            moe1.router_vector(v, step)
            moe1.vector(v)
            moe1.vector_more(v)
            for m in range(LT):
                moe1.combine_vector(v, step, m)

        @block.tensor
        def _(pe):
            setup_tensor(pe)
            pe.wait_ge(pool_set, 1)
            ada_tensor(pe, 0)
            norm_a.tensor(pe)
            proj_tensor(pe)
            back_tensor(pe)
            scan_tensor(pe)
            wout_tensor(pe)
            moe0.router_tensor(pe)
            moe0.tensor(pe)
            moe0.tensor_more(pe)
            norm_b.tensor(pe, range(LT))
            att_tensor(pe)
            moe1.router_tensor(pe)
            moe1.tensor(pe)
            moe1.tensor_more(pe)


_INS = ["x", "c", "ctx", "c_ctx", "ada_w", "ada_b", "norm1_g", "norm2_g",
        "ssd_w_in", "ssd_conv_w", "ssd_conv_b", "ssd_dt_bias", "ssd_a_log", "ssd_d", "ssd_norm_g", "ssd_w_out",
        "da_w_in", "da_q_norm", "da_k_norm", "da_lam_q", "da_lam_k", "da_sub_norm", "da_w_out",
        "router_w", "router_b", "moe_w_gate", "moe_w_up", "moe_w_down"]


def kernel(**inputs):
    import concourse.bacc as bacc
    from concourse.bass_utils import run_bass_kernel_spmd

    nc = bacc.Bacc("TRN2", target_bir_lowering=False, num_devices=1)
    arrays, aps = {}, {}
    for name in _INS:
        a = np.ascontiguousarray(inputs[name])
        arrays[f"in_{name}"] = a
        aps[name] = nc.dram_tensor(f"in_{name}", a.shape, mybir.dt.from_np(a.dtype), kind="ExternalInput").ap()
    aps["out"] = nc.dram_tensor("out_latent", (1, SEG, D), F32, kind="ExternalOutput").ap()
    backbone(nc, **aps)
    r = run_bass_kernel_spmd(nc, [arrays], core_ids=[0])
    return r.results[0]["out_latent"]
```
